# Optimizing a Trainium2 kernel written in Bass

```python
import jax, jax.numpy as jnp
from jax import lax
import numpy as np

D_MODEL = 2048
BATCH = 1
SEQ = 512
DEPTH = 1

CTX_LEN = 256
GRID_W = 64
ROPE_BASE = 10000.0
EPS = 1e-6
NEG = -1e30
BLOCK = 128

MLA_HEADS = 8
MLA_NOPE = 128
MLA_ROPE = 64
MLA_V = 128
MLA_Q_RANK = 512
MLA_KV_RANK = 512
MLA_WIDTH = MLA_HEADS * MLA_V

SWA_HEADS = 16
SWA_KV_HEADS = 4
SWA_GROUP = SWA_HEADS // SWA_KV_HEADS
SWA_HEAD_DIM = 64
SWA_WIDTH = SWA_HEADS * SWA_HEAD_DIM
SWA_KV_WIDTH = SWA_KV_HEADS * SWA_HEAD_DIM
WINDOW = 128

IN_SPLITS = (MLA_Q_RANK, MLA_KV_RANK, MLA_ROPE, MLA_WIDTH,
             SWA_WIDTH, SWA_KV_WIDTH, SWA_KV_WIDTH, SWA_WIDTH,
             D_MODEL, D_MODEL)
IN_WIDTH = 512 + 512 + 64 + 1024 + 1024 + 256 + 256 + 1024 + 2 * D_MODEL

kernel_name = "hybrid_mla_swa_sink_gated_dit_block"

def _rmsnorm(x, g):
    xf = x.astype(jnp.float32)
    y = xf * lax.rsqrt(jnp.mean(xf * xf, axis=-1, keepdims=True) + EPS)
    return (y * g.astype(jnp.float32)).astype(x.dtype)

def _rope_half(x, pos):
    n = x.shape[-1] // 2
    inv = ROPE_BASE ** (-jnp.arange(n, dtype=jnp.float32) / n)
    ang = pos.astype(jnp.float32)[:, None] * inv[None, :]
    shape = (x.shape[1],) + (1,) * (x.ndim - 3) + (n,)
    cos = jnp.cos(ang).reshape(shape).astype(x.dtype)
    sin = jnp.sin(ang).reshape(shape).astype(x.dtype)
    x1, x2 = x[..., :n], x[..., n:]
    return jnp.concatenate([x1 * cos - x2 * sin, x2 * cos + x1 * sin], axis=-1)

def _rope_2d(x, rows, cols):
    a = x.shape[-1] // 2
    return jnp.concatenate([_rope_half(x[..., :a], rows), _rope_half(x[..., a:], cols)], axis=-1)

def _branch_inputs(h, w_in, b_in, qn_g, kvn_g, w_uq, w_ukv):
    B, S, _ = h.shape
    offsets, acc = [], 0
    for w in IN_SPLITS[:-1]:
        acc += w
        offsets.append(acc)
    z = h @ w_in + b_in
    c_q, c_kv, k_pe, gate_a, q_s, k_s, v_s, gate_b, mg_a, mg_b = jnp.split(z, offsets, axis=-1)
    q_mla = (_rmsnorm(c_q, qn_g) @ w_uq).reshape(B, S, MLA_HEADS, MLA_NOPE + MLA_ROPE)
    kv = (_rmsnorm(c_kv, kvn_g) @ w_ukv).reshape(B, S, MLA_HEADS, MLA_NOPE + MLA_V)
    k_nope, v_mla = kv[..., :MLA_NOPE], kv[..., MLA_NOPE:]
    q_s = q_s.reshape(B, S, SWA_KV_HEADS, SWA_GROUP, SWA_HEAD_DIM)
    k_s = k_s.reshape(B, S, SWA_KV_HEADS, SWA_HEAD_DIM)
    v_s = v_s.reshape(B, S, SWA_KV_HEADS, SWA_HEAD_DIM)
    return q_mla, k_nope, v_mla, k_pe, gate_a, q_s, k_s, v_s, gate_b, mg_a, mg_b

def _mla_keys(k_nope, k_pe):
    B, S, H, _ = k_nope.shape
    return jnp.concatenate([k_nope, jnp.broadcast_to(k_pe[:, :, None, :], (B, S, H, MLA_ROPE))], axis=-1)

def _merge(a_heads, gate_a, b_heads, gate_b, mg_a, mg_b, w_ba, w_bb, w_o):
    y_a = (a_heads * jax.nn.silu(gate_a)) @ w_ba
    y_b = (b_heads * jax.nn.silu(gate_b)) @ w_bb
    return (jax.nn.sigmoid(mg_a) * y_a + jax.nn.sigmoid(mg_b) * y_b) @ w_o

def _mla_latent(q, k, v, k_ctx, v_ctx):
    B, S, H, dq = q.shape
    scale = dq ** -0.5
    k_all = jnp.concatenate([k, k_ctx], axis=1)
    v_all = jnp.concatenate([v, v_ctx], axis=1)

    def blk(i):
        qb = lax.dynamic_slice_in_dim(q, i * BLOCK, BLOCK, axis=1)
        s = jnp.einsum('bqhd,bkhd->bhqk', qb, k_all).astype(jnp.float32) * scale
        p = jax.nn.softmax(s, axis=-1).astype(v_all.dtype)
        return jnp.einsum('bhqk,bkhd->bqhd', p, v_all)

    o = lax.map(blk, jnp.arange(S // BLOCK))
    return o.transpose(1, 0, 2, 3, 4).reshape(B, S, H * MLA_V)

def _swa_latent(q, k, v, k_ctx, v_ctx, sink_l):
    B, S, KV, G, d = q.shape
    C = k_ctx.shape[1]
    scale = d ** -0.5
    span = BLOCK + 2 * WINDOW
    pad = ((0, 0), (WINDOW, WINDOW), (0, 0), (0, 0))
    k_pad = jnp.pad(k, pad)
    v_pad = jnp.pad(v, pad)
    qi = jnp.arange(BLOCK)[:, None]
    kj = jnp.arange(span)[None, :]
    band = jnp.abs(kj - WINDOW - qi) <= WINDOW
    sink_b = jnp.broadcast_to(sink_l.astype(jnp.float32).reshape(1, KV, G, 1, 1), (B, KV, G, BLOCK, 1))

    def blk(i):
        start = i * BLOCK
        qb = lax.dynamic_slice_in_dim(q, start, BLOCK, axis=1)
        kw = lax.dynamic_slice_in_dim(k_pad, start, span, axis=1)
        vw = lax.dynamic_slice_in_dim(v_pad, start, span, axis=1)
        pos = start - WINDOW + kj
        mask = band & (pos >= 0) & (pos < S)
        s_w = jnp.einsum('bqkgd,bpkd->bkgqp', qb, kw).astype(jnp.float32) * scale
        s_w = jnp.where(mask, s_w, NEG)
        s_c = jnp.einsum('bqkgd,bckd->bkgqc', qb, k_ctx).astype(jnp.float32) * scale
        p = jax.nn.softmax(jnp.concatenate([s_w, s_c, sink_b], axis=-1), axis=-1).astype(v.dtype)
        return (jnp.einsum('bkgqp,bpkd->bqkgd', p[..., :span], vw)
                + jnp.einsum('bkgqc,bckd->bqkgd', p[..., span:span + C], v_ctx))

    o = lax.map(blk, jnp.arange(S // BLOCK))
    return o.transpose(1, 0, 2, 3, 4, 5).reshape(B, S, KV * G * d)

def _context_mixer(cx, sink_l, w_ba, w_bb, w_o):
    q, k_nope, v, k_pe, gate_a, q_s, k_s, v_s, gate_b, mg_a, mg_b = cx
    B, C = q.shape[:2]
    k = _mla_keys(k_nope, k_pe)
    s = jnp.einsum('bqhd,bkhd->bhqk', q, k).astype(jnp.float32) * (q.shape[-1] ** -0.5)
    a = jnp.einsum('bhqk,bkhd->bqhd', jax.nn.softmax(s, axis=-1).astype(v.dtype), v).reshape(B, C, MLA_WIDTH)
    s2 = jnp.einsum('bqkgd,bckd->bkgqc', q_s, k_s).astype(jnp.float32) * (SWA_HEAD_DIM ** -0.5)
    sink_b = jnp.broadcast_to(sink_l.astype(jnp.float32).reshape(1, SWA_KV_HEADS, SWA_GROUP, 1, 1),
                              s2.shape[:-1] + (1,))
    p2 = jax.nn.softmax(jnp.concatenate([s2, sink_b], axis=-1), axis=-1)[..., :C].astype(v_s.dtype)
    b = jnp.einsum('bkgqc,bckd->bqkgd', p2, v_s).reshape(B, C, SWA_WIDTH)
    return _merge(a, gate_a, b, gate_b, mg_a, mg_b, w_ba, w_bb, w_o)

def setup_inputs(seed: int = 0) -> dict:
    key = jax.random.key(seed)
    ks = jax.random.split(key, 20)
    D = D_MODEL

    def nrm(k, shape, fan_in):
        return jax.random.normal(k, shape, jnp.float32) * (fan_in ** -0.5)

    return {
        "x": jax.random.normal(ks[0], (BATCH, SEQ, D), jnp.float32),
        "c": jax.random.normal(ks[1], (BATCH, D), jnp.float32),
        "ctx": jax.random.normal(ks[2], (BATCH, CTX_LEN, D), jnp.float32),
        "c_ctx": jax.random.normal(ks[3], (D,), jnp.float32),
        "w_ada": nrm(ks[4], (DEPTH, D, 3 * D), D),
        "b_ada": 0.02 * jax.random.normal(ks[5], (DEPTH, 3 * D), jnp.float32),
        "norm_g": 1.0 + 0.02 * jax.random.normal(ks[6], (DEPTH, D), jnp.float32),
        "w_in": nrm(ks[7], (DEPTH, D, IN_WIDTH), D),
        "b_in": 0.02 * jax.random.normal(ks[8], (DEPTH, IN_WIDTH), jnp.float32),
        "q_norm_g": 1.0 + 0.02 * jax.random.normal(ks[9], (DEPTH, MLA_Q_RANK), jnp.float32),
        "kv_norm_g": 1.0 + 0.02 * jax.random.normal(ks[10], (DEPTH, MLA_KV_RANK), jnp.float32),
        "w_uq": nrm(ks[11], (DEPTH, MLA_Q_RANK, MLA_HEADS * (MLA_NOPE + MLA_ROPE)), MLA_Q_RANK),
        "w_ukv": nrm(ks[12], (DEPTH, MLA_KV_RANK, MLA_HEADS * (MLA_NOPE + MLA_V)), MLA_KV_RANK),
        "sink": jax.random.normal(ks[13], (DEPTH, SWA_HEADS), jnp.float32),
        "w_branch_a": nrm(ks[14], (DEPTH, MLA_WIDTH, D), MLA_WIDTH),
        "w_branch_b": nrm(ks[15], (DEPTH, SWA_WIDTH, D), SWA_WIDTH),
        "w_out": nrm(ks[16], (DEPTH, D, D), D),
        "final_g": 1.0 + 0.02 * jax.random.normal(ks[17], (D,), jnp.float32),
    }

def reference(x, c, ctx, c_ctx, w_ada, b_ada, norm_g, w_in, b_in, q_norm_g, kv_norm_g,
              w_uq, w_ukv, sink, w_branch_a, w_branch_b, w_out, final_g):
    B, S, D = x.shape
    ROWS = S // GRID_W
    rows = jnp.repeat(jnp.arange(ROWS, dtype=jnp.int32), GRID_W)
    cols = jnp.tile(jnp.arange(GRID_W, dtype=jnp.int32), ROWS)
    s_c = jax.nn.silu(c)
    s_cc = jax.nn.silu(c_ctx)
    for l in range(DEPTH):
        shift, scale, gate = jnp.split((s_c @ w_ada[l] + b_ada[l])[:, None, :], 3, axis=-1)
        shift_c, scale_c, gate_c = jnp.split(s_cc @ w_ada[l] + b_ada[l], 3)
        h = _rmsnorm(x, norm_g[l]) * (1 + scale) + shift
        h_c = _rmsnorm(ctx, norm_g[l]) * (1 + scale_c) + shift_c

        lat = _branch_inputs(h, w_in[l], b_in[l], q_norm_g[l], kv_norm_g[l], w_uq[l], w_ukv[l])
        cx = _branch_inputs(h_c, w_in[l], b_in[l], q_norm_g[l], kv_norm_g[l], w_uq[l], w_ukv[l])
        q_mla, k_nope, v_mla, k_pe, gate_a, q_s, k_s, v_s, gate_b, mg_a, mg_b = lat

        q_mla = jnp.concatenate([q_mla[..., :MLA_NOPE], _rope_2d(q_mla[..., MLA_NOPE:], rows, cols)], axis=-1)
        k_mla = _mla_keys(k_nope, _rope_2d(k_pe, rows, cols))
        q_s = _rope_2d(q_s, rows, cols)
        k_s = _rope_2d(k_s, rows, cols)

        k_mla_ctx = _mla_keys(cx[1], cx[3])
        a_heads = _mla_latent(q_mla, k_mla, v_mla, k_mla_ctx, cx[2])
        b_heads = _swa_latent(q_s, k_s, v_s, cx[6], cx[7], sink[l])
        out = _merge(a_heads, gate_a, b_heads, gate_b, mg_a, mg_b, w_branch_a[l], w_branch_b[l], w_out[l])
        if l + 1 < DEPTH:
            ctx = ctx + gate_c * _context_mixer(cx, sink[l], w_branch_a[l], w_branch_b[l], w_out[l])
        x = x + gate * out
    return _rmsnorm(x, final_g)


_drawn_inputs = setup_inputs


def setup_inputs(seed=0):
    import zlib

    import numpy as np

    out = dict(_drawn_inputs(seed))
    spreads = {}
    factors = {'b_ada': 5.177,
     'norm_g': 8.0,
     'b_in': 7.587,
     'q_norm_g': 8.0,
     'kv_norm_g': 8.0,
     'sink': 8.0,
     'final_g': 2.826}
    for name, (base, spread) in spreads.items():
        noise = np.random.default_rng([zlib.crc32(name.encode()), seed]).standard_normal(out[name].shape)
        drawn = base * np.exp(spread * noise) if base else spread * noise
        out[name] = __import__('jax').numpy.asarray(drawn.astype(out[name].dtype))
    for name, factor in factors.items():
        out[name] = (out[name] * factor).astype(out[name].dtype)
    return out
```

```python
import concourse.bass as bass
from concourse import mybir
from contextlib import ExitStack

F32 = mybir.dt.float32
F32R = mybir.dt.float32r
ALU = mybir.AluOpType
ACT = mybir.ActivationFunctionType
AX = mybir.AxisListType

P = 128
D = 2048
SEQ, CTX = 512, 256
TOK = SEQ + CTX
KT = D // P
EPS = 1e-6
NEG = -1e30
RANK = 512
RT = RANK // P
MLA_HEADS, NOPE, ROPE = 8, 128, 64
MLA_SCALE = float(NOPE + ROPE) ** -0.5
SWA_HEADS, KV_GROUPS, HD = 16, 4, 64
GROUP = SWA_HEADS // KV_GROUPS
SWA_SCALE = float(HD) ** -0.5
QB = SEQ // P
CB = CTX // P
UNIT = 1024

Z_TILES = 13
U_Z = 0
U_SWA = U_Z + 2 * Z_TILES
U_MLA = U_SWA + KV_GROUPS * 8
U_MG = U_MLA + MLA_HEADS * 4
U_OUT = U_MG + KT * 6
U_END = U_OUT + 32
B_SWA, B_MLA, B_MG = 13, 13 + 16, 13 + 16 + 8
B_END = B_MG + 32
ADA_FIRST, ADA_ALL = 64, 96
RAWS, WS = 4, 2
AHEAD = 5


def raw_count(u, gate_done):
    return u // RAWS + 1 + ADA_FIRST // RAWS + ((ADA_ALL - ADA_FIRST) // RAWS if gate_done else 0)


def build(nc, xT_d, x_d, cT_d, ada_d, b_adaT_d, b_gate_d, norm_gT_d, stream_d, biasT_d, qn_gT_d, kvn_gT_d,
          sink_d, final_g_d, cos_d, sin_d, rot_d, ident_d, masks_d, out_d):
    es = ExitStack()
    with es:
        base = (nc.sbuf_base + 63) // 64 * 64
        KB = 1024

        def at(name, off_kb, shape, dt=F32):
            return nc.alloc_sbuf_tensor_at(name, shape, dt, offset=base + int(off_kb * KB))

        def sem(name):
            return es.enter_context(nc.semaphore(name))

        h_hi = at("h_hi", 0, [P, KT, SEQ], F32R)
        h_lo = at("h_lo", 32, [P, KT, SEQ], F32R)
        m_hi = at("m_hi", 0, [P, KT, SEQ], F32R)
        m_lo = at("m_lo", 32, [P, KT, SEQ], F32R)
        raw = at("raw", 64, [P, RAWS, UNIT])
        w_hi = at("w_hi", 80, [P, WS, UNIT], F32R)
        w_lo = at("w_lo", 88, [P, WS, UNIT], F32R)
        cos = at("cos", 96, [P, SEQ])
        sin = at("sin", 98, [P, SEQ])
        ident = at("ident", 100, [P, P])
        ident_r = at("ident_r", 100.5, [P, P], F32R)
        rot = at("rot", 101, [P, P])
        masks_r = at("masks_r", 101.5, [P, 2, P], F32R)
        ones = at("ones", 102.5, [P, P])
        small = at("small", 103, [P, 512])
        D0 = 105
        bias = small[:, 0:B_END]
        nbias = small[:, 72:72 + B_END]
        cT = small[:, 144:176].rearrange("p (k v) -> p k v", v=2)
        silu_c = small[:, 176:208].rearrange("p (k v) -> p k v", v=2)
        norm_g = small[:, 208:240].rearrange("p (k v) -> p k v", v=2)
        shift = small[:, 240:272].rearrange("p (k v) -> p k v", v=2)
        scale1 = small[:, 272:304].rearrange("p (k v) -> p k v", v=2)
        mod = small[:, 240:304].rearrange("p (k v) -> p k v", v=2)
        b_ada = small[:, 304:368].rearrange("p (k v) -> p k v", v=2)
        qn_g = small[:, 368:368 + RT]
        kvn_g = small[:, 372:372 + RT]
        eps_c = small[:, 376:377]
        neg_max = small[:, 378:380]
        row_sum = small[:, 380:382]
        row_inv = small[:, 382:384]
        sink = small[0:1, 384:400]
        sink8 = small[0:1, 460:476]
        sumsq = small[:, 400:416]
        tok_ms = small[:, 416:420]
        tok_inv = small[:, 456:460]
        neg_raw = small[:, 420:422]
        silu_e = small[:, 424:456].rearrange("p (k v) -> p k v", v=2)

        xT = at("xT", D0 + 22, [P, KT, TOK])
        hc_hi = at("hc_hi", D0 + 70, [P, KT, CTX], F32R)
        hc_lo = at("hc_lo", D0 + 86, [P, KT, CTX], F32R)
        sq = at("sq", D0 + 0, [P, TOK])
        sq_sum = at("sq_sum", D0 + 3, [P, TOK])
        rstd = at("rstd", D0 + 6, [P, TOK])
        ada_rows = at("ada_rows", D0 + 9, [2, 2, 512])
        masks_f = at("masks_f", D0 + 13, [P, 2, P])
        ckv = at("ckv", D0 + 0, [P, RT, TOK])
        cq = at("cq", D0 + 12, [P, RT, SEQ])
        kpe_hi = at("kpe_hi", D0 + 20, [P, TOK], F32R)
        kpe_lo = at("kpe_lo", D0 + 23, [P, TOK], F32R)
        ks_f = at("ks_f", D0 + 26, [P, 2, TOK])
        vT_f = at("vT_f", D0 + 32, [P, 2, TOK])
        kraw = at("kraw", D0 + 38, [P, 2, TOK])
        krot = at("krot", D0 + 44, [P, SEQ])
        nsq = at("nsq", D0 + 46, [P, 2, TOK])
        nrstd = at("nrstd", D0 + 52, [P, 2, TOK])
        q_st = at("q_st", D0 + 38, [P, GROUP, SEQ], F32R)
        k_hi2 = at("k_hi2", D0 + 46, [P, TOK], F32R)
        k_lo2 = at("k_lo2", D0 + 49, [P, TOK], F32R)
        v_st = at("v_st", D0 + 52, [P, QB + CB, P], F32R)
        spt_hi = at("spt_hi", D0 + 55, [P, 5, GROUP, P], F32R)
        spt_lo = at("spt_lo", D0 + 65, [P, 5, GROUP, P], F32R)
        sprob = at("sprob", D0 + 75, [P, 2, 5 * P + 1])
        q_hiT = at("q_hiT", D0 + 80.25, [P, SEQ], F32R)
        s_gate = at("s_gate", D0 + 82.25, [P, 2, SEQ])
        b_T = at("b_T", D0 + 86.25, [P, 2, SEQ])
        s_stage = at("s_stage", D0 + 90.25, [P, 2, SEQ], F32R)
        qf2 = at("qf2", D0 + 94.25, [P, 2, SEQ])
        gate_e = qf2
        qt = at("qt", D0 + 98.25, [P, SEQ])
        o_low = at("o_low", D0 + 100.25, [64, SEQ])
        qn_hi = at("qn_hi", D0 + 0, [P, SEQ], F32R)
        qn_lo = at("qn_lo", D0 + 2, [P, SEQ], F32R)
        qr_st = at("qr_st", D0 + 4, [P, SEQ], F32R)
        kn_hi = at("kn_hi", D0 + 6, [P, TOK], F32R)
        kn_lo = at("kn_lo", D0 + 9, [P, TOK], F32R)
        v_hi = at("v_hi", D0 + 12, [P, QB + CB, P], F32R)
        v_lo = at("v_lo", D0 + 15, [P, QB + CB, P], F32R)
        qrf = at("qrf", D0 + 18, [64, SEQ])
        ckv_hi = at("ckv_hi", D0 + 26, [P, RT, TOK], F32R)
        ckv_lo = at("ckv_lo", D0 + 38, [P, RT, TOK], F32R)
        cq_hi = at("cq_hi", D0 + 50, [P, RT, SEQ], F32R)
        cq_lo = at("cq_lo", D0 + 58, [P, RT, SEQ], F32R)
        pt_hi = at("pt_hi", D0 + 66, [P, QB + CB, SEQ], F32R)
        pt_lo = at("pt_lo", D0 + 78, [P, QB + CB, SEQ], F32R)
        prob = at("prob", D0 + 90, [P, 2, TOK])
        a_gate = at("a_gate", D0 + 96, [P, SEQ])
        a_stage = at("a_stage", D0 + 98, [P, 2, SEQ], F32R)
        A = at("A", D0 + 0, [P, 2, 8, SEQ], F32R)
        B = at("B", D0 + 32, [P, 2, 8, SEQ], F32R)
        m_f = at("m_f", D0 + 64, [P, KT, SEQ])
        sg_a = at("sg_a", D0 + 96, [P, SEQ])
        sg_b = at("sg_b", D0 + 98, [P, SEQ])
        y = at("y", D0 + 0, [P, QB, D])
        gate_bc = at("gate_bc", D0 + 32, [P, D])
        fin_g = at("fin_g", D0 + 40, [P, D])
        gate_rows = at("gate_rows", D0 + 48, [2, 2, 512])
        y_add = at("y_add", D0 + 52, [P, QB, 512])
        y_sq = at("y_sq", D0 + 60, [P, 512])

        spill_a = nc.dram_tensor("spill_a", [8, P, 2, SEQ], F32, kind="Internal").ap()
        spill_b = nc.dram_tensor("spill_b", [8, P, 2, SEQ], F32, kind="Internal").ap()

        ps = es.enter_context(nc.psum_tensor("ps", [P, 8, 512], F32))

        def two_banks(b):
            return ps[:, b:b + 2, :].rearrange("p b n -> p (b n)")

        def sems(names):
            return [sem(n) for n in names.split()]

        raw_full = [sem(f"raw_full{s}") for s in range(RAWS)]
        w_hi_done, w_lo_done, w_used = sems("w_hi_done w_lo_done w_used")
        const_in, x_in, late_in, y_in, ab_in = sems("const_in x_in late_in y_in ab_in")
        const_made, const_r, nbias_made, silu_exp, silu_step, silu_ready = sems("const_made const_r nbias_made silu_exp silu_step silu_ready")
        ada_used, ada_row_ready, ada_col_ready, ada_col_out, scale_made = sems("ada_used ada_row_ready ada_col_ready ada_col_out scale_made")
        sq_made, sq_added, x_sum, x_root, x_rstd, x_normed = sems("sq_made sq_added x_sum x_root x_rstd x_normed")
        h_made, h_hi_done, h_ready = sems("h_made h_hi_done h_ready")
        z_bank_free, z_lat_out, z_rest_out, k_rot_ready, k_step, k_roped = sems("z_bank_free z_lat_out z_rest_out k_rot_ready k_step k_roped")
        kpe_hi_done, kpe_lo_done, v_T_ready, v_T_out = sems("kpe_hi_done kpe_lo_done v_T_ready v_T_out")
        n_sq, n_sum, n_root, n_rstd, n_scaled, n_hi, n_lo = sems("rank_squared rank_summed rank_root rank_rstd rank_scaled rank_hi rank_lo")
        swa_q_out, swa_q_rotated, swa_q_step, swa_q_mixed, swa_q_hi, swa_q_lo = sems("swa_q_out swa_q_rotated swa_q_step swa_q_mixed swa_q_hi swa_q_lo")
        swa_k_hi, swa_k_lo, swa_v_hi, swa_v_lo = sems("swa_k_hi swa_k_lo swa_v_hi swa_v_lo")
        swa_s, swa_max, swa_negmax, swa_exp, swa_inv, swa_prob = sems("swa_scores swa_max swa_negmax swa_exp swa_inv swa_prob")
        swa_pT, swa_pT_hi, swa_pT_lo, swa_out, swa_out_low, swa_out_free = sems("swa_probT swa_probT_hi swa_probT_lo swa_out swa_out_low swa_out_free")
        swa_gate_z, swa_gate_exp, swa_gate_step, swa_gated, swa_gated_hi, swa_gated_lo, swa_spilled = sems(
            "swa_gate_z swa_gate_exp swa_gate_step swa_gated swa_gated_hi swa_gated_lo swa_spilled")
        swa_bank7_free = sem("swa_bank7_free")
        mla_q_proj, mla_k_proj, mla_qk_hi, mla_qk_lo, mla_qr_out, mla_q_rotated, mla_q_step, mla_q_mixed, mla_qr_hi, mla_qr_lo = sems(
            "mla_q_proj mla_k_proj mla_qk_hi mla_qk_lo mla_qr_out mla_q_rotated mla_q_step mla_q_mixed mla_qr_hi mla_qr_lo")
        mla_v_out, mla_v_T, mla_v_hi, mla_v_lo = sems("mla_v_out mla_v_T mla_v_hi mla_v_lo")
        mla_s, mla_max, mla_negmax, mla_exp, mla_inv, mla_prob = sems("mla_scores mla_max mla_negmax mla_exp mla_inv mla_prob")
        mla_pT, mla_pT_hi, mla_pT_lo, mla_out = sems("mla_probT mla_probT_hi mla_probT_lo mla_out")
        mla_gate_z, mla_gate_exp, mla_gate_step, mla_free, mla_gated_hi, mla_gated_lo, mla_spilled = sems(
            "mla_gate_z mla_gate_exp mla_gate_step mla_free mla_gated_hi mla_gated_lo mla_spilled")
        mg_exp, mg_step, mg_free = sems("merge_exp merge_step merge_free")
        m_hi_done, m_ready, gate_row_ready, gate_bc_sum, gate_ready = sems("m_hi_done m_ready gate_row_ready gate_bc_sum gate_ready")
        o_free, o_added, o_squared, o_ms, o_root, o_inv, o_final, stored = sems("out_free out_added out_squared out_ms out_root out_inv out_final stored")


        def vT_of(r, par):
            return vT_f[:, bass.ds(r, 1), :].rearrange("p a (k n) -> p (a k) n", n=P)[:, :, 64 * par:64 * par + 64]

        def key_blocks(b):
            return list(range(max(b - 1, 0), min(b + 1, QB - 1) + 1)) + list(range(QB, QB + CB))

        block = es.enter_context(nc.Block())

        @block.sync
        def _(sp):
            consts = [(cT, cT_d), (b_ada, b_adaT_d), (norm_g, norm_gT_d), (bias, biasT_d), (qn_g, qn_gT_d),
                      (kvn_g, kvn_gT_d), (sink, sink_d), (ident[:, :], ident_d), (rot[:, :], rot_d),
                      (masks_f[:, :, :], masks_d), (cos[:, :], cos_d), (sin[:, :], sin_d)]
            for dst, src in consts:
                sp.dma_start(dst, src).then_inc(const_in, 16)
            for a in range(RAWS):
                sp.dma_start(raw[:, a, :], ada_d[a]).then_inc(raw_full[a], 16)
            for part in range(4):
                sp.dma_start(xT[:, 4 * part:4 * part + 4, :], xT_d[:, 4 * part:4 * part + 4, :]).then_inc(x_in, 16)
            with sp.Fori(1, ADA_FIRST // RAWS) as r:
                for s in range(RAWS):
                    sp.wait_ge(ada_used, r * RAWS + (s - RAWS + 1))
                    sp.dma_start(raw[:, s, :], ada_d[bass.ds(r * RAWS + s, 1)].rearrange("u p n -> (u p) n")).then_inc(raw_full[s], 16)
            for u in range(RAWS):
                sp.wait_ge(ada_used, ADA_FIRST - RAWS + 1 + u)
                sp.dma_start(raw[:, u, :], stream_d[u]).then_inc(raw_full[u], 16)

            def load(u, s):
                sp.wait_ge(w_lo_done, u - (RAWS - 1))
                sp.dma_start(raw[:, s, :], stream_d[bass.ds(u, 1)].rearrange("u p n -> (u p) n")).then_inc(raw_full[s], 16)

            def spill(dst, stage, hi_done, lo_done, n, spilled):
                sp.wait_ge(hi_done, n)
                sp.wait_ge(lo_done, n)
                sp.dma_start(dst.rearrange("t p v n -> (t p) v n"), stage.bitcast(F32)).then_inc(spilled, 16)

            with sp.Fori(1, (U_SWA + 2) // RAWS) as r:
                for s in range(RAWS):
                    load(r * RAWS + s, s)
            for u in range(U_SWA + 2, U_SWA + AHEAD):
                load(u, u % RAWS)
            with sp.Fori(0, 2) as r:
                for par in range(2):
                    for c in range(8):
                        load(U_SWA + AHEAD + c + par * 8 + r * 16, (U_SWA + AHEAD + c) % RAWS)
                    for j in range(2):
                        spill(spill_b[bass.ds(r * 4 + par * 2 + j, 1)], s_stage[:, :, :], swa_gated_hi, swa_gated_lo,
                              r * 4 + (par * 2 + j + 1), swa_spilled)
            with sp.Fori(0, MLA_HEADS) as h:
                for c in range(4):
                    load(U_MLA + AHEAD + c + h * 4, (U_MLA + AHEAD + c) % RAWS)
                spill(spill_a[bass.ds(h, 1)], a_stage[:, :, :], mla_gated_hi, mla_gated_lo, h + 1, mla_spilled)
            sp.wait_ge(swa_spilled, 9 * 16)
            sp.wait_ge(mla_spilled, 9 * 16)
            for v in range(2):
                sp.dma_start(A[:, v, :, :].bitcast(F32), spill_a[:, :, v, :].rearrange("t p n -> p t n")).then_inc(ab_in, 16)
                sp.dma_start(B[:, v, :, :].bitcast(F32), spill_b[:, :, v, :].rearrange("t p n -> p t n")).then_inc(ab_in, 16)
            n_loop = (U_OUT - U_MG - AHEAD) // RAWS
            with sp.Fori(0, n_loop) as r:
                for c in range(RAWS):
                    load(U_MG + AHEAD + c + r * RAWS, (U_MG + AHEAD + c) % RAWS)
            for u in range(U_MG + AHEAD + n_loop * RAWS, U_OUT):
                load(u, u % RAWS)
            sp.wait_ge(w_used, U_OUT)
            sp.wait_ge(mg_free, KT + 2)
            sp.dma_start(y[:, :, :], x_d.rearrange("(t p) d -> p t d", p=P)).then_inc(y_in, 16)
            sp.dma_start(gate_bc[:, :], b_gate_d).then_inc(late_in, 16)
            sp.dma_start(fin_g[:, :], final_g_d).then_inc(late_in, 16)
            for a in range(ADA_FIRST, ADA_FIRST + RAWS):
                sp.wait_ge(w_lo_done, U_OUT)
                sp.dma_start(raw[:, a % RAWS, :], ada_d[a]).then_inc(raw_full[a % RAWS], 16)
            with sp.Fori(ADA_FIRST // RAWS + 1, ADA_ALL // RAWS) as r:
                for s in range(RAWS):
                    sp.wait_ge(ada_used, r * RAWS + (s - RAWS + 1))
                    sp.dma_start(raw[:, s, :], ada_d[bass.ds(r * RAWS + s, 1)].rearrange("u p n -> (u p) n")).then_inc(raw_full[s], 16)
            sp.wait_ge(ada_used, ADA_ALL)
            for u in range(U_OUT, U_OUT + RAWS):
                sp.dma_start(raw[:, u % RAWS, :], stream_d[u]).then_inc(raw_full[u % RAWS], 16)
            with sp.Fori(0, (U_END - U_OUT - RAWS) // RAWS) as r:
                for c in range(RAWS):
                    load(U_OUT + RAWS + r * RAWS + c, (U_OUT + c) % RAWS)
            for t in range(QB):
                sp.wait_ge(o_final, t + 1)
                sp.dma_start(out_d[t * P:(t + 1) * P, :], y[:, t, :]).then_inc(stored, 16)
            sp.wait_ge(stored, QB * 16)

        @block.gpsimd
        def _(g):
            def split_lo(u, s, w):
                g.wait_ge(w_hi_done, u + 1)
                g.tensor_tensor(w_lo[:, w, :], raw[:, s, :], w_hi[:, w, :].bitcast(F32), ALU.subtract).then_inc(w_lo_done, 1)

            with g.Fori(0, U_END // RAWS) as r:
                for s in range(RAWS):
                    split_lo(r * RAWS + s, s, s % WS)
            for u in range(U_END // RAWS * RAWS, U_END):
                split_lo(u, u % RAWS, u % WS)

        @block.tensor
        def _(pe):
            mm = nc.tensor.matmul
            PASS = ((w_hi, 0), (w_hi, 1), (w_lo, 0))

            def ada_unit(a, s, bank, first, last):
                for half in range(2):
                    ins = mm(ps[0:2, bank, :], silu_c[:, 2 * a + half, :], raw[:, s, half * 512:half * 512 + 512],
                             start=first and half == 0, stop=last and half == 1)
                ins.then_inc(ada_used, 1)

            def columns(n_done, slot, bank):
                pe.wait_ge(ada_row_ready, n_done)
                for f in range(4):
                    ins = mm(ps[:, bank, 2 * f:2 * f + 2], ada_rows[0:2, slot, f * P:f * P + P], ident[0:2, 0:2],
                             start=True, stop=True)
                ins.then_inc(ada_col_ready, 1)

            pe.wait_ge(const_in, 12 * 16)
            pe.wait_ge(const_made, 1)
            pe.wait_ge(const_r, 2)
            pe.wait_ge(nbias_made, 1)
            pe.wait_ge(silu_ready, 1)
            def ada_round(r):
                for half in range(2):
                    for a in range(8):
                        pe.wait_ge(raw_full[a % RAWS], (r * 4 + (half * 2 + a // 4 + 1)) * 16)
                        ada_unit(a, a % RAWS, half, a == 0, a == 7)
                for half in range(2):
                    pe.wait_ge(ada_col_out, r * 2 + (half + 1))
                    columns(r * 2 + (half + 1), half, 2 + half)
            with pe.Fori(0, 2) as r:
                ada_round(r)
            pe.wait_ge(sq_added, KT)
            mm(ps[:, 4, :], ones[:, :], sq_sum[:, 0:SEQ], start=True, stop=True)
            mm(ps[:, 5, 0:CTX], ones[:, :], sq_sum[:, SEQ:TOK], start=True, stop=True).then_inc(x_sum, 1)
            with pe.Fori(2, 4) as r:
                ada_round(r)

            def proj(w, kts, lat, ctx, k0=0, last_k=KT):
                for k in kts:
                    kk = k - k0
                    for n, (wt, lo) in enumerate(PASS):
                        wk = wt[:, w, kk * P:kk * P + P]
                        st, sp_ = k == 0 and n == 0, k == last_k - 1 and n == 2
                        ins = mm(lat, wk, (h_lo if lo else h_hi)[:, k, :], start=st, stop=sp_)
                        if ctx is not None:
                            ins = mm(ctx, wk, (hc_lo if lo else hc_hi)[:, k, :], start=st, stop=sp_)
                return ins

            def proj_tile(u, par, lat, ctx, first=False):
                for half in range(2):
                    pe.wait_ge(w_lo_done, u + half + 1)
                    if first:
                        for k in range(half * 8, half * 8 + 8):
                            pe.wait_ge(h_ready, k + 1)
                            ins = proj((par + half) % WS, [k], lat, ctx, half * 8)
                    else:
                        ins = proj((par + half) % WS, range(half * 8, half * 8 + 8), lat, ctx, half * 8)
                    ins.then_inc(w_used, 1)

            proj_tile(0, 0, ps[:, 0, :], ps[:, 2, 0:CTX], first=True)
            proj_tile(2, 0, ps[:, 1, :], None)
            with pe.Fori(1, RT) as r:
                pe.wait_ge(z_bank_free, r * 3 - 1)
                proj_tile(r * 4, 0, ps[:, 0, :], ps[:, 2, 0:CTX])
                pe.wait_ge(z_bank_free, r * 3)
                proj_tile(r * 4 + 2, 0, ps[:, 1, :], None)
            pe.wait_ge(z_bank_free, 3 * RT)
            def after_tile(t):
                pe.wait_ge(z_rest_out, t + 1)
                if t < 3:
                    m = 64 if t == 0 else P
                    if t >= 1:
                        pe.wait_ge(k_roped, t)
                    mm(ps[:, 4, :], rot[0:m, :], kraw[0:m, t % 2, 0:SEQ], start=True, stop=True).then_inc(k_rot_ready, 1)
                else:
                    if t == 4:
                        pe.wait_ge(v_T_out, 1)
                    for k in range(QB + CB):
                        ins = nc.tensor.transpose(two_banks(5)[:, k * P:k * P + P], kraw[:, t % 2, k * P:k * P + P], ident[:, :])
                    ins.then_inc(v_T_ready, 1)

            for t in range(5):
                b = t % 2
                if t >= 2:
                    pe.wait_ge(z_rest_out, t - 1)
                proj_tile(16 + 2 * t, 0, ps[:, b, :], ps[:, 2 + b, 0:CTX])
                if t >= 1:
                    after_tile(t - 1)
            after_tile(4)
            pe.wait_ge(v_T_out, 2)
            for k in range(RT):
                pe.wait_ge(n_sq, 2 * k + 1)
                mm(ps[:, 5, :], ones[:, :], nsq[:, 0, 0:SEQ], start=k == 0, stop=k == RT - 1)
                mm(ps[:, 6, 0:CTX], ones[:, :], nsq[:, 0, SEQ:TOK], start=k == 0, stop=k == RT - 1).then_inc(n_sum, 1)
                pe.wait_ge(n_sq, 2 * k + 2)
                mm(ps[:, 7, :], ones[:, :], nsq[:, 1, 0:SEQ], start=k == 0, stop=k == RT - 1).then_inc(n_sum, 1)

            def swa_scores(r, par, s):
                b, n = s // GROUP, s % GROUP
                sb = two_banks(2 * (s % 2))
                lo, hi = max(b - 1, 0), min(b + 1, QB - 1)
                wn = (hi - lo + 1) * P
                if s >= 2:
                    pe.wait_ge(swa_exp, r * 32 + (par * 16 + s - 1))
                q = q_st[:, n, b * P:b * P + P]
                mm(sb[:, 512 - wn:512], q, k_hi2[:, lo * P:hi * P + P], start=True, stop=False)
                mm(sb[:, 512 - wn:512], q, k_lo2[:, lo * P:hi * P + P], start=False, stop=False)
                if b > 0:
                    mm(sb[:, 512 - wn:512 - wn + P], ident_r[:, :], masks_r[:, 0, :], start=False, stop=b == QB - 1)
                if b < QB - 1:
                    mm(sb[:, 384:512], ident_r[:, :], masks_r[:, 1, :], start=False, stop=True)
                mm(sb[:, 512:768], q, k_hi2[:, SEQ:TOK], start=True, stop=False)
                mm(sb[:, 512:768], q, k_lo2[:, SEQ:TOK], start=False, stop=True)
                mm(sb[:, 768:769], ones[0:1, :], sink8[0:1, bass.ds(r * 8 + (par * 4 + n), 1)], start=True, stop=True).then_inc(swa_s, 1)

            def swa_transpose(r, par, s):
                tb = two_banks(4)
                pe.wait_ge(swa_prob, r * 32 + (par * 16 + s + 1))
                if s >= 1:
                    pe.wait_ge(swa_pT_lo, r * 32 + (par * 16 + s))
                for k in range(len(key_blocks(s // GROUP))):
                    ins = nc.tensor.transpose(tb[:, k * P:k * P + P], sprob[:, s % 2, k * P:k * P + P], ident[:, :])
                ins.then_inc(swa_pT, 1)

            def swa_values(r, par, b):
                blocks = key_blocks(b)
                pe.wait_ge(swa_pT_lo, r * 32 + (par * 16 + 4 * b + 4))
                pe.wait_ge(swa_out_free, r * 8 + (par * 4 + b + 1))
                for k, kb in enumerate(blocks):
                    mm(ps[:, 6, :], v_st[:, kb, :], spt_hi[:, k, :, :].rearrange("p g n -> p (g n)"), start=k == 0, stop=False)
                    ins = mm(ps[:, 6, :], v_st[:, kb, :], spt_lo[:, k, :, :].rearrange("p g n -> p (g n)"),
                             start=False, stop=k == len(blocks) - 1)
                ins.then_inc(swa_out, 1)

            pe.wait_ge(n_root, 3)
            with pe.Fori(0, 2) as r:
                for par in range(2):
                    u0 = U_SWA + par * 8
                    for j in range(2):
                        if j == 1:
                            pe.wait_ge(swa_out_free, r * 8 + (par * 4 + 1))
                        elif par == 1:
                            pe.wait_ge(swa_gate_z, r * 4 + 2)
                        else:
                            pe.wait_ge(swa_bank7_free, r + 1)
                        proj_tile(u0 + 2 * j + r * 16, 0, ps[:, 7 - j, :], None)
                    for j in range(2):
                        pe.wait_ge(swa_q_out, r * 4 + (par * 2 + j + 1))
                        mm(ps[:, 4 + j, :], rot[:, :], qf2[:, j, :], start=True, stop=True).then_inc(swa_q_rotated, 1)
                    pe.wait_ge(swa_q_lo, r * 4 + (par * 2 + 2))
                    pe.wait_ge(swa_q_hi, r * 4 + (par * 2 + 2))
                    pe.wait_ge(swa_k_lo, r * 2 + (par + 1))
                    pe.wait_ge(swa_v_lo, r * 2 + (par + 1))
                    swa_scores(r, par, 0)
                    for s in range(16):
                        if s < 15:
                            swa_scores(r, par, s + 1)
                        f = s // 4
                        if s % 4 == 0:
                            pe.wait_ge(w_lo_done, u0 + 4 + f + 1 + r * 16)
                        if s == 8:
                            pe.wait_ge(swa_gate_z, r * 4 + (par * 2 + 1))
                        k0 = (f % 2) * 8
                        k = k0 + 2 * (s % 4)
                        ins = proj(f % WS, [k, k + 1], ps[:, 7, :], None, k0)
                        if s % 4 == 3:
                            ins.then_inc(w_used, 1)
                        swa_transpose(r, par, s)
                        if s % GROUP == GROUP - 1:
                            swa_values(r, par, s // GROUP)

            def mla_proj(u, w, passes):
                for out, c0, mhi, mlo in passes:
                    for k in range(RT):
                        for n, (wt, lo) in enumerate(PASS):
                            ins = mm(out, wt[:, w, k * 256 + c0:k * 256 + c0 + P], (mlo if lo else mhi)(k),
                                     start=k == 0 and n == 0, stop=k == RT - 1 and n == 2)
                return ins

            def mla_scores(h, s):
                sb = two_banks(2 * (s % 2))
                if s >= 2:
                    pe.wait_ge(mla_exp, h * QB + (s - 1))
                q = slice(s * P, s * P + P)
                parts = ((qn_hi, kn_hi), (qn_lo, kn_hi), (qn_hi, kn_lo), (qr_st, kpe_hi), (qr_st, kpe_lo))
                for c0, c1 in ((0, SEQ), (SEQ, TOK)):
                    for n, (qq, kk) in enumerate(parts):
                        ins = mm(sb[:, c0:c1], qq[:, q], kk[:, c0:c1], start=n == 0, stop=n == len(parts) - 1)
                ins.then_inc(mla_s, 1)

            def mla_transpose(h, s):
                tb = two_banks(4)
                pe.wait_ge(mla_prob, h * QB + (s + 1))
                if s >= 1:
                    pe.wait_ge(mla_pT_lo, h * QB + s)
                for k in range(QB + CB):
                    ins = nc.tensor.transpose(tb[:, k * P:k * P + P], prob[:, s % 2, k * P:k * P + P], ident[:, :])
                ins.then_inc(mla_pT, 1)

            pe.wait_ge(n_lo, 2 * RT)
            pe.wait_ge(n_hi, 2 * RT)
            pe.wait_ge(swa_gate_z, 8)
            pe.wait_ge(swa_out_free, 17)
            lat = slice(0, SEQ)
            with pe.Fori(0, MLA_HEADS) as h:
                u0 = U_MLA
                pe.wait_ge(w_lo_done, h * 4 + (u0 + 1))
                pe.wait_ge(mla_free, h + 1)
                mla_proj(0, 0, [(ps[:, 7, :], 0, lambda k: cq_hi[:, k, :], lambda k: cq_lo[:, k, :])]).then_inc(mla_q_proj, 1)
                mla_proj(0, 0, [(ps[:, 6, :], P, lambda k: cq_hi[:, k, :], lambda k: cq_lo[:, k, :])]).then_inc(w_used, 1)
                pe.wait_ge(w_lo_done, h * 4 + (u0 + 2))
                for c0, b in ((0, 0), (P, 2)):
                    ins = mla_proj(0, 1, [
                        (ps[:, b, :], c0, lambda k: ckv_hi[:, k, 0:SEQ], lambda k: ckv_lo[:, k, 0:SEQ]),
                        (ps[:, b + 1, 0:CTX], c0, lambda k: ckv_hi[:, k, SEQ:TOK], lambda k: ckv_lo[:, k, SEQ:TOK])])
                    if b == 0:
                        ins.then_inc(mla_k_proj, 1)
                        pe.wait_ge(mla_qr_out, h + 1)
                        mm(ps[:, 4, :], rot[0:64, :], qrf[:, :], start=True, stop=True).then_inc(mla_q_rotated, 1)
                    else:
                        ins.then_inc(w_used, 1)
                pe.wait_ge(mla_v_out, h + 1)
                pe.wait_ge(mla_q_mixed, h + 1)
                for k in range(QB + CB):
                    ins = nc.tensor.transpose(two_banks(4)[:, k * P:k * P + P], prob[:, 0, k * P:k * P + P], ident[:, :])
                ins.then_inc(mla_v_T, 1)
                pe.wait_ge(mla_qk_lo, h * 2 + 2)
                pe.wait_ge(mla_qr_lo, h + 1)
                pe.wait_ge(mla_v_lo, h + 1)
                mla_scores(h, 0)
                for s in range(QB):
                    if s < QB - 1:
                        mla_scores(h, s + 1)
                    if s % 2 == 0:
                        pe.wait_ge(w_lo_done, h * 4 + (u0 + 3 + s // 2))
                    k0 = (s // 2) * 8
                    ins = proj((s // 2) % WS, range(4 * s, 4 * s + 4), ps[:, 7, :], None, k0)
                    if s % 2 == 1:
                        ins.then_inc(w_used, 1)
                    mla_transpose(h, s)
                pe.wait_ge(mla_pT_lo, h * QB + QB)
                for k in range(QB + CB):
                    mm(ps[:, 6, :], v_hi[:, k, :], pt_hi[:, k, :], start=k == 0, stop=False)
                    mm(ps[:, 6, :], v_hi[:, k, :], pt_lo[:, k, :], start=False, stop=False)
                    ins = mm(ps[:, 6, :], v_lo[:, k, :], pt_hi[:, k, :], start=False, stop=k == QB + CB - 1)
                ins.then_inc(mla_out, 1)

            pe.wait_ge(mla_free, MLA_HEADS + 1)
            with pe.Fori(0, KT // 2) as r:
                for par in range(2):
                    u0 = U_MG + par * 6
                    b0 = 4 * par
                    pe.wait_ge(mg_free, r * 2 + (par + 1))
                    proj_tile(u0 + r * 12, 0, ps[:, b0, :], None)
                    proj_tile(u0 + 2 + r * 12, 0, ps[:, b0 + 1, :], None)
                    pe.wait_ge(ab_in, 64)
                    for j, x in enumerate((A, B)):
                        pe.wait_ge(w_lo_done, u0 + 4 + j + 1 + r * 12)
                        for k in range(8):
                            for n, (wt, lo) in enumerate(PASS):
                                ins = mm(ps[:, b0 + 2 + j, :], wt[:, j, k * P:k * P + P], x[:, lo, k, :],
                                         start=k == 0 and n == 0, stop=k == 7 and n == 2)
                        ins.then_inc(w_used, 1)

            pe.wait_ge(mg_free, KT + 2)
            for c in range(4):
                for a in range(8):
                    g = ADA_FIRST + c * 8 + a
                    n_main = (U_OUT - g % RAWS + RAWS - 1) // RAWS
                    pe.wait_ge(raw_full[g % RAWS], (n_main + g // RAWS + 1) * 16)
                    ada_unit(a, g % RAWS, c % 2, a == 0, a == 7)
                if c >= 1:
                    pe.wait_ge(gate_row_ready, c)
                    if c >= 3:
                        pe.wait_ge(gate_ready, c - 2)
                    mm(ps[:, 2 + (c - 1) % 2, :], ones[0:1, :], gate_rows[0:1, (c - 1) % 2, :], start=True, stop=True).then_inc(gate_bc_sum, 1)
            pe.wait_ge(gate_row_ready, 4)
            pe.wait_ge(gate_ready, 2)
            mm(ps[:, 3, :], ones[0:1, :], gate_rows[0:1, 1, :], start=True, stop=True).then_inc(gate_bc_sum, 1)

            pe.wait_ge(gate_ready, 4)
            with pe.Fori(0, 2) as r:
                for par in range(2):
                    for c in range(8):
                        pe.wait_ge(w_lo_done, U_OUT + par * 8 + c + 1 + r * 16)
                        for half in range(2):
                            k = 2 * c + half
                            if par == 0:
                                pe.wait_ge(m_ready, k + 1)
                            for t in range(QB):
                                if k == 0:
                                    pe.wait_ge(o_free, (r * 2 + par) * QB + (t + 1))
                                tt = slice(t * P, t * P + P)
                                mv = slice(half * 512, half * 512 + 512)
                                o = ps[:, 4 * par + t, :]
                                mm(o, m_hi[:, k, tt], w_hi[:, c % WS, mv], start=k == 0, stop=False)
                                mm(o, m_lo[:, k, tt], w_hi[:, c % WS, mv], start=False, stop=False)
                                ins = mm(o, m_hi[:, k, tt], w_lo[:, c % WS, mv], start=False, stop=k == KT - 1)
                        ins.then_inc(w_used, 1)

        @block.scalar
        def _(act):
            def split_hi(c, off=0, per=0, late=False):
                n = c // RAWS + 1 + ADA_FIRST // RAWS + ((ADA_ALL - ADA_FIRST) // RAWS if late else 0)
                act.wait_ge(raw_full[c % RAWS], (n if per == 0 else off * (per // RAWS) + n) * 16)
                if per or c >= WS:
                    act.wait_ge(w_used, c - 1 if per == 0 else off * per + (c - 1))
                act.copy(w_hi[:, c % WS, :], raw[:, c % RAWS, :]).then_inc(w_hi_done, 1)

            def biased(dst, src, b):
                return act.activation(dst, src, ACT.Identity, bias=b)

            act.wait_ge(const_in, 12 * 16)
            act.activation(silu_e, cT, ACT.Exp, scale=-1.0).then_inc(silu_exp, 1)
            act.copy(ident_r[:, :], ident[:, :]).then_inc(const_r, 1)
            act.copy(masks_r[:, :, :], masks_f[:, :, :]).then_inc(const_r, 1)

            def ada_round(r):
                for half in range(2):
                    act.wait_ge(ada_used, r * 16 + (half * 8 + 8))
                    act.wait_ge(ada_col_ready, r * 2 + (half + 1))
                    act.copy(ada_rows[:, half, :], ps[0:2, half, :]).then_inc(ada_row_ready, 1)

            with act.Fori(0, 2) as r:
                ada_round(r)
            act.wait_ge(x_sum, 1)
            act.wait_ge(const_made, 1)
            act.activation(rstd[:, 0:SEQ], ps[:, 4, :], ACT.Sqrt, scale=1.0 / D, bias=eps_c)
            act.activation(rstd[:, SEQ:TOK], ps[:, 5, 0:CTX], ACT.Sqrt, scale=1.0 / D, bias=eps_c).then_inc(x_root, 1)
            with act.Fori(2, 4) as r:
                ada_round(r)
            split_hi(0)
            split_hi(1)
            for k in range(KT):
                act.wait_ge(h_made, k + 1)
                act.copy(h_hi[:, k, :], xT[:, k, 0:SEQ])
                act.copy(hc_hi[:, k, :], xT[:, k, SEQ:TOK]).then_inc(h_hi_done, 1)

            def z_round(r, per):
                i = slice(r, r + 1) if per == 0 else bass.ds(r, 1)
                b0 = bias[:, 0:1] if per == 0 else bias[:, bass.ds(r * 2, 1)]
                b1 = bias[:, 1:2] if per == 0 else bias[:, bass.ds(r * 2 + 1, 1)]
                split_hi(2, r, per)
                act.wait_ge(w_used, r * 4 + 2)
                biased(ckv[:, i, 0:SEQ], ps[:, 0, :], b0).then_inc(z_bank_free, 1)
                biased(ckv[:, i, SEQ:TOK], ps[:, 2, 0:CTX], b0).then_inc(z_bank_free, 1)
                split_hi(3, r, per)
                split_hi(4, r, per)
                act.wait_ge(w_used, r * 4 + 4)
                biased(cq[:, i, :], ps[:, 1, :], b1).then_inc(z_bank_free, 1)
                split_hi(5, r, per)

            act.wait_ge(h_ready, KT)
            z_round(0, 0)
            with act.Fori(1, RT) as r:
                z_round(r, 4)
            for t in range(5):
                u = 16 + 2 * t
                split_hi(u + 2)
                act.wait_ge(w_used, u + 2)
                if t >= 2:
                    act.wait_ge(k_roped, t - 1)
                if t == 2:
                    act.wait_ge(kpe_lo_done, 1)
                biased(kraw[:, t % 2, 0:SEQ], ps[:, t % 2, :], bias[:, 8 + t:9 + t])
                biased(kraw[:, t % 2, SEQ:TOK], ps[:, 2 + t % 2, 0:CTX], bias[:, 8 + t:9 + t]).then_inc(z_rest_out, 1)
                split_hi(u + 3)
                if t == 1:
                    act.wait_ge(k_roped, 1)
                    act.copy(kpe_hi[0:64, :], kraw[0:64, 0, :])
                    act.copy(kpe_hi[64:P, :], kraw[0:64, 0, :]).then_inc(kpe_hi_done, 1)
                if t == 4:
                    act.wait_ge(v_T_ready, 1)
                    act.copy(vT_f[:, 0, :], two_banks(5)[:, 0:TOK]).then_inc(v_T_out, 1)
            act.wait_ge(v_T_ready, 2)
            act.copy(vT_f[:, 1, :], two_banks(5)[:, 0:TOK]).then_inc(v_T_out, 1)
            act.wait_ge(n_sum, 2 * RT)
            for row, cols, src in ((0, slice(0, SEQ), ps[:, 5, :]), (0, slice(SEQ, TOK), ps[:, 6, 0:CTX]), (1, slice(0, SEQ), ps[:, 7, :])):
                act.activation(nrstd[:, row, cols], src, ACT.Sqrt, scale=1.0 / RANK, bias=eps_c).then_inc(n_root, 1)
            act.wait_ge(n_scaled, 2 * RT)

            def swa_softmax(r, par, s):
                wn = P * len(key_blocks(s // GROUP)) + 1
                act.wait_ge(swa_negmax, r * 32 + (par * 16 + s + 1))
                if s >= 2:
                    act.wait_ge(swa_pT, r * 32 + (par * 16 + s - 1))
                act.activation(sprob[:, s % 2, 0:wn], two_banks(2 * (s % 2))[:, 769 - wn:769], ACT.Exp,
                               bias=neg_max[:, s % 2:s % 2 + 1], scale=SWA_SCALE,
                               accum_out=row_sum[:, s % 2:s % 2 + 1]).then_inc(swa_exp, 1)

            with act.Fori(0, 2) as r:
                for par in range(2):
                    u0 = U_SWA + par * 8
                    rows = slice(64 * par, 64 * par + 64)
                    kr = ks_f[rows, bass.ds(r, 1), :].rearrange("p a n -> p (a n)")
                    act.copy(k_hi2[0:64, :], kr)
                    act.copy(k_hi2[64:P, :], kr).then_inc(swa_k_hi, 1)
                    act.copy(v_st[:, :, 0:64], vT_of(r, par)).then_inc(swa_v_hi, 1)
                    for j in range(2):
                        split_hi(u0 + 2 * j + 2, r, 16)
                        act.wait_ge(w_used, r * 16 + (u0 + 2 * j + 2))
                        biased(qf2[:, j, :], ps[:, 7 - j, :], bias[:, bass.ds(r * 8 + (B_SWA + par * 4 + j), 1)]).then_inc(swa_q_out, 1)
                        split_hi(u0 + 2 * j + 3, r, 16)
                    for j in range(2):
                        act.wait_ge(swa_q_mixed, r * 4 + (par * 2 + j + 1))
                        act.copy(q_st[0:64, 2 * j, :], qf2[0:64, j, :])
                        act.copy(q_st[0:64, 2 * j + 1, :], qf2[64:P, j, :])
                        if j == 1:
                            act.wait_ge(swa_q_lo, r * 4 + (par * 2 + 1))
                        act.copy(q_hiT[64:P, :], qf2[64:P, j, :]).then_inc(swa_q_hi, 1)
                    swa_softmax(r, par, 0)
                    for s in range(16):
                        b, n = s // GROUP, s % GROUP
                        nb = len(key_blocks(b))
                        if s < 15:
                            swa_softmax(r, par, s + 1)
                        if s % 4 == 3:
                            split_hi(u0 + 4 + s // 4 + 2, r, 16)
                        act.wait_ge(swa_pT, r * 32 + (par * 16 + s + 1))
                        if n == 0 and b >= 1:
                            act.wait_ge(swa_out, r * 8 + (par * 4 + b))
                        act.copy(spt_hi[:, 0:nb, n, :], two_banks(4)[:, 0:nb * P].rearrange("p (k n) -> p k n", n=P)).then_inc(swa_pT_hi, 1)
                        if n == GROUP - 1:
                            act.wait_ge(swa_out, r * 8 + (par * 4 + b + 1))
                            act.copy(o_low[:, :], ps[64:P, 6, :]).then_inc(swa_out_low, 1)
                    for j in range(2):
                        act.wait_ge(swa_gate_z, r * 4 + (par * 2 + j + 1))
                        act.activation(gate_e[:, j, :], s_gate[:, j, :], ACT.Exp, scale=-1.0).then_inc(swa_gate_exp, 1)
                    for j in range(2):
                        n = par * 2 + j + 1
                        act.wait_ge(swa_gated, r * 4 + n)
                        act.wait_ge(swa_spilled, (r * 4 + n) * 16)
                        act.copy(s_stage[:, 0, :], b_T[:, j, :]).then_inc(swa_gated_hi, 1)

            act.wait_ge(swa_gated_lo, 8)
            for k in range(RT):
                act.copy(ckv_hi[:, k, :], ckv[:, k, :]).then_inc(n_hi, 1)
                act.copy(cq_hi[:, k, :], cq[:, k, :]).then_inc(n_hi, 1)
            act.wait_ge(n_lo, 2 * RT)
            act.wait_ge(swa_spilled, 9 * 16)

            def mla_softmax(h, s):
                act.wait_ge(mla_negmax, h * QB + (s + 1))
                if s >= 2:
                    act.wait_ge(mla_pT, h * QB + (s - 1))
                act.activation(prob[:, s % 2, :], two_banks(2 * (s % 2))[:, 0:TOK], ACT.Exp,
                               bias=neg_max[:, s % 2:s % 2 + 1], scale=MLA_SCALE,
                               accum_out=row_sum[:, s % 2:s % 2 + 1]).then_inc(mla_exp, 1)

            with act.Fori(0, MLA_HEADS) as h:
                u0 = U_MLA
                act.wait_ge(mla_q_proj, h + 1)
                act.copy(qn_hi[:, :], ps[:, 7, :]).then_inc(mla_qk_hi, 1)
                split_hi(u0 + 2, h, 4)
                act.copy(qrf[:, :], ps[0:64, 6, :]).then_inc(mla_qr_out, 1)
                act.wait_ge(mla_k_proj, h + 1)
                act.copy(kn_hi[:, :], two_banks(0)[:, 0:TOK]).then_inc(mla_qk_hi, 1)
                act.wait_ge(mla_q_mixed, h + 1)
                act.copy(qr_st[0:64, :], qrf[:, :]).then_inc(mla_qr_hi, 1)
                split_hi(u0 + 3, h, 4)
                act.copy(prob[:, 0, :], two_banks(2)[:, 0:TOK]).then_inc(mla_v_out, 1)
                act.wait_ge(mla_v_T, h + 1)
                act.copy(v_hi[:, :, :], two_banks(4)[:, 0:TOK].rearrange("p (k n) -> p k n", n=P)).then_inc(mla_v_hi, 1)
                mla_softmax(h, 0)
                for s in range(QB):
                    if s < QB - 1:
                        mla_softmax(h, s + 1)
                    if s % 2 == 1:
                        split_hi(u0 + 4 + s // 2, h, 4)
                    act.wait_ge(mla_pT, h * QB + (s + 1))
                    act.copy(pt_hi[:, :, s * P:s * P + P], two_banks(4)[:, 0:TOK].rearrange("p (k n) -> p k n", n=P)).then_inc(mla_pT_hi, 1)
                act.wait_ge(mla_gate_z, h + 1)
                act.activation(prob[:, 0, 0:SEQ], a_gate[:, :], ACT.Exp, scale=-1.0).then_inc(mla_gate_exp, 1)
                act.wait_ge(mla_free, h + 2)
                act.wait_ge(mla_spilled, (h + 1) * 16)
                act.copy(a_stage[:, 0, :], a_gate[:, :]).then_inc(mla_gated_hi, 1)

            act.wait_ge(mla_spilled, 9 * 16)
            def merge_round(r, last):
                for par in range(2):
                    u0 = U_MG + par * 6
                    for j, sg in enumerate((sg_a, sg_b)):
                        split_hi(u0 + 2 * j + 2, r, 12)
                        act.wait_ge(w_used, r * 12 + (u0 + 2 * j + 2))
                        if j == 0:
                            act.wait_ge(mg_free, r * 2 + (par + 2))
                        col = r * 4 + (B_MG + par * 2 + j)
                        act.activation(sg[:, :], ps[:, 4 * par + j, :], ACT.Exp, scale=-1.0,
                                       bias=nbias[:, (slice(col, col + 1) if last else bass.ds(col, 1))]).then_inc(mg_exp, 1)
                        split_hi(u0 + 2 * j + 3, r, 12)
                    if not (last and par == 1):
                        split_hi(u0 + 6, r, 12)
                        split_hi(u0 + 7, r, 12)

            act.wait_ge(nbias_made, 1)
            with act.Fori(0, KT // 2 - 1) as r:
                merge_round(r, False)
            merge_round(KT // 2 - 1, True)

            act.wait_ge(w_used, U_OUT)
            for k in range(KT):
                act.wait_ge(mg_free, k + 3)
                act.copy(m_hi[:, k, :], m_f[:, k, :]).then_inc(m_hi_done, 1)
            for c in range(4):
                act.wait_ge(ada_used, ADA_FIRST + 8 * c + 8)
                if c >= 2:
                    act.wait_ge(gate_bc_sum, c - 1)
                act.copy(gate_rows[:, c % 2, :], ps[0:2, c % 2, :]).then_inc(gate_row_ready, 1)

            split_hi(U_OUT, late=True)
            split_hi(U_OUT + 1, late=True)

            def out_chunk(r, par, last):
                for c in range(8):
                    if not (last and c >= 6):
                        split_hi(U_OUT + par * 8 + c + 2, r, 16, late=True)
                for t in range(QB):
                    n = (r * 2 + par) * QB + t
                    act.wait_ge(o_added, n + 1)
                    if n:
                        act.wait_ge(o_squared, n)
                    col = r * 8 + (par * 4 + t)
                    act.activation(y_sq[:, :], y[:, t, (2 * r + par) * 512:(2 * r + par) * 512 + 512], ACT.Square,
                                   accum_out=sumsq[:, (slice(col, col + 1) if isinstance(col, int) else bass.ds(col, 1))]).then_inc(o_squared, 1)

            out_chunk(0, 0, False)
            out_chunk(0, 1, False)
            out_chunk(1, 0, False)
            out_chunk(1, 1, True)
            act.wait_ge(o_ms, 1)
            act.activation(tok_ms, tok_ms, ACT.Sqrt, scale=1.0 / D, bias=eps_c).then_inc(o_root, 1)

        @block.vector
        def _(dve):
            tt, ts, stt = dve.tensor_tensor, dve.tensor_scalar, dve.scalar_tensor_tensor

            def f(ap):
                return ap.bitcast(F32)

            dve.memset(ones[:, :], 1.0).then_inc(ada_col_out, 2)
            dve.memset(eps_c, EPS).then_inc(const_made, 1)
            dve.memset(row_sum, 0.0).then_inc(ada_col_ready, 2)
            dve.memset(neg_max, 0.0).then_inc(swa_out_free, 1)
            dve.memset(neg_raw, 0.0).then_inc(swa_bank7_free, 1)
            dve.memset(row_inv, 0.0).then_inc(mla_free, 1)
            dve.memset(tok_ms, 0.0).then_inc(mg_free, 2)
            dve.memset(tok_inv, 0.0).then_inc(o_free, 2 * QB)
            dve.memset(sumsq, 0.0).then_inc(swa_spilled, 16)
            dve.memset(shift, 0.0).then_inc(mla_spilled, 16)
            dve.wait_ge(const_in, 12 * 16)
            ts(nbias, bias, -1.0, None, ALU.mult)
            ts(sink8, sink, 1.0 / SWA_SCALE, None, ALU.mult).then_inc(nbias_made, 1)
            dve.wait_ge(silu_exp, 1)
            ts(silu_e, silu_e, 1.0, None, ALU.add).then_inc(silu_step, 1)
            dve.wait_ge(silu_step, 1)
            dve.reciprocal(silu_e, silu_e).then_inc(silu_step, 1)
            dve.wait_ge(silu_step, 2)
            tt(silu_c, silu_e, cT, ALU.mult).then_inc(silu_ready, 1)

            dve.wait_ge(x_in, 4 * 16)
            tt(sq_sum[:, :], xT[:, 0, :], xT[:, 0, :], ALU.mult).then_inc(sq_added, 1)
            with dve.Fori(1, KT) as k:
                xk = xT[:, bass.ds(k, 1), :].rearrange("p a n -> p (a n)")
                dve.wait_ge(sq_added, k)
                tt(sq[:, :], xk, xk, ALU.mult).then_inc(sq_made, 1)
                dve.wait_ge(sq_made, k)
                tt(sq_sum[:, :], sq_sum[:, :], sq[:, :], ALU.add).then_inc(sq_added, 1)

            def ada_round(r):
                for half in range(2):
                    dve.wait_ge(ada_col_ready, r * 2 + (half + 3))
                    cols = bass.ds(r * 8 + half * 4, 4)
                    tt(mod[:, cols, :], ps[:, 2 + half, 0:8].rearrange("p (f v) -> p f v", v=2), b_ada[:, cols, :], ALU.add).then_inc(ada_col_out, 1)

            with dve.Fori(0, 2) as r:
                ada_round(r)
            dve.wait_ge(x_root, 1)
            dve.reciprocal(rstd[:, :], rstd[:, :]).then_inc(x_rstd, 1)
            dve.wait_ge(x_rstd, 1)
            with dve.Fori(0, KT) as k:
                xk = xT[:, bass.ds(k, 1), :].rearrange("p a n -> p (a n)")
                tt(xk, xk, rstd[:, :], ALU.mult).then_inc(x_normed, 1)
            with dve.Fori(2, 4) as r:
                ada_round(r)
            dve.wait_ge(ada_col_out, 10)
            stt(scale1, scale1, 1.0, norm_g, ALU.add, ALU.mult).then_inc(scale_made, 1)
            dve.wait_ge(scale_made, 1)
            dve.wait_ge(x_normed, KT)

            def h_make(k):
                for v, c in ((0, slice(0, SEQ)), (1, slice(SEQ, TOK))):
                    ins = ts(xT[:, k, c], xT[:, k, c], scale1[:, k, v:v + 1], shift[:, k, v:v + 1], ALU.mult, ALU.add)
                ins.then_inc(h_made, 1)

            h_make(0)
            for k in range(KT):
                if k < KT - 1:
                    h_make(k + 1)
                dve.wait_ge(h_hi_done, k + 1)
                tt(h_lo[:, k, :], xT[:, k, 0:SEQ], f(h_hi[:, k, :]), ALU.subtract)
                tt(hc_lo[:, k, :], xT[:, k, SEQ:TOK], f(hc_hi[:, k, :]), ALU.subtract).then_inc(h_ready, 1)

            for t in range(3):
                m = 64 if t == 0 else P
                dst = kraw[0:m, 0, 0:SEQ] if t == 0 else ks_f[:, t - 1, 0:SEQ]
                dve.wait_ge(k_rot_ready, t + 1)
                tt(krot[0:m, :], ps[0:m, 4, :], sin[0:m, :], ALU.mult).then_inc(k_step, 1)
                if t >= 1:
                    dve.tensor_copy(ks_f[:, t - 1, SEQ:TOK], kraw[:, t % 2, SEQ:TOK])
                tt(dst, kraw[0:m, t % 2, 0:SEQ], cos[0:m, :], ALU.mult).then_inc(k_step, 1)
                dve.wait_ge(k_step, 2 * t + 2)
                tt(dst, dst, krot[0:m, :], ALU.add).then_inc(k_roped, 1)
                if t == 0:
                    dve.wait_ge(kpe_hi_done, 1)
                    dve.wait_ge(k_roped, 1)
                    tt(kpe_lo[0:64, :], kraw[0:64, 0, :], f(kpe_hi[0:64, :]), ALU.subtract)
                    tt(kpe_lo[64:P, :], kraw[0:64, 0, :], f(kpe_hi[0:64, :]), ALU.subtract).then_inc(kpe_lo_done, 1)
            dve.wait_ge(z_bank_free, 3 * RT)
            for k in range(RT):
                if k:
                    dve.wait_ge(n_sum, 2 * k - 1)
                tt(nsq[:, 0, :], ckv[:, k, :], ckv[:, k, :], ALU.mult).then_inc(n_sq, 1)
                if k:
                    dve.wait_ge(n_sum, 2 * k)
                tt(nsq[:, 1, 0:SEQ], cq[:, k, :], cq[:, k, :], ALU.mult).then_inc(n_sq, 1)
            dve.wait_ge(n_root, 3)
            dve.reciprocal(nrstd[:, 0, :], nrstd[:, 0, :]).then_inc(n_rstd, 1)
            dve.reciprocal(nrstd[:, 1, 0:SEQ], nrstd[:, 1, 0:SEQ]).then_inc(n_rstd, 1)
            dve.wait_ge(n_rstd, 2)
            for k in range(RT):
                stt(ckv[:, k, :], ckv[:, k, :], kvn_g[:, k:k + 1], nrstd[:, 0, :], ALU.mult, ALU.mult).then_inc(n_scaled, 1)
                stt(cq[:, k, :], cq[:, k, :], qn_g[:, k:k + 1], nrstd[:, 1, 0:SEQ], ALU.mult, ALU.mult).then_inc(n_scaled, 1)

            def row_max(n, s, src, scores, max_done, negmax_done, scale):
                dve.wait_ge(scores, n)
                dve.tensor_reduce(neg_raw[:, s:s + 1], src, AX.X, ALU.max, negate=True).then_inc(max_done, 1)
                dve.wait_ge(max_done, n)
                ts(neg_max[:, s:s + 1], neg_raw[:, s:s + 1], scale, None, ALU.mult).then_inc(negmax_done, 1)

            def normalise(n, s, p, exp_done, inv_done, prob_done):
                dve.wait_ge(exp_done, n)
                dve.reciprocal(row_inv[:, s:s + 1], row_sum[:, s:s + 1]).then_inc(inv_done, 1)
                dve.wait_ge(inv_done, n)
                ts(p, p, row_inv[:, s:s + 1], None, ALU.mult).then_inc(prob_done, 1)

            def swa_unit(r, par, s):
                nb = len(key_blocks(s // GROUP))
                n = r * 32 + (par * 16 + s + 1)
                row_max(n, s % 2, two_banks(2 * (s % 2))[:, 768 - nb * P:769], swa_s, swa_max, swa_negmax, SWA_SCALE)
                normalise(n, s % 2, sprob[:, s % 2, 0:nb * P], swa_exp, swa_inv, swa_prob)

            def sigmoid_of(e, n, step):
                ts(e, e, 1.0, None, ALU.add).then_inc(step, 1)
                dve.wait_ge(step, n + 1)
                dve.reciprocal(e, e).then_inc(step, 1)
                dve.wait_ge(step, n + 2)

            with dve.Fori(0, 2) as r:
                for par in range(2):
                    g = r * 2 + par
                    u0 = U_SWA + par * 8
                    rows = slice(64 * par, 64 * par + 64)
                    kr = ks_f[rows, bass.ds(r, 1), :].rearrange("p a n -> p (a n)")
                    dve.wait_ge(swa_k_hi, g + 1)
                    tt(k_lo2[0:64, :], kr, f(k_hi2[rows, :]), ALU.subtract)
                    tt(k_lo2[64:P, :], kr, f(k_hi2[rows, :]), ALU.subtract).then_inc(swa_k_lo, 1)
                    dve.wait_ge(swa_v_hi, g + 1)
                    tt(v_st[:, :, 64:P], vT_of(r, par), f(v_st[:, :, 0:64]), ALU.subtract).then_inc(swa_v_lo, 1)
                    for j in range(2):
                        n = r * 4 + (par * 2 + j)
                        dve.wait_ge(swa_q_rotated, n + 1)
                        tt(qt[:, :], ps[:, 4 + j, :], sin[:, :], ALU.mult)
                        tt(qf2[:, j, :], qf2[:, j, :], cos[:, :], ALU.mult).then_inc(swa_q_step, 1)
                        dve.wait_ge(swa_q_step, n + 1)
                        tt(qf2[:, j, :], qf2[:, j, :], qt[:, :], ALU.add).then_inc(swa_q_mixed, 1)
                        dve.wait_ge(swa_q_hi, n + 1)
                        dve.wait_ge(swa_q_mixed, n + 1)
                        tt(q_st[64:P, 2 * j, :], qf2[0:64, j, :], f(q_st[0:64, 2 * j, :]), ALU.subtract)
                        tt(q_st[64:P, 2 * j + 1, :], qf2[64:P, j, :], f(q_hiT[64:P, :]), ALU.subtract).then_inc(swa_q_lo, 1)
                    swa_unit(r, par, 0)
                    for s in range(16):
                        b, n = s // GROUP, s % GROUP
                        nb = len(key_blocks(b))
                        if s < 15:
                            swa_unit(r, par, s + 1)
                        if s % 8 == 7:
                            j = s // 8
                            dve.wait_ge(w_used, r * 16 + (u0 + 6 + 2 * j))
                            ins = ts(s_gate[:, j, :], ps[:, 7, :], bias[:, bass.ds(r * 8 + (B_SWA + par * 4 + 2 + j), 1)], None, ALU.add)
                            ins.then_inc(swa_gate_z, 1)
                        dve.wait_ge(swa_pT_hi, r * 32 + (par * 16 + s + 1))
                        tt(spt_lo[:, 0:nb, n, :], two_banks(4)[:, 0:nb * P].rearrange("p (k n) -> p k n", n=P),
                           f(spt_hi[:, 0:nb, n, :]), ALU.subtract).then_inc(swa_pT_lo, 1)
                        if n == GROUP - 1:
                            dve.wait_ge(swa_out_low, r * 8 + (par * 4 + b + 1))
                            for odd in range(2):
                                ins = tt(b_T[64 * odd:64 * odd + 64, :, b * P:b * P + P],
                                         ps[0:64, 6, :].rearrange("p (j o n) -> p j o n", o=2, n=P)[:, :, odd, :],
                                         o_low[:, :].rearrange("p (j o n) -> p j o n", o=2, n=P)[:, :, odd, :], ALU.add)
                            ins.then_inc(swa_out_free, 1)
                    for j in range(2):
                        n = r * 4 + (par * 2 + j)
                        dve.wait_ge(swa_gate_exp, n + 1)
                        sigmoid_of(gate_e[:, j, :], n * 3, swa_gate_step)
                        tt(s_gate[:, j, :], s_gate[:, j, :], gate_e[:, j, :], ALU.mult).then_inc(swa_gate_step, 1)
                        dve.wait_ge(swa_gate_step, n * 3 + 3)
                        if j == 0:
                            dve.wait_ge(swa_out_free, r * 8 + (par * 4 + 5))
                        tt(b_T[:, j, :], b_T[:, j, :], s_gate[:, j, :], ALU.mult).then_inc(swa_gated, 1)
                    for j in range(2):
                        n = r * 4 + (par * 2 + j)
                        dve.wait_ge(swa_gated_hi, n + 1)
                        ins = tt(s_stage[:, 1, :], b_T[:, j, :], f(s_stage[:, 0, :]), ALU.subtract)
                        ins.then_inc(swa_gated_lo, 1)
                dve.memset(neg_raw, 0.0).then_inc(swa_bank7_free, 1)

            for k in range(RT):
                dve.wait_ge(n_hi, 2 * k + 2)
                tt(ckv_lo[:, k, :], ckv[:, k, :], f(ckv_hi[:, k, :]), ALU.subtract).then_inc(n_lo, 1)
                tt(cq_lo[:, k, :], cq[:, k, :], f(cq_hi[:, k, :]), ALU.subtract).then_inc(n_lo, 1)

            def mla_unit(h, s):
                n = h * QB + (s + 1)
                row_max(n, s % 2, two_banks(2 * (s % 2))[:, 0:TOK], mla_s, mla_max, mla_negmax, MLA_SCALE)
                normalise(n, s % 2, prob[:, s % 2, :], mla_exp, mla_inv, mla_prob)

            with dve.Fori(0, MLA_HEADS) as h:
                u0 = U_MLA
                dve.wait_ge(mla_qk_hi, h * 2 + 1)
                tt(qn_lo[:, :], ps[:, 7, :], f(qn_hi[:, :]), ALU.subtract).then_inc(mla_qk_lo, 1)
                dve.wait_ge(mla_q_rotated, h + 1)
                tt(a_gate[0:64, :], ps[0:64, 4, :], sin[0:64, :], ALU.mult)
                tt(qrf[:, :], qrf[:, :], cos[0:64, :], ALU.mult).then_inc(mla_q_step, 1)
                dve.wait_ge(mla_q_step, h + 1)
                tt(qrf[:, :], qrf[:, :], a_gate[0:64, :], ALU.add).then_inc(mla_q_mixed, 1)
                dve.wait_ge(mla_qk_hi, h * 2 + 2)
                tt(kn_lo[:, :], two_banks(0)[:, 0:TOK], f(kn_hi[:, :]), ALU.subtract).then_inc(mla_qk_lo, 1)
                dve.wait_ge(mla_qr_hi, h + 1)
                tt(qr_st[64:P, :], qrf[:, :], f(qr_st[0:64, :]), ALU.subtract).then_inc(mla_qr_lo, 1)
                dve.wait_ge(mla_v_hi, h + 1)
                tt(v_lo[:, :, :], two_banks(4)[:, 0:TOK].rearrange("p (k n) -> p k n", n=P), f(v_hi[:, :, :]), ALU.subtract).then_inc(mla_v_lo, 1)
                mla_unit(h, 0)
                for s in range(QB):
                    if s < QB - 1:
                        mla_unit(h, s + 1)
                    else:
                        dve.wait_ge(w_used, h * 4 + (u0 + 4))
                        ts(a_gate[:, :], ps[:, 7, :], bias[:, bass.ds(h + B_MLA, 1)], None, ALU.add).then_inc(mla_gate_z, 1)
                    dve.wait_ge(mla_pT_hi, h * QB + (s + 1))
                    tt(pt_lo[:, :, s * P:s * P + P], two_banks(4)[:, 0:TOK].rearrange("p (k n) -> p k n", n=P),
                       f(pt_hi[:, :, s * P:s * P + P]), ALU.subtract).then_inc(mla_pT_lo, 1)
                e = prob[:, 0, 0:SEQ]
                dve.wait_ge(mla_gate_exp, h + 1)
                sigmoid_of(e, h * 3, mla_gate_step)
                tt(a_gate[:, :], a_gate[:, :], e, ALU.mult).then_inc(mla_gate_step, 1)
                dve.wait_ge(mla_gate_step, h * 3 + 3)
                dve.wait_ge(mla_out, h + 1)
                tt(a_gate[:, :], ps[:, 6, :], a_gate[:, :], ALU.mult).then_inc(mla_free, 1)
                dve.wait_ge(mla_gated_hi, h + 1)
                tt(a_stage[:, 1, :], a_gate[:, :], f(a_stage[:, 0, :]), ALU.subtract).then_inc(mla_gated_lo, 1)
                dve.wait_ge(mla_gated_lo, h + 1)

            with dve.Fori(0, KT // 2) as r:
                for par in range(2):
                    for j, sg in enumerate((sg_a, sg_b)):
                        n = (r * 4 + (par * 2 + j)) * 3
                        dve.wait_ge(mg_exp, r * 4 + (par * 2 + j + 1))
                        sigmoid_of(sg[:, :], n, mg_step)
                        dve.wait_ge(w_used, r * 12 + (U_MG + par * 6 + 5 + j))
                        tt(sg[:, :], sg[:, :], ps[:, 4 * par + 2 + j, :], ALU.mult).then_inc(mg_step, 1)
                    dve.wait_ge(mg_step, (r * 4 + (par * 2 + 2)) * 3)
                    tt(m_f[:, bass.ds(r * 2 + par, 1), :].rearrange("p a n -> p (a n)"), sg_a[:, :], sg_b[:, :], ALU.add).then_inc(mg_free, 1)
            for k in range(KT):
                dve.wait_ge(m_hi_done, k + 1)
                tt(m_lo[:, k, :], m_f[:, k, :], f(m_hi[:, k, :]), ALU.subtract).then_inc(m_ready, 1)
            dve.wait_ge(late_in, 32)
            for c in range(4):
                dve.wait_ge(gate_bc_sum, c + 1)
                gc = gate_bc[:, c * 512:c * 512 + 512]
                tt(gc, gc, ps[:, 2 + c % 2, :], ALU.add).then_inc(gate_ready, 1)

            dve.wait_ge(y_in, 16)
            dve.wait_ge(gate_ready, 4)
            with dve.Fori(0, 2) as r:
                for par in range(2):
                    cc = bass.ds(r * 1024 + par * 512, 512)
                    dve.wait_ge(w_used, r * 16 + (U_OUT + par * 8 + 8))
                    for t in range(QB):
                        n = (r * 2 + par) * QB + (t + 1)
                        tt(y_add[:, t, :], ps[:, 4 * par + t, :], gate_bc[:, cc], ALU.mult).then_inc(o_free, 1)
                        dve.wait_ge(o_free, n + 2 * QB)
                        tt(y[:, t, cc], y[:, t, cc], y_add[:, t, :], ALU.add).then_inc(o_added, 1)
            dve.wait_ge(o_squared, 4 * QB)
            dve.tensor_reduce(tok_ms, sumsq.rearrange("p (n t) -> p t n", t=QB), AX.X, ALU.add).then_inc(o_ms, 1)
            dve.wait_ge(o_root, 1)
            dve.reciprocal(tok_inv, tok_ms).then_inc(o_inv, 1)
            dve.wait_ge(o_inv, 1)
            for t in range(QB):
                stt(y[:, t, :], y[:, t, :], tok_inv[:, t:t + 1], fin_g[:, :], ALU.mult, ALU.mult).then_inc(o_final, 1)


def rope_tables(np):
    n, grid_w = 16, 64
    inv = (np.float32(10000.0) ** (-np.arange(n, dtype=np.float32) / np.float32(n))).astype(np.float32)
    tok = np.arange(SEQ)
    pos = np.stack([tok // grid_w, tok % grid_w]).astype(np.float32)
    feat = np.arange(P) % 64
    ang = (pos[feat // 32] * inv[feat % 16][:, None]).astype(np.float32)
    rot = np.zeros((P, P), np.float32)
    for d in range(P):
        if d % 32 < 16:
            rot[d + 16, d] = -1.0
        else:
            rot[d - 16, d] = 1.0
    q, k = np.arange(P)[:, None], np.arange(P)[None, :]
    masks = np.zeros((P, 2, P), np.float32)
    masks[:, 0][k < q] = NEG
    masks[:, 1][k > q] = NEG
    return np.cos(ang).astype(np.float32), np.sin(ang).astype(np.float32), rot, np.eye(P, dtype=np.float32), masks


def kernel(**inputs):
    import numpy as np
    import concourse.bacc as bacc
    from concourse.bass_utils import run_bass_kernel_spmd as run

    a = {k: np.asarray(v) for k, v in inputs.items()}
    w_in, b_in = a["w_in"][0], a["b_in"][0]
    c_q, c_kv, k_pe, gate_a, q_s, k_s, v_s, gate_b, mg_a, mg_b = (
        0, 512, 1024, 1088, 2112, 3136, 3392, 3648, 4672, 6720)

    cols = []
    for i in range(RT):
        cols += [c_kv + P * i, c_q + P * i]
    cols += [k_pe, k_s, k_s + P, v_s, v_s + P]
    swa_cols = []
    for g in range(KV_GROUPS):
        swa_cols += [q_s + 256 * g, q_s + 256 * g + P, gate_b + 256 * g, gate_b + 256 * g + P]
    mla_cols = [gate_a + P * h for h in range(MLA_HEADS)]
    mg_cols = []
    for j in range(KT):
        mg_cols += [mg_a + P * j, mg_b + P * j]

    def tile_units(w, c):
        t = w[:, c:c + P].reshape(-1, 8, P, P)
        return [u.transpose(1, 0, 2).reshape(P, UNIT) for u in t]

    def rank_unit(w, cs):
        t = np.concatenate([w[:, c0:c1] for c0, c1 in cs], axis=1)
        return t.reshape(RT, P, 256).transpose(1, 0, 2).reshape(P, UNIT)

    units = []
    for c in cols + swa_cols:
        units += tile_units(w_in, c)
    w_uq, w_ukv = a["w_uq"][0], a["w_ukv"][0]
    for h in range(MLA_HEADS):
        q0, k0 = h * (NOPE + ROPE), h * 256
        units.append(rank_unit(w_uq, [(q0, q0 + 192), (q0, q0 + 64)]))
        units.append(rank_unit(w_ukv, [(k0, k0 + 256)]))
        units += tile_units(w_in, mla_cols[h])
    for j in range(KT):
        units += tile_units(w_in, mg_cols[2 * j]) + tile_units(w_in, mg_cols[2 * j + 1])
        units += tile_units(a["w_branch_a"][0], P * j) + tile_units(a["w_branch_b"][0], P * j)
    w_out = a["w_out"][0]
    for n in range(4):
        for c in range(8):
            t = w_out[256 * c:256 * c + 256, 512 * n:512 * n + 512]
            units.append(t.reshape(2, P, 512).transpose(1, 0, 2).reshape(P, UNIT))
    stream = np.stack(units)
    ada = a["w_ada"][0].reshape(8, 2, P, 12, 512).transpose(3, 0, 2, 1, 4).reshape(ADA_ALL, P, UNIT)

    def columns(v):
        return v.reshape(-1, P).T

    def twice(v):
        return np.stack([columns(v), columns(v)], axis=-1)

    b_cols = [b_in[c:c + P] for c in cols + swa_cols + mla_cols + mg_cols]
    cos, sin, rot, ident, masks = rope_tables(np)
    b_ada = a["b_ada"][0]
    data = {
        "xT": np.concatenate([a["x"][0].T.reshape(KT, P, SEQ), a["ctx"][0].T.reshape(KT, P, CTX)], axis=2).transpose(1, 0, 2),
        "x": a["x"][0],
        "cT": np.stack([columns(a["c"][0]), columns(a["c_ctx"])], axis=-1),
        "ada": ada,
        "b_adaT": twice(b_ada[0:2 * D]),
        "b_gate": np.broadcast_to(b_ada[2 * D:3 * D], (P, D)),
        "norm_gT": twice(a["norm_g"][0]),
        "stream": stream,
        "biasT": np.stack(b_cols, axis=1),
        "qn_gT": columns(a["q_norm_g"][0]),
        "kvn_gT": columns(a["kv_norm_g"][0]),
        "sink": a["sink"],
        "final_g": np.broadcast_to(a["final_g"], (P, D)),
        "cos": cos, "sin": sin, "rot": rot, "ident": ident, "masks": masks,
    }
    nc = bacc.Bacc("TRN2", target_bir_lowering=False, num_devices=1)
    arrays, args = {}, []
    for name, v in data.items():
        v = np.ascontiguousarray(v)
        arrays["in_" + name] = v
        args.append(nc.dram_tensor("in_" + name, v.shape, mybir.dt.from_np(v.dtype), kind="ExternalInput").ap())
    out = nc.dram_tensor("out", (SEQ, D), F32, kind="ExternalOutput").ap()
    build(nc, *args, out)
    r = run(nc, [arrays], core_ids=[0])
    return r.results[0]["out"].reshape(1, SEQ, D)
```

```python
import concourse.bass as bass
from concourse import mybir
from contextlib import ExitStack

F32 = mybir.dt.float32
F32R = mybir.dt.float32r
ALU = mybir.AluOpType
ACT = mybir.ActivationFunctionType
AX = mybir.AxisListType

P = 128
D = 2048
SEQ, CTX = 512, 256
TOK = SEQ + CTX
KT = D // P
EPS = 1e-6
NEG = -1e30
RANK = 512
RT = RANK // P
MLA_HEADS, NOPE, ROPE = 8, 128, 64
MLA_SCALE = float(NOPE + ROPE) ** -0.5
SWA_HEADS, KV_GROUPS, HD = 16, 4, 64
GROUP = SWA_HEADS // KV_GROUPS
SWA_SCALE = float(HD) ** -0.5
QB = SEQ // P
CB = CTX // P
UNIT = 1024

Z_TILES = 13
U_Z = 0
U_Q = U_Z + 2 * Z_TILES
U_SWA = U_Q + 4
U_MLA = U_SWA + KV_GROUPS * 8 - 4
U_MG = U_MLA + MLA_HEADS * 4
U_OUT = U_MG + KT * 6
U_END = U_OUT + 32
B_SWA, B_MLA, B_MG = 13, 13 + 16, 13 + 16 + 8
B_END = B_MG + 32
ADA_FIRST, ADA_ALL = 64, 96
RAWS, WS = 4, 2
ROTATE = (5, 9)
AHEAD = 5


def raw_count(u, gate_done):
    return u // RAWS + 1 + ADA_FIRST // RAWS + ((ADA_ALL - ADA_FIRST) // RAWS if gate_done else 0)


def build(nc, xT_d, x_d, cT_d, ada_d, b_adaT_d, b_gate_d, norm_gT_d, stream_d, biasT_d, qn_gT_d, kvn_gT_d,
          sink_d, final_g_d, cos_d, sin_d, rot_d, ident_d, masks_d, out_d):
    es = ExitStack()
    with es:
        base = (nc.sbuf_base + 63) // 64 * 64
        KB = 1024

        def at(name, off_kb, shape, dt=F32):
            return nc.alloc_sbuf_tensor_at(name, shape, dt, offset=base + int(off_kb * KB))

        def sem(name):
            return es.enter_context(nc.semaphore(name))

        h_hi = at("h_hi", 0, [P, KT, SEQ], F32R)
        h_lo = at("h_lo", 32, [P, KT, SEQ], F32R)
        m_hi = at("m_hi", 0, [P, KT, SEQ], F32R)
        m_lo = at("m_lo", 32, [P, KT, SEQ], F32R)
        raw = at("raw", 64, [P, RAWS, UNIT])
        w_hi = at("w_hi", 80, [P, WS, UNIT], F32R)
        w_lo = at("w_lo", 88, [P, WS, UNIT], F32R)
        cos = at("cos", 96, [P, SEQ])
        sin = at("sin", 98, [P, SEQ])
        ident = at("ident", 100, [P, P])
        ident_r = at("ident_r", 100.5, [P, P], F32R)
        rot = at("rot", 101, [P, P])
        masks_r = at("masks_r", 101.5, [P, 2, P], F32R)
        ones = at("ones", 102.5, [P, P])
        small = at("small", 103, [P, 512])
        D0 = 105
        bias = small[:, 0:B_END]
        nbias = small[:, 72:72 + B_END]
        cT = small[:, 144:176].rearrange("p (k v) -> p k v", v=2)
        silu_c = small[:, 176:208].rearrange("p (k v) -> p k v", v=2)
        norm_g = small[:, 208:240].rearrange("p (k v) -> p k v", v=2)
        shift = small[:, 240:272].rearrange("p (k v) -> p k v", v=2)
        scale1 = small[:, 272:304].rearrange("p (k v) -> p k v", v=2)
        mod = small[:, 240:304].rearrange("p (k v) -> p k v", v=2)
        b_ada = small[:, 304:368].rearrange("p (k v) -> p k v", v=2)
        qn_g = small[:, 368:368 + RT]
        kvn_g = small[:, 372:372 + RT]
        eps_c = small[:, 376:377]
        neg_max = small[:, 378:380]
        row_sum = small[:, 380:382]
        row_inv = small[:, 382:384]
        sink = small[0:1, 384:400]
        sink8 = small[0:1, 460:476]
        sumsq = small[:, 400:416]
        tok_ms = small[:, 416:420]
        tok_inv = small[:, 456:460]
        neg_raw = small[:, 420:422]
        silu_e = small[:, 424:456].rearrange("p (k v) -> p k v", v=2)

        xT = at("xT", D0 + 22, [P, KT, TOK])
        hc_hi = at("hc_hi", D0 + 70, [P, KT, CTX], F32R)
        hc_lo = at("hc_lo", D0 + 86, [P, KT, CTX], F32R)
        sq = at("sq", D0 + 0, [P, TOK])
        sq_sum = at("sq_sum", D0 + 3, [P, TOK])
        rstd = at("rstd", D0 + 6, [P, TOK])
        ada_rows = at("ada_rows", D0 + 9, [2, 2, 512])
        masks_f = at("masks_f", D0 + 13, [P, 2, P])
        ckv = at("ckv", D0 + 0, [P, RT, TOK])
        cq = at("cq", D0 + 12, [P, RT, SEQ])
        kpe_hi = at("kpe_hi", D0 + 20, [P, TOK], F32R)
        kpe_lo = at("kpe_lo", D0 + 23, [P, TOK], F32R)
        ks_f = at("ks_f", D0 + 26, [P, 2, TOK])
        vT_f = at("vT_f", D0 + 32, [P, 2, TOK])
        kraw = at("kraw", D0 + 38, [P, 2, TOK])
        krot = at("krot", D0 + 44, [P, SEQ])
        nsq_kv = at("nsq_kv", D0 + 46, [P, RT, TOK])
        nsq_q = at("nsq_q", D0 + 58, [P, RT, SEQ])
        nrstd = at("nrstd", D0 + 46, [P, 2, TOK])
        q_st = at("q_st", D0 + 38, [P, GROUP, SEQ], F32R)
        k_hi2 = at("k_hi2", D0 + 46, [P, TOK], F32R)
        k_lo2 = at("k_lo2", D0 + 49, [P, TOK], F32R)
        v_st = at("v_st", D0 + 52, [P, QB + CB, P], F32R)
        spt_hi = at("spt_hi", D0 + 55, [P, 5, GROUP, P], F32R)
        spt_lo = at("spt_lo", D0 + 65, [P, 5, GROUP, P], F32R)
        sprob = at("sprob", D0 + 75, [P, 2, 5 * P + 1])
        q_hiT = at("q_hiT", D0 + 80.25, [P, SEQ], F32R)
        s_gate = at("s_gate", D0 + 82.25, [P, 2, SEQ])
        b_T = at("b_T", D0 + 86.25, [P, 2, SEQ])
        s_stage = at("s_stage", D0 + 90.25, [P, 2, SEQ], F32R)
        qf2 = at("qf2", D0 + 94.25, [P, 2, SEQ])
        gate_e = at("gate_e", D0 + 80.25, [P, SEQ])
        qt = at("qt", D0 + 98.25, [P, SEQ])
        o_low = at("o_low", D0 + 100.25, [64, SEQ])
        qn_hi = at("qn_hi", D0 + 0, [P, SEQ], F32R)
        qn_lo = at("qn_lo", D0 + 2, [P, SEQ], F32R)
        qr_st = at("qr_st", D0 + 4, [P, SEQ], F32R)
        kn_hi = at("kn_hi", D0 + 6, [P, TOK], F32R)
        kn_lo = at("kn_lo", D0 + 9, [P, TOK], F32R)
        v_hi = at("v_hi", D0 + 12, [P, QB + CB, P], F32R)
        v_lo = at("v_lo", D0 + 15, [P, QB + CB, P], F32R)
        qrf = at("qrf", D0 + 18, [64, SEQ])
        ckv_hi = at("ckv_hi", D0 + 26, [P, RT, TOK], F32R)
        ckv_lo = at("ckv_lo", D0 + 38, [P, RT, TOK], F32R)
        cq_hi = at("cq_hi", D0 + 50, [P, RT, SEQ], F32R)
        cq_lo = at("cq_lo", D0 + 58, [P, RT, SEQ], F32R)
        pt_hi = at("pt_hi", D0 + 66, [P, QB + CB, SEQ], F32R)
        pt_lo = at("pt_lo", D0 + 78, [P, QB + CB, SEQ], F32R)
        prob = at("prob", D0 + 96, [P, 2, TOK])
        a_gate = at("a_gate", D0 + 90, [P, SEQ])
        a_stage = at("a_stage", D0 + 92, [P, 2, SEQ], F32R)
        A = at("A", D0 + 0, [P, 2, 8, SEQ], F32R)
        B = at("B", D0 + 32, [P, 2, 8, SEQ], F32R)
        m_f = at("m_f", D0 + 64, [P, KT, SEQ])
        sg_a = at("sg_a", D0 + 96, [P, SEQ])
        sg_b = at("sg_b", D0 + 98, [P, SEQ])
        y = at("y", D0 + 0, [P, QB, D])
        gate_bc = at("gate_bc", D0 + 32, [P, D])
        fin_g = at("fin_g", D0 + 40, [P, D])
        gate_rows = at("gate_rows", D0 + 48, [2, 2, 512])
        y_add = at("y_add", D0 + 52, [P, QB, 512])
        y_sq = at("y_sq", D0 + 60, [P, 512])

        spill_a = nc.dram_tensor("spill_a", [8, P, 2, SEQ], F32, kind="Internal").ap()
        spill_b = nc.dram_tensor("spill_b", [8, P, 2, SEQ], F32, kind="Internal").ap()

        ps = es.enter_context(nc.psum_tensor("ps", [P, 8, 512], F32))

        def two_banks(b):
            return ps[:, b:b + 2, :].rearrange("p b n -> p (b n)")

        def sems(names):
            return [sem(n) for n in names.split()]

        raw_full = [sem(f"raw_full{s}") for s in range(RAWS)]
        w_hi_done, w_lo_done, w_used = sems("w_hi_done w_lo_done w_used")
        const_in, x_in, late_in, y_in, a_in, b_in = sems("const_in x_in late_in y_in a_in b_in")
        const_made, const_r, nbias_made, silu_exp, silu_step, silu_ready = sems("const_made const_r nbias_made silu_exp silu_step silu_ready")
        ada_used, ada_row_ready, ada_col_ready, ada_col_out, scale_made = sems("ada_used ada_row_ready ada_col_ready ada_col_out scale_made")
        sq_made, sq_added, x_sum, x_root, x_rstd, x_normed = sems("sq_made sq_added x_sum x_root x_rstd x_normed")
        h_made, h_hi_done, h_ready = sems("h_made h_hi_done h_ready")
        z_bank_free, z_lat_out, z_rest_out, k_rot_ready, k_step, k_roped = sems("z_bank_free z_lat_out z_rest_out k_rot_ready k_step k_roped")
        kpe_hi_done, kpe_lo_done, v_T_ready, v_T_out = sems("kpe_hi_done kpe_lo_done v_T_ready v_T_out")
        n_sq, n_sum, n_root, n_rstd, n_scaled, n_hi, n_lo = sems("rank_squared rank_summed rank_root rank_rstd rank_scaled rank_hi rank_lo")
        swa_q_out, swa_q_rotated, swa_q_step, swa_q_mixed, swa_q_hi, swa_q_lo = sems("swa_q_out swa_q_rotated swa_q_step swa_q_mixed swa_q_hi swa_q_lo")
        swa_k_hi, swa_k_lo, swa_v_hi, swa_v_lo = sems("swa_k_hi swa_k_lo swa_v_hi swa_v_lo")
        swa_s, swa_max, swa_negmax, swa_exp, swa_inv, swa_prob = sems("swa_scores swa_max swa_negmax swa_exp swa_inv swa_prob")
        swa_pT, swa_pT_hi, swa_pT_lo, swa_out, swa_out_low, swa_out_free = sems("swa_probT swa_probT_hi swa_probT_lo swa_out swa_out_low swa_out_free")
        swa_gate_z, swa_gate_exp, swa_gate_step, swa_gated, swa_gated_hi, swa_gated_lo, swa_spilled = sems(
            "swa_gate_z swa_gate_exp swa_gate_step swa_gated swa_gated_hi swa_gated_lo swa_spilled")
        mla_v_proj, mla_qr_proj = sem("mla_v_proj"), sem("mla_qr_proj")
        mla_qk_hi, mla_qk_lo, mla_qr_out, mla_q_rotated, mla_q_step, mla_q_mixed, mla_qr_hi, mla_qr_lo = sems(
            "mla_qk_hi mla_qk_lo mla_qr_out mla_q_rotated mla_q_step mla_q_mixed mla_qr_hi mla_qr_lo")
        mla_v_out, mla_v_T, mla_v_hi, mla_v_lo = sems("mla_v_out mla_v_T mla_v_hi mla_v_lo")
        mla_s, mla_max, mla_negmax, mla_exp, mla_inv, mla_prob = sems("mla_scores mla_max mla_negmax mla_exp mla_inv mla_prob")
        mla_pT, mla_pT_hi, mla_pT_lo, mla_out = sems("mla_probT mla_probT_hi mla_probT_lo mla_out")
        mla_gate_z, mla_gate_exp, mla_gate_step, mla_free, mla_gated_hi, mla_gated_lo, mla_spilled = sems(
            "mla_gate_z mla_gate_exp mla_gate_step mla_free mla_gated_hi mla_gated_lo mla_spilled")
        mg_exp, mg_step, mg_free = sems("merge_exp merge_step merge_free")
        m_hi_done, m_ready, gate_row_ready, gate_bc_sum, gate_ready = sems("m_hi_done m_ready gate_row_ready gate_bc_sum gate_ready")
        o_free, o_added, o_squared, o_ms, o_root, o_inv, o_final, stored = sems("out_free out_added out_squared out_ms out_root out_inv out_final stored")


        def vT_of(g):
            return vT_f[:, g // 2, :].rearrange("p (k n) -> p k n", n=P)[:, :, 64 * (g % 2):64 * (g % 2) + 64]

        def key_blocks(b):
            return list(range(max(b - 1, 0), min(b + 1, QB - 1) + 1)) + list(range(QB, QB + CB))

        block = es.enter_context(nc.Block())

        @block.sync
        def _(sp):
            consts = [(cT, cT_d), (b_ada, b_adaT_d), (norm_g, norm_gT_d), (bias, biasT_d), (qn_g, qn_gT_d),
                      (kvn_g, kvn_gT_d), (sink, sink_d), (ident[:, :], ident_d), (rot[:, :], rot_d),
                      (masks_f[:, :, :], masks_d), (cos[:, :], cos_d), (sin[:, :], sin_d)]
            for dst, src in consts:
                sp.dma_start(dst, src).then_inc(const_in, 16)
            for a in range(RAWS):
                sp.dma_start(raw[:, a, :], ada_d[a]).then_inc(raw_full[a], 16)
            for part in range(4):
                sp.dma_start(xT[:, 4 * part:4 * part + 4, :], xT_d[:, 4 * part:4 * part + 4, :]).then_inc(x_in, 16)
            with sp.Fori(1, ADA_FIRST // RAWS) as r:
                for s in range(RAWS):
                    sp.wait_ge(ada_used, r * RAWS + (s - RAWS + 1))
                    sp.dma_start(raw[:, s, :], ada_d[bass.ds(r * RAWS + s, 1)].rearrange("u p n -> (u p) n")).then_inc(raw_full[s], 16)
            for u in range(RAWS):
                sp.wait_ge(ada_used, ADA_FIRST - RAWS + 1 + u)
                sp.dma_start(raw[:, u, :], stream_d[u]).then_inc(raw_full[u], 16)

            def load(u, s):
                sp.wait_ge(w_lo_done, u - (RAWS - 1))
                sp.dma_start(raw[:, s, :], (stream_d[u] if isinstance(u, int) else stream_d[bass.ds(u, 1)].rearrange("u p n -> (u p) n"))).then_inc(raw_full[s], 16)

            def spill(dst, stage, hi_done, lo_done, n, spilled):
                sp.wait_ge(hi_done, n)
                sp.wait_ge(lo_done, n)
                sp.dma_start(dst.rearrange("t p v n -> (t p) v n"), stage.bitcast(F32)).then_inc(spilled, 16)

            n_loop = (U_SWA + AHEAD) // RAWS
            with sp.Fori(1, n_loop) as r:
                for s in range(RAWS):
                    load(r * RAWS + s, s)
            for u in range(n_loop * RAWS, U_SWA + AHEAD):
                load(u, u % RAWS)
            for g in range(KV_GROUPS):
                for u in range(U_SWA + 8 * g + AHEAD, min(U_SWA + 8 * g + 8, U_MLA) + AHEAD):
                    load(u, u % RAWS)
                for j in range(2):
                    spill(spill_b[2 * g + j:2 * g + j + 1], s_stage[:, :, :], swa_gated_hi, swa_gated_lo, 2 * g + j + 1, swa_spilled)
            with sp.Fori(0, MLA_HEADS) as h:
                for c in range(4):
                    load(U_MLA + AHEAD + c + h * 4, (U_MLA + AHEAD + c) % RAWS)
                spill(spill_a[bass.ds(h, 1)], a_stage[:, :, :], mla_gated_hi, mla_gated_lo, h + 1, mla_spilled)
            sp.wait_ge(swa_spilled, 9 * 16)
            sp.wait_ge(mla_out, MLA_HEADS)
            for v in range(2):
                sp.dma_start(B[:, v, :, :].bitcast(F32), spill_b[:, :, v, :].rearrange("t p n -> p t n")).then_inc(b_in, 16)
            sp.wait_ge(mla_spilled, 9 * 16)
            for v in range(2):
                sp.dma_start(A[:, v, :, :].bitcast(F32), spill_a[:, :, v, :].rearrange("t p n -> p t n")).then_inc(a_in, 16)
            n_loop = (U_OUT - U_MG - AHEAD) // RAWS
            with sp.Fori(0, n_loop) as r:
                for c in range(RAWS):
                    load(U_MG + AHEAD + c + r * RAWS, (U_MG + AHEAD + c) % RAWS)
            for u in range(U_MG + AHEAD + n_loop * RAWS, U_OUT):
                load(u, u % RAWS)
            sp.wait_ge(w_used, U_OUT)
            sp.wait_ge(mg_free, KT + 2)
            sp.dma_start(y[:, :, :], x_d.rearrange("(t p) d -> p t d", p=P)).then_inc(y_in, 16)
            sp.dma_start(gate_bc[:, :], b_gate_d).then_inc(late_in, 16)
            sp.dma_start(fin_g[:, :], final_g_d).then_inc(late_in, 16)
            for a in range(ADA_FIRST, ADA_FIRST + RAWS):
                sp.wait_ge(w_lo_done, U_OUT)
                sp.dma_start(raw[:, a % RAWS, :], ada_d[a]).then_inc(raw_full[a % RAWS], 16)
            with sp.Fori(ADA_FIRST // RAWS + 1, ADA_ALL // RAWS) as r:
                for s in range(RAWS):
                    sp.wait_ge(ada_used, r * RAWS + (s - RAWS + 1))
                    sp.dma_start(raw[:, s, :], ada_d[bass.ds(r * RAWS + s, 1)].rearrange("u p n -> (u p) n")).then_inc(raw_full[s], 16)
            sp.wait_ge(ada_used, ADA_ALL)
            for u in range(U_OUT, U_OUT + RAWS):
                sp.dma_start(raw[:, u % RAWS, :], stream_d[u]).then_inc(raw_full[u % RAWS], 16)
            with sp.Fori(0, (U_END - U_OUT - RAWS) // RAWS) as r:
                for c in range(RAWS):
                    load(U_OUT + RAWS + r * RAWS + c, (U_OUT + c) % RAWS)
            for t in range(QB):
                sp.wait_ge(o_final, t + 1)
                sp.dma_start(out_d[t * P:(t + 1) * P, :], y[:, t, :]).then_inc(stored, 16)
            sp.wait_ge(stored, QB * 16)

        @block.gpsimd
        def _(g):
            def split_lo(u, s, w):
                g.wait_ge(w_hi_done, u + 1)
                g.tensor_tensor(w_lo[:, w, :], raw[:, s, :], w_hi[:, w, :].bitcast(F32), ALU.subtract).then_inc(w_lo_done, 1)

            with g.Fori(0, U_END // RAWS) as r:
                for s in range(RAWS):
                    split_lo(r * RAWS + s, s, s % WS)
            for u in range(U_END // RAWS * RAWS, U_END):
                split_lo(u, u % RAWS, u % WS)

        @block.tensor
        def _(pe):
            mm = nc.tensor.matmul
            PASS = ((w_hi, 0), (w_hi, 1), (w_lo, 0))

            def ada_unit(a, s, bank, first, last):
                for half in range(2):
                    ins = mm(ps[0:2, bank, :], silu_c[:, 2 * a + half, :], raw[:, s, half * 512:half * 512 + 512],
                             start=first and half == 0, stop=last and half == 1)
                ins.then_inc(ada_used, 1)

            def columns(n_done, slot, bank):
                pe.wait_ge(ada_row_ready, n_done)
                for f in range(4):
                    ins = mm(ps[:, bank, 2 * f:2 * f + 2], ada_rows[0:2, slot, f * P:f * P + P], ident[0:2, 0:2],
                             start=True, stop=True)
                ins.then_inc(ada_col_ready, 1)

            pe.wait_ge(const_in, 12 * 16)
            pe.wait_ge(const_made, 1)
            pe.wait_ge(const_r, 2)
            pe.wait_ge(nbias_made, 1)
            pe.wait_ge(silu_ready, 1)
            def ada_round(r):
                for half in range(2):
                    for a in range(8):
                        pe.wait_ge(raw_full[a % RAWS], (r * 4 + (half * 2 + a // 4 + 1)) * 16)
                        ada_unit(a, a % RAWS, half, a == 0, a == 7)
                for half in range(2):
                    pe.wait_ge(ada_col_out, r * 2 + (half + 1))
                    columns(r * 2 + (half + 1), half, 2 + half)
            with pe.Fori(0, 2) as r:
                ada_round(r)
            pe.wait_ge(sq_added, KT)
            mm(ps[:, 4, :], ones[:, :], sq_sum[:, 0:SEQ], start=True, stop=True)
            mm(ps[:, 5, 0:CTX], ones[:, :], sq_sum[:, SEQ:TOK], start=True, stop=True).then_inc(x_sum, 1)
            with pe.Fori(2, 4) as r:
                ada_round(r)

            def proj(w, kts, lat, ctx, k0=0, last_k=KT):
                for k in kts:
                    kk = k - k0
                    for n, (wt, lo) in enumerate(PASS):
                        wk = wt[:, w, kk * P:kk * P + P]
                        st, sp_ = k == 0 and n == 0, k == last_k - 1 and n == 2
                        ins = mm(lat, wk, (h_lo if lo else h_hi)[:, k, :], start=st, stop=sp_)
                        if ctx is not None:
                            ins = mm(ctx, wk, (hc_lo if lo else hc_hi)[:, k, :], start=st, stop=sp_)
                return ins

            def proj_tile(u, par, lat, ctx, first=False):
                for half in range(2):
                    pe.wait_ge(w_lo_done, u + half + 1)
                    if first:
                        for k in range(half * 8, half * 8 + 8):
                            pe.wait_ge(h_ready, k + 1)
                            ins = proj((par + half) % WS, [k], lat, ctx, half * 8)
                    else:
                        ins = proj((par + half) % WS, range(half * 8, half * 8 + 8), lat, ctx, half * 8)
                    ins.then_inc(w_used, 1)

            proj_tile(0, 0, ps[:, 0, :], ps[:, 2, 0:CTX], first=True)
            proj_tile(2, 0, ps[:, 1, :], None)
            with pe.Fori(1, RT) as r:
                pe.wait_ge(z_bank_free, r * 3 - 1)
                proj_tile(r * 4, 0, ps[:, 0, :], ps[:, 2, 0:CTX])
                pe.wait_ge(z_bank_free, r * 3)
                proj_tile(r * 4 + 2, 0, ps[:, 1, :], None)
            pe.wait_ge(z_bank_free, 3 * RT)
            def after_tile(t):
                pe.wait_ge(z_rest_out, t + 1)
                if t < 3:
                    m = 64 if t == 0 else P
                    if t >= 1:
                        pe.wait_ge(k_roped, t)
                    mm(ps[:, 4, :], rot[0:m, :], kraw[0:m, t % 2, 0:SEQ], start=True, stop=True).then_inc(k_rot_ready, 1)
                else:
                    if t == 4:
                        pe.wait_ge(v_T_out, 1)
                    for k in range(QB + CB):
                        ins = nc.tensor.transpose(two_banks(5)[:, k * P:k * P + P], kraw[:, t % 2, k * P:k * P + P], ident[:, :])
                    ins.then_inc(v_T_ready, 1)

            for t in range(5):
                b = t % 2
                if t >= 2:
                    pe.wait_ge(z_rest_out, t - 1)
                proj_tile(16 + 2 * t, 0, ps[:, b, :], ps[:, 2 + b, 0:CTX])
                if t == 3:
                    pe.wait_ge(n_sq, 2 * RT)
                    for k in range(RT):
                        st, sp_ = k == 0, k == RT - 1
                        mm(ps[:, 5, :], ones[:, :], nsq_kv[:, k, 0:SEQ], start=st, stop=sp_)
                        mm(ps[:, 6, 0:CTX], ones[:, :], nsq_kv[:, k, SEQ:TOK], start=st, stop=sp_)
                        ins = mm(ps[:, 7, :], ones[:, :], nsq_q[:, k, :], start=st, stop=sp_)
                    ins.then_inc(n_sum, 1)
                if t == 4:
                    pe.wait_ge(n_root, 3)
                if t >= 1:
                    after_tile(t - 1)
            proj_tile(U_Q, 0, ps[:, 7, :], None)
            after_tile(4)
            pe.wait_ge(v_T_out, 2)
            pe.wait_ge(k_roped, 3)
            proj_tile(U_Q + 2, 0, ps[:, 4, :], None)
            for j in range(2):
                pe.wait_ge(swa_q_out, j + 1)
                mm(ps[:, 5 + j, :], rot[:, :], qf2[:, j, :], start=True, stop=True).then_inc(swa_q_rotated, 1)

            def swa_scores(g, s):
                b, n = s // GROUP, s % GROUP
                sb = two_banks(2 * (s % 2))
                lo, hi = max(b - 1, 0), min(b + 1, QB - 1)
                wn = (hi - lo + 1) * P
                if s >= 2:
                    pe.wait_ge(swa_exp, g * 16 + s - 1)
                elif s == 0:
                    pe.wait_ge(swa_q_lo, g * 2 + 2)
                    pe.wait_ge(swa_k_lo, g + 1)
                q = q_st[:, n, b * P:b * P + P]
                mm(sb[:, 512 - wn:512], q, k_hi2[:, lo * P:hi * P + P], start=True, stop=False)
                mm(sb[:, 512 - wn:512], q, k_lo2[:, lo * P:hi * P + P], start=False, stop=False)
                if b > 0:
                    mm(sb[:, 512 - wn:512 - wn + P], ident_r[:, :], masks_r[:, 0, :], start=False, stop=b == QB - 1)
                if b < QB - 1:
                    mm(sb[:, 384:512], ident_r[:, :], masks_r[:, 1, :], start=False, stop=True)
                mm(sb[:, 512:768], q, k_hi2[:, SEQ:TOK], start=True, stop=False)
                mm(sb[:, 512:768], q, k_lo2[:, SEQ:TOK], start=False, stop=True)
                head = GROUP * g + n
                mm(sb[:, 768:769], ones[0:1, :], sink8[0:1, head:head + 1], start=True, stop=True).then_inc(swa_s, 1)

            def swa_filler(g, s):
                shares = 2 if g < KV_GROUPS - 1 else 4
                f, part = s // shares, s % shares
                u = U_SWA + 8 * g + f
                if part == 0:
                    pe.wait_ge(w_lo_done, u + 1)
                    if f in (2, 4) and g < KV_GROUPS - 1:
                        pe.wait_ge(swa_q_out, 2 * (g + 1) + f // 2)
                    elif f % 2 == 0 and g + f:
                        pe.wait_ge(swa_gate_z, 2 * g + (1 if f else 0))
                    elif f == 0:
                        pe.wait_ge(swa_q_out, 1)
                ks = range((f % 2) * 8 + part * (8 // shares), (f % 2) * 8 + (part + 1) * (8 // shares))
                ins = proj(u % WS, ks, ps[:, 7, :], None, (f % 2) * 8)
                if part == shares - 1:
                    ins.then_inc(w_used, 1)

            def swa_transpose(g, s):
                tb = two_banks(4)
                pe.wait_ge(swa_prob, g * 16 + s + 1)
                if g * 16 + s >= 1:
                    pe.wait_ge(swa_pT_lo, g * 16 + s)
                for k in range(len(key_blocks(s // GROUP))):
                    ins = nc.tensor.transpose(tb[:, k * P:k * P + P], sprob[:, s % 2, k * P:k * P + P], ident[:, :])
                ins.then_inc(swa_pT, 1)

            def swa_values(g, b):
                blocks = key_blocks(b)
                pe.wait_ge(swa_v_lo, g + 1)
                pe.wait_ge(swa_out_free, g * 4 + b + 1)
                for half, pt in enumerate((spt_hi, spt_lo)):
                    pe.wait_ge((swa_pT_hi, swa_pT_lo)[half], g * 16 + 4 * b + 4)
                    for k, kb in enumerate(blocks):
                        ins = mm(ps[:, 6, :], v_st[:, kb, :], pt[:, k, :, :].rearrange("p g n -> p (g n)"),
                                 start=half == 0 and k == 0, stop=half == 1 and k == len(blocks) - 1)
                ins.then_inc(swa_out, 1)

            swa_scores(0, 0)
            for g in range(KV_GROUPS):
                last = g == KV_GROUPS - 1
                for s in range(16):
                    if s < 15:
                        swa_scores(g, s + 1)
                    swa_filler(g, s)
                    if s in ROTATE and not last:
                        j = ROTATE.index(s)
                        pe.wait_ge(swa_q_out, 2 * g + 2 + j + 1)
                        pe.wait_ge(swa_out_free, g * 4 + s // 4 + 1)
                        mm(ps[:, 6, :], rot[:, :], qf2[:, j, :], start=True, stop=True).then_inc(swa_q_rotated, 1)
                    swa_transpose(g, s)
                    if s == 15 and not last:
                        swa_scores(g + 1, 0)
                    if s % GROUP == GROUP - 1:
                        if s // GROUP in (1, 2) and not last:
                            pe.wait_ge(swa_q_mixed, 2 * g + 2 + s // GROUP)
                        swa_values(g, s // GROUP)

            def mla_proj(u, w, passes):
                for out, c0, mhi, mlo in passes:
                    for k in range(RT):
                        for n, (wt, lo) in enumerate(PASS):
                            ins = mm(out, wt[:, w, k * 256 + c0:k * 256 + c0 + P], (mlo if lo else mhi)(k),
                                     start=k == 0 and n == 0, stop=k == RT - 1 and n == 2)
                return ins

            def mla_scores(h, s):
                sb = two_banks(2 * (s % 2))
                if s >= 2:
                    pe.wait_ge(mla_exp, h * QB + (s - 1))
                q = slice(s * P, s * P + P)
                parts = ((qn_hi, kn_hi), (qn_lo, kn_hi), (qn_hi, kn_lo), (qr_st, kpe_hi), (qr_st, kpe_lo))
                for c0, c1 in ((0, SEQ), (SEQ, TOK)):
                    for n, (qq, kk) in enumerate(parts):
                        ins = mm(sb[:, c0:c1], qq[:, q], kk[:, c0:c1], start=n == 0, stop=n == len(parts) - 1)
                ins.then_inc(mla_s, 1)

            def mla_transpose(h, s):
                tb = two_banks(4)
                pe.wait_ge(mla_prob, h * QB + (s + 1))
                if s >= 1:
                    pe.wait_ge(mla_pT_lo, h * QB + s)
                for k in range(QB + CB):
                    ins = nc.tensor.transpose(tb[:, k * P:k * P + P], prob[:, s % 2, k * P:k * P + P], ident[:, :])
                ins.then_inc(mla_pT, 1)

            lat, cx = slice(0, SEQ), slice(SEQ, TOK)
            pe.wait_ge(n_lo, 2 * RT)
            pe.wait_ge(swa_out_free, 17)
            pe.wait_ge(swa_gate_z, 8)
            with pe.Fori(0, MLA_HEADS) as h:
                u0 = U_MLA

                def kv_proj(c0, b):
                    return mla_proj(0, 0, [
                        (ps[:, b, :], c0, lambda k: ckv_hi[:, k, lat], lambda k: ckv_lo[:, k, lat]),
                        (ps[:, b + 1, 0:CTX], c0, lambda k: ckv_hi[:, k, cx], lambda k: ckv_lo[:, k, cx])])

                def q_proj(c0, b):
                    return mla_proj(0, 1, [(ps[:, b, :], c0, lambda k: cq_hi[:, k, :], lambda k: cq_lo[:, k, :])])

                def filler(part):
                    if part % 2 == 0:
                        pe.wait_ge(w_lo_done, h * 4 + (u0 + 3 + part // 2))
                    ins = proj(part // 2, range(4 * part, 4 * part + 4), ps[:, 7, :], None, (part // 2) * 8)
                    if part % 2 == 1:
                        ins.then_inc(w_used, 1)

                def values(half):
                    cols = slice(half * 256, half * 256 + 256)
                    for p, (vv, pt) in enumerate(((v_hi, pt_hi), (v_lo, pt_hi), (v_hi, pt_lo))):
                        if p != 1:
                            pe.wait_ge(mla_pT_lo if p else mla_pT_hi, h * QB + (2 * half + 2))
                        for k in range(QB + CB):
                            ins = mm(ps[:, 6, cols], vv[:, k, :], pt[:, k, cols], start=p == 0 and k == 0,
                                     stop=p == 2 and k == QB + CB - 1)
                    return ins

                pe.wait_ge(w_lo_done, h * 4 + (u0 + 1))
                kv_proj(P, 2).then_inc(mla_v_proj, 1)
                kv_proj(0, 0).then_inc(w_used, 1)
                pe.wait_ge(mla_v_out, h + 1)
                for k in range(QB + CB):
                    ins = nc.tensor.transpose(two_banks(4)[:, k * P:k * P + P], prob[:, 0, k * P:k * P + P], ident[:, :])
                ins.then_inc(mla_v_T, 1)
                pe.wait_ge(mla_free, h + 1)
                pe.wait_ge(w_lo_done, h * 4 + (u0 + 2))
                q_proj(P, 6).then_inc(mla_qr_proj, 1)
                pe.wait_ge(mla_v_lo, h + 1)
                q_proj(0, 4).then_inc(w_used, 1)
                pe.wait_ge(mla_qr_out, h + 1)
                mm(ps[:, 5, :], rot[0:64, :], qrf[:, :], start=True, stop=True).then_inc(mla_q_rotated, 1)
                filler(0)
                pe.wait_ge(mla_qk_lo, h * 2 + 2)
                pe.wait_ge(mla_qr_lo, h + 1)
                mla_scores(h, 0)
                for s in range(QB - 1):
                    mla_scores(h, s + 1)
                    filler(s + 1)
                    mla_transpose(h, s)
                values(0)
                mla_transpose(h, QB - 1)
                values(1).then_inc(mla_out, 1)

            pe.wait_ge(mla_free, MLA_HEADS + 1)
            with pe.Fori(0, KT // 2) as r:
                for par in range(2):
                    u0 = U_MG + par * 6
                    b0 = 4 * par
                    pe.wait_ge(mg_free, r * 2 + (par + 1))
                    proj_tile(u0 + r * 12, 0, ps[:, b0, :], None)
                    proj_tile(u0 + 2 + r * 12, 0, ps[:, b0 + 1, :], None)
                    for j, x in enumerate((B, A)):
                        pe.wait_ge((b_in, a_in)[j], 32)
                        pe.wait_ge(w_lo_done, u0 + 4 + j + 1 + r * 12)
                        for k in range(8):
                            for n, (wt, lo) in enumerate(PASS):
                                ins = mm(ps[:, b0 + 3 - j, :], wt[:, j, k * P:k * P + P], x[:, lo, k, :],
                                         start=k == 0 and n == 0, stop=k == 7 and n == 2)
                        ins.then_inc(w_used, 1)

            pe.wait_ge(mg_free, KT + 2)
            for c in range(4):
                for a in range(8):
                    g = ADA_FIRST + c * 8 + a
                    n_main = (U_OUT - g % RAWS + RAWS - 1) // RAWS
                    pe.wait_ge(raw_full[g % RAWS], (n_main + g // RAWS + 1) * 16)
                    ada_unit(a, g % RAWS, c % 2, a == 0, a == 7)
                if c >= 1:
                    pe.wait_ge(gate_row_ready, c)
                    if c >= 3:
                        pe.wait_ge(gate_ready, c - 2)
                    mm(ps[:, 2 + (c - 1) % 2, :], ones[0:1, :], gate_rows[0:1, (c - 1) % 2, :], start=True, stop=True).then_inc(gate_bc_sum, 1)
            pe.wait_ge(gate_row_ready, 4)
            pe.wait_ge(gate_ready, 2)
            mm(ps[:, 3, :], ones[0:1, :], gate_rows[0:1, 1, :], start=True, stop=True).then_inc(gate_bc_sum, 1)

            pe.wait_ge(gate_ready, 4)
            with pe.Fori(0, 2) as r:
                for par in range(2):
                    for c in range(8):
                        pe.wait_ge(w_lo_done, U_OUT + par * 8 + c + 1 + r * 16)
                        for half in range(2):
                            k = 2 * c + half
                            if par == 0:
                                pe.wait_ge(m_ready, k + 1)
                            for t in range(QB):
                                if k == 0:
                                    pe.wait_ge(o_free, (r * 2 + par) * QB + (t + 1))
                                tt = slice(t * P, t * P + P)
                                mv = slice(half * 512, half * 512 + 512)
                                o = ps[:, 4 * par + t, :]
                                mm(o, m_hi[:, k, tt], w_hi[:, c % WS, mv], start=k == 0, stop=False)
                                mm(o, m_lo[:, k, tt], w_hi[:, c % WS, mv], start=False, stop=False)
                                ins = mm(o, m_hi[:, k, tt], w_lo[:, c % WS, mv], start=False, stop=k == KT - 1)
                        ins.then_inc(w_used, 1)

        @block.scalar
        def _(act):
            def split_hi(c, off=0, per=0, late=False):
                n = c // RAWS + 1 + ADA_FIRST // RAWS + ((ADA_ALL - ADA_FIRST) // RAWS if late else 0)
                act.wait_ge(raw_full[c % RAWS], (n if per == 0 else off * (per // RAWS) + n) * 16)
                if per or c >= WS:
                    act.wait_ge(w_used, c - 1 if per == 0 else off * per + (c - 1))
                act.copy(w_hi[:, c % WS, :], raw[:, c % RAWS, :]).then_inc(w_hi_done, 1)

            def biased(dst, src, b):
                return act.activation(dst, src, ACT.Identity, bias=b)

            act.wait_ge(const_in, 12 * 16)
            act.activation(silu_e, cT, ACT.Exp, scale=-1.0).then_inc(silu_exp, 1)
            act.copy(ident_r[:, :], ident[:, :]).then_inc(const_r, 1)
            act.copy(masks_r[:, :, :], masks_f[:, :, :]).then_inc(const_r, 1)

            def ada_round(r):
                for half in range(2):
                    act.wait_ge(ada_used, r * 16 + (half * 8 + 8))
                    act.wait_ge(ada_col_ready, r * 2 + (half + 1))
                    act.copy(ada_rows[:, half, :], ps[0:2, half, :]).then_inc(ada_row_ready, 1)

            with act.Fori(0, 2) as r:
                ada_round(r)
            act.wait_ge(x_sum, 1)
            act.wait_ge(const_made, 1)
            act.activation(rstd[:, 0:SEQ], ps[:, 4, :], ACT.Sqrt, scale=1.0 / D, bias=eps_c)
            act.activation(rstd[:, SEQ:TOK], ps[:, 5, 0:CTX], ACT.Sqrt, scale=1.0 / D, bias=eps_c).then_inc(x_root, 1)
            with act.Fori(2, 4) as r:
                ada_round(r)
            split_hi(0)
            split_hi(1)
            for k in range(KT):
                act.wait_ge(h_made, k + 1)
                act.copy(h_hi[:, k, :], xT[:, k, 0:SEQ])
                act.copy(hc_hi[:, k, :], xT[:, k, SEQ:TOK]).then_inc(h_hi_done, 1)

            def z_round(r, per):
                i = slice(r, r + 1) if per == 0 else bass.ds(r, 1)
                b0 = bias[:, 0:1] if per == 0 else bias[:, bass.ds(r * 2, 1)]
                b1 = bias[:, 1:2] if per == 0 else bias[:, bass.ds(r * 2 + 1, 1)]
                split_hi(2, r, per)
                act.wait_ge(w_used, r * 4 + 2)
                biased(ckv[:, i, 0:SEQ], ps[:, 0, :], b0).then_inc(z_bank_free, 1)
                biased(ckv[:, i, SEQ:TOK], ps[:, 2, 0:CTX], b0).then_inc(z_bank_free, 1)
                split_hi(3, r, per)
                split_hi(4, r, per)
                act.wait_ge(w_used, r * 4 + 4)
                biased(cq[:, i, :], ps[:, 1, :], b1).then_inc(z_bank_free, 1)
                split_hi(5, r, per)

            act.wait_ge(h_ready, KT)
            z_round(0, 0)
            with act.Fori(1, RT) as r:
                z_round(r, 4)
            def rank_roots():
                act.wait_ge(n_sum, 1)
                for row, cols, src in ((0, slice(0, SEQ), ps[:, 5, :]), (0, slice(SEQ, TOK), ps[:, 6, 0:CTX]), (1, slice(0, SEQ), ps[:, 7, :])):
                    act.activation(nrstd[:, row, cols], src, ACT.Sqrt, scale=1.0 / RANK, bias=eps_c).then_inc(n_root, 1)

            for t in range(5):
                u = 16 + 2 * t
                split_hi(u + 2)
                act.wait_ge(w_used, u + 2)
                if t >= 2:
                    act.wait_ge(k_roped, t - 1)
                if t == 2:
                    act.wait_ge(kpe_lo_done, 1)
                biased(kraw[:, t % 2, 0:SEQ], ps[:, t % 2, :], bias[:, 8 + t:9 + t])
                biased(kraw[:, t % 2, SEQ:TOK], ps[:, 2 + t % 2, 0:CTX], bias[:, 8 + t:9 + t]).then_inc(z_rest_out, 1)
                split_hi(u + 3)
                if t == 1:
                    act.wait_ge(k_roped, 1)
                    act.copy(kpe_hi[0:64, :], kraw[0:64, 0, :])
                    act.copy(kpe_hi[64:P, :], kraw[0:64, 0, :]).then_inc(kpe_hi_done, 1)
                if t == 3:
                    rank_roots()
                if t == 4:
                    act.wait_ge(v_T_ready, 1)
                    act.copy(vT_f[:, 0, :], two_banks(5)[:, 0:TOK]).then_inc(v_T_out, 1)
            split_hi(U_Q + 2)
            act.wait_ge(w_used, U_Q + 2)
            biased(qf2[:, 0, :], ps[:, 7, :], bias[:, B_SWA:B_SWA + 1]).then_inc(swa_q_out, 1)
            act.wait_ge(v_T_ready, 2)
            act.copy(vT_f[:, 1, :], two_banks(5)[:, 0:TOK]).then_inc(v_T_out, 1)
            split_hi(U_Q + 3)
            split_hi(U_Q + 4)
            act.wait_ge(w_used, U_Q + 4)
            biased(qf2[:, 1, :], ps[:, 4, :], bias[:, B_SWA + 1:B_SWA + 2]).then_inc(swa_q_out, 1)
            split_hi(U_Q + 5)
            act.wait_ge(n_scaled, 2 * RT)

            def swa_softmax(g, s):
                wn = P * len(key_blocks(s // GROUP)) + 1
                n = g * 16 + s
                act.wait_ge(swa_negmax, n + 1)
                if n >= 2:
                    act.wait_ge(swa_pT, n - 1)
                act.activation(sprob[:, s % 2, 0:wn], two_banks(2 * (s % 2))[:, 769 - wn:769], ACT.Exp,
                               bias=neg_max[:, s % 2:s % 2 + 1], scale=SWA_SCALE,
                               accum_out=row_sum[:, s % 2:s % 2 + 1]).then_inc(swa_exp, 1)

            def swa_keys(g):
                kr = ks_f[64 * (g % 2):64 * (g % 2) + 64, g // 2, :]
                act.copy(k_hi2[0:64, :], kr)
                act.copy(k_hi2[64:P, :], kr).then_inc(swa_k_hi, 1)

            def swa_queries(g, j):
                act.wait_ge(swa_q_mixed, 2 * g + j + 1)
                act.copy(q_st[0:64, 2 * j, :], qf2[0:64, j, :])
                act.copy(q_st[0:64, 2 * j + 1, :], qf2[64:P, j, :])
                if 2 * g + j:
                    act.wait_ge(swa_q_lo, 2 * g + j)
                if g:
                    act.wait_ge(swa_gate_step, 6 * g - 3)
                act.copy(q_hiT[64:P, :], qf2[64:P, j, :]).then_inc(swa_q_hi, 1)

            def swa_gate_exp_of(g, j):
                act.wait_ge(swa_gate_z, 2 * g + j + 1)
                if j == 0:
                    act.wait_ge(swa_q_lo, 2 * g + 2)
                    if g:
                        act.wait_ge(swa_gate_step, 6 * g)
                else:
                    act.wait_ge(swa_gate_step, 6 * g + 3)
                    if g < KV_GROUPS - 1:
                        act.wait_ge(swa_q_lo, 2 * g + 4)
                act.activation(gate_e[:, :], s_gate[:, j, :], ACT.Exp, scale=-1.0).then_inc(swa_gate_exp, 1)

            def swa_gated_hi_of(g, j):
                act.wait_ge(swa_gated, 2 * g + j + 1)
                act.wait_ge(swa_spilled, (2 * g + j + 1) * 16)
                act.copy(s_stage[:, 0, :], b_T[:, j, :]).then_inc(swa_gated_hi, 1)

            swa_keys(0)
            swa_queries(0, 0)
            swa_queries(0, 1)
            act.copy(v_st[:, :, 0:64], vT_of(0)).then_inc(swa_v_hi, 1)
            swa_softmax(0, 0)
            for g in range(KV_GROUPS):
                last = g == KV_GROUPS - 1
                shares = 4 if last else 2
                for s in range(16):
                    b, n = s // GROUP, s % GROUP
                    nb = len(key_blocks(b))
                    if s < 15:
                        swa_softmax(g, s + 1)
                    if s == 15 and not last:
                        swa_keys(g + 1)
                        swa_queries(g + 1, 0)
                        swa_queries(g + 1, 1)
                    if s % shares == shares - 1:
                        split_hi(U_SWA + 8 * g + s // shares + 2)
                        if s in (3, 7) and not last:
                            j = s // 4
                            act.wait_ge(w_used, U_SWA + 8 * g + 2 * j + 2)
                            if j == 0:
                                act.wait_ge(swa_q_lo, 2 * g + 2)
                            c = B_SWA + 4 * (g + 1) + j
                            biased(qf2[:, j, :], ps[:, 7, :], bias[:, c:c + 1]).then_inc(swa_q_out, 1)
                    act.wait_ge(swa_pT, g * 16 + s + 1)
                    if n == 0 and g * 4 + b >= 1:
                        act.wait_ge(swa_out, g * 4 + b)
                    act.copy(spt_hi[:, 0:nb, n, :], two_banks(4)[:, 0:nb * P].rearrange("p (k n) -> p k n", n=P)).then_inc(swa_pT_hi, 1)
                    if s == 15 and not last:
                        swa_softmax(g + 1, 0)
                    if s == 1 and g:
                        swa_gated_hi_of(g - 1, 0)
                    if s == 2 and g:
                        swa_gated_hi_of(g - 1, 1)
                    if n == GROUP - 1:
                        act.wait_ge(swa_out, g * 4 + b + 1)
                        act.copy(o_low[:, :], ps[64:P, 6, :]).then_inc(swa_out_low, 1)
                    if s == (7 if last else 11):
                        swa_gate_exp_of(g, 0)
                    if s == 15:
                        if not last:
                            act.copy(v_st[:, :, 0:64], vT_of(g + 1)).then_inc(swa_v_hi, 1)
                        else:
                            act.wait_ge(swa_pT_lo, 64)
                            for k in range(RT):
                                act.copy(ckv_hi[:, k, :], ckv[:, k, :]).then_inc(n_hi, 1)
                            for k in range(RT):
                                act.copy(cq_hi[:, k, :], cq[:, k, :]).then_inc(n_hi, 1)
                        swa_gate_exp_of(g, 1)
            swa_gated_hi_of(3, 0)
            swa_gated_hi_of(3, 1)
            act.wait_ge(n_lo, 2 * RT)

            def mla_softmax(h, s):
                act.wait_ge(mla_negmax, h * QB + (s + 1))
                if s >= 2:
                    act.wait_ge(mla_pT, h * QB + (s - 1))
                act.activation(prob[:, s % 2, :], two_banks(2 * (s % 2))[:, 0:TOK], ACT.Exp,
                               bias=neg_max[:, s % 2:s % 2 + 1], scale=MLA_SCALE,
                               accum_out=row_sum[:, s % 2:s % 2 + 1]).then_inc(mla_exp, 1)

            with act.Fori(0, MLA_HEADS) as h:
                u0 = U_MLA
                act.wait_ge(mla_v_proj, h + 1)
                act.wait_ge(mla_free, h + 1)
                act.copy(prob[:, 0, :], two_banks(2)[:, 0:TOK]).then_inc(mla_v_out, 1)
                split_hi(u0 + 2, h, 4)
                act.copy(kn_hi[:, :], two_banks(0)[:, 0:TOK]).then_inc(mla_qk_hi, 1)
                act.wait_ge(mla_v_T, h + 1)
                act.copy(v_hi[:, :, :], two_banks(4)[:, 0:TOK].rearrange("p (k n) -> p k n", n=P)).then_inc(mla_v_hi, 1)
                act.wait_ge(mla_qr_proj, h + 1)
                act.copy(qrf[:, :], ps[0:64, 6, :]).then_inc(mla_qr_out, 1)
                split_hi(u0 + 3, h, 4)
                act.copy(qn_hi[:, :], ps[:, 4, :]).then_inc(mla_qk_hi, 1)
                act.wait_ge(mla_q_mixed, h + 1)
                act.copy(qr_st[0:64, :], qrf[:, :]).then_inc(mla_qr_hi, 1)
                mla_softmax(h, 0)
                for s in range(QB):
                    if s < QB - 1:
                        mla_softmax(h, s + 1)
                    if s % 2 == 0:
                        split_hi(u0 + 4 + s // 2, h, 4)
                    act.wait_ge(mla_pT, h * QB + (s + 1))
                    act.copy(pt_hi[:, :, s * P:s * P + P], two_banks(4)[:, 0:TOK].rearrange("p (k n) -> p k n", n=P)).then_inc(mla_pT_hi, 1)
                    if s == QB - 2:
                        act.wait_ge(mla_gate_z, h + 1)
                        act.activation(prob[:, 0, 0:SEQ], a_gate[:, :], ACT.Exp, scale=-1.0).then_inc(mla_gate_exp, 1)
                act.wait_ge(mla_free, h + 2)
                act.wait_ge(mla_spilled, (h + 1) * 16)
                act.copy(a_stage[:, 0, :], a_gate[:, :]).then_inc(mla_gated_hi, 1)

            act.wait_ge(mla_spilled, 9 * 16)
            def merge_round(r, last):
                for par in range(2):
                    u0 = U_MG + par * 6
                    for j, sg in enumerate((sg_a, sg_b)):
                        split_hi(u0 + 2 * j + 2, r, 12)
                        act.wait_ge(w_used, r * 12 + (u0 + 2 * j + 2))
                        if j == 0:
                            act.wait_ge(mg_free, r * 2 + (par + 2))
                        col = r * 4 + (B_MG + par * 2 + j)
                        act.activation(sg[:, :], ps[:, 4 * par + j, :], ACT.Exp, scale=-1.0,
                                       bias=nbias[:, (slice(col, col + 1) if last else bass.ds(col, 1))]).then_inc(mg_exp, 1)
                        split_hi(u0 + 2 * j + 3, r, 12)
                    if not (last and par == 1):
                        split_hi(u0 + 6, r, 12)
                        split_hi(u0 + 7, r, 12)

            act.wait_ge(nbias_made, 1)
            with act.Fori(0, KT // 2 - 1) as r:
                merge_round(r, False)
            merge_round(KT // 2 - 1, True)

            act.wait_ge(w_used, U_OUT)
            for k in range(KT):
                act.wait_ge(mg_free, k + 3)
                act.copy(m_hi[:, k, :], m_f[:, k, :]).then_inc(m_hi_done, 1)
            for c in range(4):
                act.wait_ge(ada_used, ADA_FIRST + 8 * c + 8)
                if c >= 2:
                    act.wait_ge(gate_bc_sum, c - 1)
                act.copy(gate_rows[:, c % 2, :], ps[0:2, c % 2, :]).then_inc(gate_row_ready, 1)

            split_hi(U_OUT, late=True)
            split_hi(U_OUT + 1, late=True)

            def out_chunk(r, par, last):
                for c in range(8):
                    if not (last and c >= 6):
                        split_hi(U_OUT + par * 8 + c + 2, r, 16, late=True)
                for t in range(QB):
                    n = (r * 2 + par) * QB + t
                    act.wait_ge(o_added, n + 1)
                    if n:
                        act.wait_ge(o_squared, n)
                    col = r * 8 + (par * 4 + t)
                    act.activation(y_sq[:, :], y[:, t, (2 * r + par) * 512:(2 * r + par) * 512 + 512], ACT.Square,
                                   accum_out=sumsq[:, (slice(col, col + 1) if isinstance(col, int) else bass.ds(col, 1))]).then_inc(o_squared, 1)

            out_chunk(0, 0, False)
            out_chunk(0, 1, False)
            out_chunk(1, 0, False)
            out_chunk(1, 1, True)
            act.wait_ge(o_ms, 1)
            act.activation(tok_ms, tok_ms, ACT.Sqrt, scale=1.0 / D, bias=eps_c).then_inc(o_root, 1)

        @block.vector
        def _(dve):
            tt, ts, stt = dve.tensor_tensor, dve.tensor_scalar, dve.scalar_tensor_tensor

            def f(ap):
                return ap.bitcast(F32)

            dve.memset(ones[:, :], 1.0).then_inc(ada_col_out, 2)
            dve.memset(eps_c, EPS).then_inc(const_made, 1)
            dve.memset(row_sum, 0.0).then_inc(ada_col_ready, 2)
            dve.memset(neg_max, 0.0).then_inc(swa_out_free, 1)
            dve.memset(row_inv, 0.0).then_inc(mla_free, 1)
            dve.memset(tok_ms, 0.0).then_inc(mg_free, 2)
            dve.memset(tok_inv, 0.0).then_inc(o_free, 2 * QB)
            dve.memset(sumsq, 0.0).then_inc(swa_spilled, 16)
            dve.memset(shift, 0.0).then_inc(mla_spilled, 16)
            dve.wait_ge(const_in, 12 * 16)
            ts(nbias, bias, -1.0, None, ALU.mult)
            ts(sink8, sink, 1.0 / SWA_SCALE, None, ALU.mult).then_inc(nbias_made, 1)
            dve.wait_ge(silu_exp, 1)
            ts(silu_e, silu_e, 1.0, None, ALU.add).then_inc(silu_step, 1)
            dve.wait_ge(silu_step, 1)
            dve.reciprocal(silu_e, silu_e).then_inc(silu_step, 1)
            dve.wait_ge(silu_step, 2)
            tt(silu_c, silu_e, cT, ALU.mult).then_inc(silu_ready, 1)

            dve.wait_ge(x_in, 4 * 16)
            tt(sq_sum[:, :], xT[:, 0, :], xT[:, 0, :], ALU.mult).then_inc(sq_added, 1)
            with dve.Fori(1, KT) as k:
                xk = xT[:, bass.ds(k, 1), :].rearrange("p a n -> p (a n)")
                dve.wait_ge(sq_added, k)
                tt(sq[:, :], xk, xk, ALU.mult).then_inc(sq_made, 1)
                dve.wait_ge(sq_made, k)
                tt(sq_sum[:, :], sq_sum[:, :], sq[:, :], ALU.add).then_inc(sq_added, 1)

            def ada_round(r):
                for half in range(2):
                    dve.wait_ge(ada_col_ready, r * 2 + (half + 3))
                    cols = bass.ds(r * 8 + half * 4, 4)
                    tt(mod[:, cols, :], ps[:, 2 + half, 0:8].rearrange("p (f v) -> p f v", v=2), b_ada[:, cols, :], ALU.add).then_inc(ada_col_out, 1)

            with dve.Fori(0, 2) as r:
                ada_round(r)
            dve.wait_ge(x_root, 1)
            dve.reciprocal(rstd[:, :], rstd[:, :]).then_inc(x_rstd, 1)
            dve.wait_ge(x_rstd, 1)
            with dve.Fori(0, KT) as k:
                xk = xT[:, bass.ds(k, 1), :].rearrange("p a n -> p (a n)")
                tt(xk, xk, rstd[:, :], ALU.mult).then_inc(x_normed, 1)
            with dve.Fori(2, 4) as r:
                ada_round(r)
            dve.wait_ge(ada_col_out, 10)
            stt(scale1, scale1, 1.0, norm_g, ALU.add, ALU.mult).then_inc(scale_made, 1)
            dve.wait_ge(scale_made, 1)
            dve.wait_ge(x_normed, KT)

            def h_make(k):
                for v, c in ((0, slice(0, SEQ)), (1, slice(SEQ, TOK))):
                    ins = ts(xT[:, k, c], xT[:, k, c], scale1[:, k, v:v + 1], shift[:, k, v:v + 1], ALU.mult, ALU.add)
                ins.then_inc(h_made, 1)

            h_make(0)
            for k in range(KT):
                if k < KT - 1:
                    h_make(k + 1)
                dve.wait_ge(h_hi_done, k + 1)
                tt(h_lo[:, k, :], xT[:, k, 0:SEQ], f(h_hi[:, k, :]), ALU.subtract)
                tt(hc_lo[:, k, :], xT[:, k, SEQ:TOK], f(hc_hi[:, k, :]), ALU.subtract).then_inc(h_ready, 1)

            dve.wait_ge(z_bank_free, 3 * RT)
            for k in range(RT):
                tt(nsq_kv[:, k, :], ckv[:, k, :], ckv[:, k, :], ALU.mult).then_inc(n_sq, 1)
                tt(nsq_q[:, k, :], cq[:, k, :], cq[:, k, :], ALU.mult).then_inc(n_sq, 1)
            for t in range(3):
                m = 64 if t == 0 else P
                dst = kraw[0:m, 0, 0:SEQ] if t == 0 else ks_f[:, t - 1, 0:SEQ]
                dve.wait_ge(k_rot_ready, t + 1)
                tt(krot[0:m, :], ps[0:m, 4, :], sin[0:m, :], ALU.mult).then_inc(k_step, 1)
                if t >= 1:
                    dve.tensor_copy(ks_f[:, t - 1, SEQ:TOK], kraw[:, t % 2, SEQ:TOK])
                tt(dst, kraw[0:m, t % 2, 0:SEQ], cos[0:m, :], ALU.mult).then_inc(k_step, 1)
                dve.wait_ge(k_step, 2 * t + 2)
                tt(dst, dst, krot[0:m, :], ALU.add).then_inc(k_roped, 1)
                if t == 0:
                    dve.wait_ge(kpe_hi_done, 1)
                    dve.wait_ge(k_roped, 1)
                    tt(kpe_lo[0:64, :], kraw[0:64, 0, :], f(kpe_hi[0:64, :]), ALU.subtract)
                    tt(kpe_lo[64:P, :], kraw[0:64, 0, :], f(kpe_hi[0:64, :]), ALU.subtract).then_inc(kpe_lo_done, 1)
            dve.wait_ge(n_root, 3)
            dve.reciprocal(nrstd[:, 0, :], nrstd[:, 0, :]).then_inc(n_rstd, 1)
            dve.reciprocal(nrstd[:, 1, 0:SEQ], nrstd[:, 1, 0:SEQ]).then_inc(n_rstd, 1)
            dve.wait_ge(n_rstd, 2)
            for k in range(RT):
                stt(ckv[:, k, :], ckv[:, k, :], kvn_g[:, k:k + 1], nrstd[:, 0, :], ALU.mult, ALU.mult).then_inc(n_scaled, 1)
                stt(cq[:, k, :], cq[:, k, :], qn_g[:, k:k + 1], nrstd[:, 1, 0:SEQ], ALU.mult, ALU.mult).then_inc(n_scaled, 1)

            def row_max(n, s, src, scores, max_done, negmax_done, scale):
                dve.wait_ge(scores, n)
                dve.tensor_reduce(neg_raw[:, s:s + 1], src, AX.X, ALU.max, negate=True).then_inc(max_done, 1)
                dve.wait_ge(max_done, n)
                ts(neg_max[:, s:s + 1], neg_raw[:, s:s + 1], scale, None, ALU.mult).then_inc(negmax_done, 1)

            def normalise(n, s, p, exp_done, inv_done, prob_done):
                dve.wait_ge(exp_done, n)
                dve.reciprocal(row_inv[:, s:s + 1], row_sum[:, s:s + 1]).then_inc(inv_done, 1)
                dve.wait_ge(inv_done, n)
                ts(p, p, row_inv[:, s:s + 1], None, ALU.mult).then_inc(prob_done, 1)

            def swa_unit(g, s):
                nb = len(key_blocks(s // GROUP))
                n = g * 16 + s + 1
                row_max(n, s % 2, two_banks(2 * (s % 2))[:, 768 - nb * P:769], swa_s, swa_max, swa_negmax, SWA_SCALE)
                normalise(n, s % 2, sprob[:, s % 2, 0:nb * P], swa_exp, swa_inv, swa_prob)

            def sigmoid_of(e, n, step):
                ts(e, e, 1.0, None, ALU.add).then_inc(step, 1)
                dve.wait_ge(step, n + 1)
                dve.reciprocal(e, e).then_inc(step, 1)
                dve.wait_ge(step, n + 2)

            def swa_rope(n):
                j = n % 2
                if n:
                    dve.wait_ge(swa_q_mixed, n)
                dve.wait_ge(swa_q_rotated, n + 1)
                tt(qt[:, :], ps[:, (5 + j if n < 2 else 6), :], sin[:, :], ALU.mult)
                tt(qf2[:, j, :], qf2[:, j, :], cos[:, :], ALU.mult).then_inc(swa_q_step, 1)
                dve.wait_ge(swa_q_step, n + 1)
                tt(qf2[:, j, :], qf2[:, j, :], qt[:, :], ALU.add).then_inc(swa_q_mixed, 1)

            def swa_operands(g):
                rows = slice(64 * (g % 2), 64 * (g % 2) + 64)
                kr = ks_f[rows, g // 2, :]
                dve.wait_ge(swa_k_hi, g + 1)
                tt(k_lo2[0:64, :], kr, f(k_hi2[rows, :]), ALU.subtract)
                tt(k_lo2[64:P, :], kr, f(k_hi2[rows, :]), ALU.subtract).then_inc(swa_k_lo, 1)
                for j in range(2):
                    dve.wait_ge(swa_q_hi, 2 * g + j + 1)
                    dve.wait_ge(swa_q_mixed, 2 * g + j + 1)
                    tt(q_st[64:P, 2 * j, :], qf2[0:64, j, :], f(q_st[0:64, 2 * j, :]), ALU.subtract)
                    tt(q_st[64:P, 2 * j + 1, :], qf2[64:P, j, :], f(q_hiT[64:P, :]), ALU.subtract).then_inc(swa_q_lo, 1)

            def swa_values_lo(g):
                dve.wait_ge(swa_v_hi, g + 1)
                tt(v_st[:, :, 64:P], vT_of(g), f(v_st[:, :, 0:64]), ALU.subtract).then_inc(swa_v_lo, 1)

            def swa_gate_of(g, j):
                n = 2 * g + j
                dve.wait_ge(swa_gate_exp, n + 1)
                sigmoid_of(gate_e[:, :], n * 3, swa_gate_step)
                tt(s_gate[:, j, :], s_gate[:, j, :], gate_e[:, :], ALU.mult).then_inc(swa_gate_step, 1)

            def swa_gated_of(g, j):
                n = 2 * g + j
                dve.wait_ge(swa_gate_step, n * 3 + 3)
                dve.wait_ge(swa_out_free, g * 4 + 5)
                tt(b_T[:, j, :], b_T[:, j, :], s_gate[:, j, :], ALU.mult).then_inc(swa_gated, 1)

            def swa_gated_lo_of(g, j):
                dve.wait_ge(swa_gated_hi, 2 * g + j + 1)
                tt(s_stage[:, 1, :], b_T[:, j, :], f(s_stage[:, 0, :]), ALU.subtract).then_inc(swa_gated_lo, 1)

            swa_rope(0)
            swa_rope(1)
            swa_operands(0)
            swa_values_lo(0)
            swa_unit(0, 0)
            for g in range(KV_GROUPS):
                last = g == KV_GROUPS - 1
                for s in range(16):
                    b, n = s // GROUP, s % GROUP
                    nb = len(key_blocks(b))
                    if s < 15:
                        swa_unit(g, s + 1)
                    elif not last:
                        swa_operands(g + 1)
                    if s in ((7, 15) if last else (11, 15)):
                        j = int(s == 15)
                        c = B_SWA + 4 * g + 2 + j
                        u = U_SWA + 8 * g + (0 if last else 4) + 2 * j + 2
                        dve.wait_ge(w_used, u)
                        ts(s_gate[:, j, :], ps[:, 7, :], bias[:, c:c + 1], None, ALU.add).then_inc(swa_gate_z, 1)
                    dve.wait_ge(swa_pT_hi, g * 16 + s + 1)
                    tt(spt_lo[:, 0:nb, n, :], two_banks(4)[:, 0:nb * P].rearrange("p (k n) -> p k n", n=P),
                       f(spt_hi[:, 0:nb, n, :]), ALU.subtract).then_inc(swa_pT_lo, 1)
                    if s == 15 and not last:
                        swa_unit(g + 1, 0)
                    if s in ROTATE and not last:
                        swa_rope(2 * g + 2 + ROTATE.index(s))
                    if g and s == 0:
                        swa_gate_of(g - 1, 1)
                        swa_gated_of(g - 1, 0)
                    if g and s == 1:
                        swa_gated_of(g - 1, 1)
                        swa_gated_lo_of(g - 1, 0)
                    if g and s == 2:
                        swa_gated_lo_of(g - 1, 1)
                    if n == GROUP - 1:
                        dve.wait_ge(swa_out_low, g * 4 + b + 1)
                        if g and b == 0:
                            dve.wait_ge(swa_gated_lo, 2 * g)
                        for odd in range(2):
                            ins = tt(b_T[64 * odd:64 * odd + 64, :, b * P:b * P + P],
                                     ps[0:64, 6, :].rearrange("p (j o n) -> p j o n", o=2, n=P)[:, :, odd, :],
                                     o_low[:, :].rearrange("p (j o n) -> p j o n", o=2, n=P)[:, :, odd, :], ALU.add)
                        ins.then_inc(swa_out_free, 1)
                    if s == (8 if last else 12):
                        swa_gate_of(g, 0)
                    if s == 15:
                        if not last:
                            swa_values_lo(g + 1)
                        else:
                            for k in range(RT):
                                dve.wait_ge(n_hi, k + 1)
                                tt(ckv_lo[:, k, :], ckv[:, k, :], f(ckv_hi[:, k, :]), ALU.subtract).then_inc(n_lo, 1)
                            for k in range(RT):
                                dve.wait_ge(n_hi, RT + k + 1)
                                tt(cq_lo[:, k, :], cq[:, k, :], f(cq_hi[:, k, :]), ALU.subtract).then_inc(n_lo, 1)
            swa_gate_of(3, 1)
            for j in range(2):
                swa_gated_of(3, j)
            for j in range(2):
                swa_gated_lo_of(3, j)
            dve.wait_ge(swa_spilled, 9 * 16)

            def mla_unit(h, s):
                n = h * QB + (s + 1)
                row_max(n, s % 2, two_banks(2 * (s % 2))[:, 0:TOK], mla_s, mla_max, mla_negmax, MLA_SCALE)
                normalise(n, s % 2, prob[:, s % 2, :], mla_exp, mla_inv, mla_prob)

            with dve.Fori(0, MLA_HEADS) as h:
                u0 = U_MLA
                dve.wait_ge(mla_qk_hi, h * 2 + 1)
                tt(kn_lo[:, :], two_banks(0)[:, 0:TOK], f(kn_hi[:, :]), ALU.subtract).then_inc(mla_qk_lo, 1)
                dve.wait_ge(mla_v_hi, h + 1)
                tt(v_lo[:, :, :], two_banks(4)[:, 0:TOK].rearrange("p (k n) -> p k n", n=P), f(v_hi[:, :, :]), ALU.subtract).then_inc(mla_v_lo, 1)
                dve.wait_ge(mla_qk_hi, h * 2 + 2)
                tt(qn_lo[:, :], ps[:, 4, :], f(qn_hi[:, :]), ALU.subtract).then_inc(mla_qk_lo, 1)
                dve.wait_ge(mla_q_rotated, h + 1)
                tt(a_gate[0:64, :], ps[0:64, 5, :], sin[0:64, :], ALU.mult)
                tt(qrf[:, :], qrf[:, :], cos[0:64, :], ALU.mult).then_inc(mla_q_step, 1)
                dve.wait_ge(mla_q_step, h + 1)
                tt(qrf[:, :], qrf[:, :], a_gate[0:64, :], ALU.add).then_inc(mla_q_mixed, 1)
                dve.wait_ge(mla_qr_hi, h + 1)
                tt(qr_st[64:P, :], qrf[:, :], f(qr_st[0:64, :]), ALU.subtract).then_inc(mla_qr_lo, 1)
                mla_unit(h, 0)
                for s in range(QB):
                    if s < QB - 1:
                        mla_unit(h, s + 1)
                    if s == QB - 2:
                        dve.wait_ge(w_used, h * 4 + (u0 + 4))
                        ts(a_gate[:, :], ps[:, 7, :], bias[:, bass.ds(h + B_MLA, 1)], None, ALU.add).then_inc(mla_gate_z, 1)
                    dve.wait_ge(mla_pT_hi, h * QB + (s + 1))
                    tt(pt_lo[:, :, s * P:s * P + P], two_banks(4)[:, 0:TOK].rearrange("p (k n) -> p k n", n=P),
                       f(pt_hi[:, :, s * P:s * P + P]), ALU.subtract).then_inc(mla_pT_lo, 1)
                e = prob[:, 0, 0:SEQ]
                dve.wait_ge(mla_gate_exp, h + 1)
                sigmoid_of(e, h * 3, mla_gate_step)
                tt(a_gate[:, :], a_gate[:, :], e, ALU.mult).then_inc(mla_gate_step, 1)
                dve.wait_ge(mla_gate_step, h * 3 + 3)
                dve.wait_ge(mla_out, h + 1)
                tt(a_gate[:, :], ps[:, 6, :], a_gate[:, :], ALU.mult).then_inc(mla_free, 1)
                dve.wait_ge(mla_gated_hi, h + 1)
                tt(a_stage[:, 1, :], a_gate[:, :], f(a_stage[:, 0, :]), ALU.subtract).then_inc(mla_gated_lo, 1)
                dve.wait_ge(mla_gated_lo, h + 1)

            with dve.Fori(0, KT // 2) as r:
                for par in range(2):
                    for j, sg in enumerate((sg_a, sg_b)):
                        n = (r * 4 + (par * 2 + j)) * 3
                        dve.wait_ge(mg_exp, r * 4 + (par * 2 + j + 1))
                        sigmoid_of(sg[:, :], n, mg_step)
                        dve.wait_ge(w_used, r * 12 + (U_MG + par * 6 + 6 - j))
                        tt(sg[:, :], sg[:, :], ps[:, 4 * par + 2 + j, :], ALU.mult).then_inc(mg_step, 1)
                    dve.wait_ge(mg_step, (r * 4 + (par * 2 + 2)) * 3)
                    tt(m_f[:, bass.ds(r * 2 + par, 1), :].rearrange("p a n -> p (a n)"), sg_a[:, :], sg_b[:, :], ALU.add).then_inc(mg_free, 1)
            for k in range(KT):
                dve.wait_ge(m_hi_done, k + 1)
                tt(m_lo[:, k, :], m_f[:, k, :], f(m_hi[:, k, :]), ALU.subtract).then_inc(m_ready, 1)
            dve.wait_ge(late_in, 32)
            for c in range(4):
                dve.wait_ge(gate_bc_sum, c + 1)
                gc = gate_bc[:, c * 512:c * 512 + 512]
                tt(gc, gc, ps[:, 2 + c % 2, :], ALU.add).then_inc(gate_ready, 1)

            dve.wait_ge(y_in, 16)
            dve.wait_ge(gate_ready, 4)
            with dve.Fori(0, 2) as r:
                for par in range(2):
                    cc = bass.ds(r * 1024 + par * 512, 512)
                    dve.wait_ge(w_used, r * 16 + (U_OUT + par * 8 + 8))
                    for t in range(QB):
                        n = (r * 2 + par) * QB + (t + 1)
                        tt(y_add[:, t, :], ps[:, 4 * par + t, :], gate_bc[:, cc], ALU.mult).then_inc(o_free, 1)
                        dve.wait_ge(o_free, n + 2 * QB)
                        tt(y[:, t, cc], y[:, t, cc], y_add[:, t, :], ALU.add).then_inc(o_added, 1)
            dve.wait_ge(o_squared, 4 * QB)
            dve.tensor_reduce(tok_ms, sumsq.rearrange("p (n t) -> p t n", t=QB), AX.X, ALU.add).then_inc(o_ms, 1)
            dve.wait_ge(o_root, 1)
            dve.reciprocal(tok_inv, tok_ms).then_inc(o_inv, 1)
            dve.wait_ge(o_inv, 1)
            for t in range(QB):
                stt(y[:, t, :], y[:, t, :], tok_inv[:, t:t + 1], fin_g[:, :], ALU.mult, ALU.mult).then_inc(o_final, 1)


def rope_tables(np):
    n, grid_w = 16, 64
    inv = (np.float32(10000.0) ** (-np.arange(n, dtype=np.float32) / np.float32(n))).astype(np.float32)
    tok = np.arange(SEQ)
    pos = np.stack([tok // grid_w, tok % grid_w]).astype(np.float32)
    feat = np.arange(P) % 64
    ang = (pos[feat // 32] * inv[feat % 16][:, None]).astype(np.float32)
    rot = np.zeros((P, P), np.float32)
    for d in range(P):
        if d % 32 < 16:
            rot[d + 16, d] = -1.0
        else:
            rot[d - 16, d] = 1.0
    q, k = np.arange(P)[:, None], np.arange(P)[None, :]
    masks = np.zeros((P, 2, P), np.float32)
    masks[:, 0][k < q] = NEG
    masks[:, 1][k > q] = NEG
    return np.cos(ang).astype(np.float32), np.sin(ang).astype(np.float32), rot, np.eye(P, dtype=np.float32), masks


def kernel(**inputs):
    import numpy as np
    import concourse.bacc as bacc
    from concourse.bass_utils import run_bass_kernel_spmd as run

    a = {k: np.asarray(v) for k, v in inputs.items()}
    w_in, b_in = a["w_in"][0], a["b_in"][0]
    c_q, c_kv, k_pe, gate_a, q_s, k_s, v_s, gate_b, mg_a, mg_b = (
        0, 512, 1024, 1088, 2112, 3136, 3392, 3648, 4672, 6720)

    cols = []
    for i in range(RT):
        cols += [c_kv + P * i, c_q + P * i]
    cols += [k_pe, k_s, k_s + P, v_s, v_s + P]
    swa_cols = []
    swa_stream = [q_s, q_s + P]
    for g in range(KV_GROUPS):
        swa_cols += [q_s + 256 * g, q_s + 256 * g + P, gate_b + 256 * g, gate_b + 256 * g + P]
        if g < KV_GROUPS - 1:
            swa_stream += [q_s + 256 * (g + 1), q_s + 256 * (g + 1) + P]
        swa_stream += [gate_b + 256 * g, gate_b + 256 * g + P]
    mla_cols = [gate_a + P * h for h in range(MLA_HEADS)]
    mg_cols = []
    for j in range(KT):
        mg_cols += [mg_a + P * j, mg_b + P * j]

    def tile_units(w, c):
        t = w[:, c:c + P].reshape(-1, 8, P, P)
        return [u.transpose(1, 0, 2).reshape(P, UNIT) for u in t]

    def rank_unit(w, cs):
        t = np.concatenate([w[:, c0:c1] for c0, c1 in cs], axis=1)
        return t.reshape(RT, P, 256).transpose(1, 0, 2).reshape(P, UNIT)

    units = []
    for c in cols + swa_stream:
        units += tile_units(w_in, c)
    w_uq, w_ukv = a["w_uq"][0], a["w_ukv"][0]
    for h in range(MLA_HEADS):
        q0, k0 = h * (NOPE + ROPE), h * 256
        units.append(rank_unit(w_ukv, [(k0, k0 + 256)]))
        units.append(rank_unit(w_uq, [(q0, q0 + 192), (q0, q0 + 64)]))
        units += tile_units(w_in, mla_cols[h])
    for j in range(KT):
        units += tile_units(w_in, mg_cols[2 * j]) + tile_units(w_in, mg_cols[2 * j + 1])
        units += tile_units(a["w_branch_b"][0], P * j) + tile_units(a["w_branch_a"][0], P * j)
    w_out = a["w_out"][0]
    for n in range(4):
        for c in range(8):
            t = w_out[256 * c:256 * c + 256, 512 * n:512 * n + 512]
            units.append(t.reshape(2, P, 512).transpose(1, 0, 2).reshape(P, UNIT))
    stream = np.stack(units)
    ada = a["w_ada"][0].reshape(8, 2, P, 12, 512).transpose(3, 0, 2, 1, 4).reshape(ADA_ALL, P, UNIT)

    def columns(v):
        return v.reshape(-1, P).T

    def twice(v):
        return np.stack([columns(v), columns(v)], axis=-1)

    b_cols = [b_in[c:c + P] for c in cols + swa_cols + mla_cols + mg_cols]
    cos, sin, rot, ident, masks = rope_tables(np)
    b_ada = a["b_ada"][0]
    data = {
        "xT": np.concatenate([a["x"][0].T.reshape(KT, P, SEQ), a["ctx"][0].T.reshape(KT, P, CTX)], axis=2).transpose(1, 0, 2),
        "x": a["x"][0],
        "cT": np.stack([columns(a["c"][0]), columns(a["c_ctx"])], axis=-1),
        "ada": ada,
        "b_adaT": twice(b_ada[0:2 * D]),
        "b_gate": np.broadcast_to(b_ada[2 * D:3 * D], (P, D)),
        "norm_gT": twice(a["norm_g"][0]),
        "stream": stream,
        "biasT": np.stack(b_cols, axis=1),
        "qn_gT": columns(a["q_norm_g"][0]),
        "kvn_gT": columns(a["kv_norm_g"][0]),
        "sink": a["sink"],
        "final_g": np.broadcast_to(a["final_g"], (P, D)),
        "cos": cos, "sin": sin, "rot": rot, "ident": ident, "masks": masks,
    }
    nc = bacc.Bacc("TRN2", target_bir_lowering=False, num_devices=1)
    arrays, args = {}, []
    for name, v in data.items():
        v = np.ascontiguousarray(v)
        arrays["in_" + name] = v
        args.append(nc.dram_tensor("in_" + name, v.shape, mybir.dt.from_np(v.dtype), kind="ExternalInput").ap())
    out = nc.dram_tensor("out", (SEQ, D), F32, kind="ExternalOutput").ap()
    build(nc, *args, out)
    r = run(nc, [arrays], core_ids=[0])
    return r.results[0]["out"].reshape(1, SEQ, D)
```

```python
import concourse.bass as bass
from concourse import mybir
from contextlib import ExitStack

F32 = mybir.dt.float32
F32R = mybir.dt.float32r
ALU = mybir.AluOpType
ACT = mybir.ActivationFunctionType
AX = mybir.AxisListType

P = 128
D = 2048
SEQ, CTX = 512, 256
TOK = SEQ + CTX
KT = D // P
EPS = 1e-6
NEG = -1e30
RANK = 512
RT = RANK // P
MLA_HEADS, NOPE, ROPE = 8, 128, 64
MLA_SCALE = float(NOPE + ROPE) ** -0.5
SWA_HEADS, KV_GROUPS, HD = 16, 4, 64
GROUP = SWA_HEADS // KV_GROUPS
SWA_SCALE = float(HD) ** -0.5
QB = SEQ // P
CB = CTX // P
UNIT = 1024

CHUNKS = 8
EARLY = 4
U_S = 8 * CHUNKS + EARLY
U_Z = U_S + EARLY
U_REST = U_Z + 2 * (8 - EARLY)
U_Q = U_REST + 2 * 5
U_SWA = U_Q + 4
U_MLA = U_SWA + KV_GROUPS * 8 - 4
U_MG = U_MLA + MLA_HEADS * 4
U_OUT = U_MG + KT * 6
U_END = U_OUT + 32
U_LAST = U_END - 4
B_SWA, B_MLA, B_MG = 13, 13 + 16, 13 + 16 + 8
B_END = B_MG + 32
RAWS, WS = 4, 2
ROTATE = (5, 9)
K_PARTS = (slice(0, 2 * P), slice(SEQ, TOK), slice(2 * P, SEQ))
Q_PARTS = (slice(0, 3 * P), slice(3 * P, SEQ))
AHEAD = 5
GATE_TILES = 64


def chunk_unit(n):
    return 8 * n + max(0, n - (CHUNKS - EARLY))


def early_unit(i):
    return chunk_unit(CHUNKS - EARLY + i) + 8


WS0, U_WS0 = 3, 66


def w_slot(u):
    if u >= U_LAST:
        return None, 0
    if u < U_WS0:
        return u % WS0, u - WS0 + 1
    return u % WS, (u - WS if u >= U_WS0 + WS else U_WS0 - WS0 + u % WS) + 1


SQ0 = 8
U_ROOT = SQ0 + KT + 1
H_AT = dict(zip((28, 30, 32, 34, 37, 38, 39, 40, 56, 58, 60, 62), range(12)))


def build(nc, xT_d, x_d, cT_d, gate_w_d, pair_d, b_adaT_d, b_gate_d, norm_gT_d, stream_d, biasT_d, qn_gT_d, kvn_gT_d,
          sink_d, final_g_d, cos_d, sin_d, rot_d, ident_d, masks_d, out_d):
    es = ExitStack()
    with es:
        base = (nc.sbuf_base + 63) // 64 * 64
        KB = 1024

        def at(name, off_kb, shape, dt=F32):
            return nc.alloc_sbuf_tensor_at(name, shape, dt, offset=base + int(off_kb * KB))

        def sem(name):
            return es.enter_context(nc.semaphore(name))

        h_hi = at("h_hi", 0, [P, KT, SEQ], F32R)
        h_lo = at("h_lo", 32, [P, KT, SEQ], F32R)
        m_hi = at("m_hi", 0, [P, KT, SEQ], F32R)
        m_lo = at("m_lo", 32, [P, KT, SEQ], F32R)
        raw = at("raw", 64, [P, RAWS, UNIT])
        w_hi = at("w_hi", 80, [P, WS, UNIT], F32R)
        w_lo = at("w_lo", 88, [P, WS, UNIT], F32R)
        cos = at("cos", 96, [P, SEQ])
        sin = at("sin", 98, [P, SEQ])
        ident = at("ident", 100, [P, P])
        ident_r = at("ident_r", 100.5, [P, P], F32R)
        rot = at("rot", 101, [P, P])
        masks_r = at("masks_r", 101.5, [P, 2, P], F32R)
        ones = at("ones", 102.5, [P, P])
        small = at("small", 103, [P, 512])
        D0 = 105
        bias = small[:, 0:B_END]
        nbias = small[:, 72:72 + B_END]
        cT = small[:, 144:176].rearrange("p (k v) -> p k v", v=2)
        silu_c = small[:, 176:208].rearrange("p (k v) -> p k v", v=2)
        norm_g = small[:, 208:240].rearrange("p (k v) -> p k v", v=2)
        shift = small[:, 240:272].rearrange("p (k v) -> p k v", v=2)
        scale1 = small[:, 272:304].rearrange("p (k v) -> p k v", v=2)
        b_ada = small[:, 304:368].rearrange("p (k v) -> p k v", v=2)
        qn_g = small[:, 368:368 + RT]
        kvn_g = small[:, 372:372 + RT]
        eps_c = small[:, 376:377]
        neg_max = small[:, 378:380]
        row_sum = small[:, 380:382]
        row_inv = small[:, 382:384]
        sink = small[0:1, 384:400]
        sink8 = small[0:1, 460:476]
        sumsq = small[:, 400:416]
        tok_ms = small[:, 416:420]
        tok_inv = small[:, 456:460]
        neg_raw = small[:, 420:422]
        act_scratch = small[:, 422:423]
        pair = small[0:4, 476:478]
        silu_e = small[:, 424:456].rearrange("p (k v) -> p k v", v=2)

        silu_r = at("silu_r", D0 + 102.25, [P, KT, 4], F32R)

        xT = at("xT", D0 + 22, [P, KT, TOK])
        hc_hi = at("hc_hi", D0 + 70, [P, KT, CTX], F32R)
        hc_lo = at("hc_lo", D0 + 86, [P, KT, CTX], F32R)
        sq = at("sq", D0 + 0, [P, 2, TOK])
        w_hi_third = at("w_hi_third", D0 + 14, [P, UNIT], F32R)
        w_lo_third = at("w_lo_third", D0 + 18, [P, UNIT], F32R)
        rstd = at("rstd", D0 + 6, [P, TOK])
        ada_rows = at("ada_rows", D0 + 9, [4, 2, 512])
        masks_f = at("masks_f", D0 + 13, [P, 2, P])
        ckv = at("ckv", D0 + 0, [P, RT, TOK])
        cq = at("cq", D0 + 12, [P, RT, SEQ])
        kpe_hi = at("kpe_hi", D0 + 20, [P, TOK], F32R)
        kpe_lo = at("kpe_lo", D0 + 23, [P, TOK], F32R)
        ks_f = at("ks_f", D0 + 26, [P, 2, TOK])
        vT_f = at("vT_f", D0 + 32, [P, 2, TOK])
        kraw = at("kraw", D0 + 38, [P, 2, TOK])
        krot = at("krot", D0 + 44, [P, SEQ])
        nsq_kv = at("nsq_kv", D0 + 46, [P, RT, TOK])
        nsq_q = at("nsq_q", D0 + 58, [P, RT, SEQ])
        nsum_kv = at("nsum_kv", D0 + 66, [P, TOK])
        nsum_q = at("nsum_q", D0 + 36, [P, SEQ])
        nrstd = at("nrstd", D0 + 46, [P, 2, TOK])
        q_st = at("q_st", D0 + 38, [P, GROUP, SEQ], F32R)
        k_hi2 = at("k_hi2", D0 + 46, [P, TOK], F32R)
        k_lo2 = at("k_lo2", D0 + 49, [P, TOK], F32R)
        v_st = at("v_st", D0 + 52, [P, QB + CB, P], F32R)
        spt_hi = at("spt_hi", D0 + 55, [P, 5, GROUP, P], F32R)
        spt_lo = at("spt_lo", D0 + 65, [P, 5, GROUP, P], F32R)
        sprob = at("sprob", D0 + 75, [P, 2, 5 * P + 1])
        q_hiT = at("q_hiT", D0 + 100.25, [P, SEQ], F32R)
        s_gate = at("s_gate", D0 + 82.25, [P, 2, SEQ])
        b_T = at("b_T", D0 + 86.25, [P, 2, SEQ])
        s_stage = at("s_stage", D0 + 90.25, [P, 2, SEQ], F32R)
        qf2 = at("qf2", D0 + 94.25, [P, 2, SEQ])
        s_stage_last = at("s_stage_last", D0 + 75, [P, 2, SEQ], F32R)
        gate_e = at("gate_e", D0 + 80.25, [P, SEQ])
        qt = at("qt", D0 + 98.25, [P, SEQ])
        o_low = at("o_low", D0 + 100.25, [64, SEQ])
        qn_hi = at("qn_hi", D0 + 0, [P, SEQ], F32R)
        qn_lo = at("qn_lo", D0 + 2, [P, SEQ], F32R)
        qr_st = at("qr_st", D0 + 4, [P, SEQ], F32R)
        kn_hi = at("kn_hi", D0 + 6, [P, TOK], F32R)
        kn_lo = at("kn_lo", D0 + 9, [P, TOK], F32R)
        v_hi = at("v_hi", D0 + 12, [P, QB + CB, P], F32R)
        v_lo = at("v_lo", D0 + 15, [P, QB + CB, P], F32R)
        qrf = at("qrf", D0 + 18, [64, SEQ])
        ckv_hi = at("ckv_hi", D0 + 26, [P, RT, TOK], F32R)
        ckv_lo = at("ckv_lo", D0 + 38, [P, RT, TOK], F32R)
        cq_hi = at("cq_hi", D0 + 50, [P, RT, SEQ], F32R)
        cq_lo = at("cq_lo", D0 + 58, [P, RT, SEQ], F32R)
        pt_hi = at("pt_hi", D0 + 66, [P, QB + CB, SEQ], F32R)
        pt_lo = at("pt_lo", D0 + 78, [P, QB + CB, SEQ], F32R)
        prob = at("prob", D0 + 96, [P, 2, TOK])
        a_gate = at("a_gate", D0 + 90, [P, SEQ])
        a_stage = at("a_stage", D0 + 92, [P, 2, SEQ], F32R)
        A = at("A", D0 + 0, [P, 2, 8, SEQ], F32R)
        B = at("B", D0 + 32, [P, 2, 8, SEQ], F32R)
        m_f = at("m_f", D0 + 64, [P, KT, SEQ])
        sg_a = at("sg_a", D0 + 96, [P, SEQ])
        sg_b = at("sg_b", D0 + 98, [P, SEQ])
        gate_row = at("gate_row", D0 + 100, [2, 512])
        g_w = at("g_w", 96, [P, 512])
        g_hi = at("g_hi", 98, [P, 512], F32R)
        g_lo = at("g_lo", 100, [P, 512], F32R)
        y = at("y", D0 + 0, [P, QB, D])
        gate_bc = at("gate_bc", D0 + 32, [P, D])
        fin_g = at("fin_g", D0 + 40, [P, D])
        w_last_hi = at("w_last_hi", D0 + 64, [P, 4, UNIT], F32R)
        w_last_lo = at("w_last_lo", D0 + 80, [P, 4, UNIT], F32R)
        gate_rows = at("gate_rows", D0 + 48, [2, D])
        y_add = at("y_add", D0 + 56, [P, QB, 512])
        y_sq = at("y_sq", D0 + 96, [P, 512])

        spill_a = nc.dram_tensor("spill_a", [8, P, 2, SEQ], F32, kind="Internal").ap()
        spill_b = nc.dram_tensor("spill_b", [8, P, 2, SEQ], F32, kind="Internal").ap()

        spill_gate = nc.dram_tensor("spill_gate", [4, 2, 512], F32, kind="Internal").ap()

        ps = es.enter_context(nc.psum_tensor("ps", [P, 8, 512], F32))

        def two_banks(b):
            return ps[:, b:b + 2, :].rearrange("p b n -> p (b n)")

        def sems(names):
            return [sem(n) for n in names.split()]

        raw_full = [sem(f"raw_full{s}") for s in range(RAWS)]
        w_hi_done, w_lo_done, w_used = sems("w_hi_done w_lo_done w_used")
        const_in, x_in, late_in, y_in, a_in, b_in = sems("const_in x_in late_in y_in a_in b_in")
        c_in, gate_w_in, gate_spilled, gate_rows_in = sems("c_in gate_w_in gate_spilled gate_rows_in")
        const_made, const_r, nbias_made, silu_exp, silu_step, silu_hi, silu_ready = sems(
            "const_made const_r nbias_made silu_exp silu_step silu_hi silu_ready")
        ada_row_ready, ada_col_ready, ada_col_out, scale_made = sems("ada_row_ready ada_col_ready ada_col_out scale_made")
        sq_made, sq_added, x_root, x_rstd, x_normed = sems("sq_made sq_added x_root x_rstd x_normed")
        h_made, h_hi_done, h_ready = sems("h_made h_hi_done h_ready")
        z_bank_free, z_rest_out, k_rot_ready, k_step, k_roped = sems("z_bank_free z_rest_out k_rot_ready k_step k_roped")
        kpe_hi_done, kpe_lo_done, v_T_ready, v_T_out = sems("kpe_hi_done kpe_lo_done v_T_ready v_T_out")
        n_added = sem("rank_added")
        n_sq, n_sum, n_root, n_rstd, n_scaled, n_hi, n_lo = sems("rank_squared rank_summed rank_root rank_rstd rank_scaled rank_hi rank_lo")
        swa_q_out, swa_q_rotated, swa_q_step, swa_q_mixed, swa_q_hi, swa_q_lo = sems(
            "swa_q_out swa_q_rotated swa_q_step swa_q_mixed swa_q_hi swa_q_lo")
        swa_k_hi, swa_k_lo, swa_v_hi, swa_v_lo = sems("swa_k_hi swa_k_lo swa_v_hi swa_v_lo")
        swa_s, swa_max, swa_negmax, swa_exp, swa_inv, swa_prob = sems("swa_scores swa_max swa_negmax swa_exp swa_inv swa_prob")
        swa_pT, swa_pT_hi, swa_pT_lo, swa_out, swa_out_low, swa_out_free = sems(
            "swa_probT swa_probT_hi swa_probT_lo swa_out swa_out_low swa_out_free")
        swa_gate_z, swa_gate_exp, swa_gate_step, swa_gated, swa_gated_hi, swa_gated_lo, swa_spilled = sems(
            "swa_gate_z swa_gate_exp swa_gate_step swa_gated swa_gated_hi swa_gated_lo swa_spilled")
        swa_last_spilled, mla_v_proj, mla_qr_proj = sem("swa_last_spilled"), sem("mla_v_proj"), sem("mla_qr_proj")
        mla_qk_hi, mla_qk_lo, mla_qr_out, mla_q_rotated, mla_q_step, mla_q_mixed, mla_qr_hi, mla_qr_lo = sems(
            "mla_qk_hi mla_qk_lo mla_qr_out mla_q_rotated mla_q_step mla_q_mixed mla_qr_hi mla_qr_lo")
        mla_v_out, mla_v_T, mla_v_hi, mla_v_lo = sems("mla_v_out mla_v_T mla_v_hi mla_v_lo")
        mla_s, mla_max, mla_negmax, mla_exp, mla_inv, mla_prob = sems("mla_scores mla_max mla_negmax mla_exp mla_inv mla_prob")
        mla_pT, mla_pT_hi, mla_pT_lo, mla_out = sems("mla_probT mla_probT_hi mla_probT_lo mla_out")
        mla_gate_z, mla_gate_exp, mla_gate_step, mla_free, mla_gated_hi, mla_gated_lo, mla_spilled = sems(
            "mla_gate_z mla_gate_exp mla_gate_step mla_free mla_gated_hi mla_gated_lo mla_spilled")
        mg_exp, mg_step, mg_mixed, mg_free = sems("merge_exp merge_step merge_mixed merge_free")
        g_hi_done, g_lo_done, g_used = sems("gate_w_hi_done gate_w_lo_done gate_w_used")
        m_hi_done, m_ready, gate_row_ready, gate_bc_sum, gate_ready = sems("m_hi_done m_ready gate_row_ready gate_bc_sum gate_ready")
        out_done = sem("out_done")
        o_free, o_added, o_squared, o_ms, o_root, o_inv, o_final, stored = sems(
            "out_free out_added out_squared out_ms out_root out_inv out_final stored")


        def vT_of(g):
            return vT_f[:, g // 2, :].rearrange("p (k n) -> p k n", n=P)[:, :, 64 * (g % 2):64 * (g % 2) + 64]

        def key_blocks(b):
            return list(range(max(b - 1, 0), min(b + 1, QB - 1) + 1)) + list(range(QB, QB + CB))

        def w_parts(u):
            if u >= U_LAST:
                return w_last_hi[:, u - U_LAST, :], w_last_lo[:, u - U_LAST, :]
            w = w_slot(u)[0]
            return (w_hi_third[:, :], w_lo_third[:, :]) if w == 2 else (w_hi[:, w, :], w_lo[:, w, :])

        def z_out(t):
            ctx = {0: ps[:, 4, 0:CTX], 2: ps[:, 7, 0:CTX]}.get(t % 4)
            return ps[:, (3, 5, 6, 0, 3, 5, 6, 1)[t], :], ctx

        block = es.enter_context(nc.Block())

        @block.sync
        def _(sp):
            sp.dma_start(cT, cT_d).then_inc(c_in, 16)
            for u in range(RAWS):
                sp.dma_start(raw[:, u, :], stream_d[u]).then_inc(raw_full[u], 16)
            consts = [(pair, pair_d), (b_ada, b_adaT_d), (norm_g, norm_gT_d), (bias, biasT_d), (qn_g, qn_gT_d),
                      (kvn_g, kvn_gT_d), (sink, sink_d), (ident[:, :], ident_d), (rot[:, :], rot_d),
                      (masks_f[:, :, :], masks_d), (cos[:, :], cos_d), (sin[:, :], sin_d)]
            for dst, src in consts:
                sp.dma_start(dst, src).then_inc(const_in, 16)
            def load(u, s):
                sp.wait_ge(w_lo_done, u - (RAWS - 1))
                sp.dma_start(raw[:, s, :], (stream_d[u] if isinstance(u, int) else stream_d[bass.ds(u, 1)].rearrange("u p n -> (u p) n"))).then_inc(raw_full[s], 16)

            def spill(dst, stage, hi_done, lo_done, n, spilled):
                sp.wait_ge(hi_done, n)
                sp.wait_ge(lo_done, n)
                sp.dma_start(dst.rearrange("t p v n -> (t p) v n"), stage.bitcast(F32)).then_inc(spilled, 16)

            for u in range(RAWS, 12):
                load(u, u % RAWS)
                if u % 2 == 0:
                    k = 2 * (u - RAWS)
                    sp.dma_start(xT[:, k:k + 4, :], xT_d[:, k:k + 4, :]).then_inc(x_in, 16)
            n_loop = (U_SWA + AHEAD) // RAWS
            with sp.Fori(3, n_loop) as r:
                for s in range(RAWS):
                    load(r * RAWS + s, s)
            for u in range(n_loop * RAWS, U_SWA + AHEAD):
                load(u, u % RAWS)
            for g in range(KV_GROUPS):
                for u in range(U_SWA + 8 * g + AHEAD, min(U_SWA + 8 * g + 8, U_MLA) + AHEAD):
                    load(u, u % RAWS)
                for n in (2 * g + 1, 2 * g + 2):
                    stage, spilled = (s_stage_last, swa_last_spilled) if n == 8 else (s_stage, swa_spilled)
                    spill(spill_b[n - 1:n], stage[:, :, :], swa_gated_hi, swa_gated_lo, n, spilled)
            def head_loads(h, cs):
                for c in cs:
                    load(U_MLA + AHEAD + c + h * 4, (U_MLA + AHEAD + c) % RAWS)

            with sp.Fori(0, MLA_HEADS - 1) as h:
                head_loads(h, range(4))
                spill(spill_a[bass.ds(h, 1)], a_stage[:, :, :], mla_gated_hi, mla_gated_lo, h + 1, mla_spilled)
            head_loads(MLA_HEADS - 1, range(3))
            sp.wait_ge(swa_spilled, 8 * 16)
            sp.wait_ge(swa_last_spilled, 16)
            sp.wait_ge(w_used, U_MG - 2)
            for v in range(2):
                sp.dma_start(B[:, v, :, :].bitcast(F32), spill_b[:, :, v, :].rearrange("t p n -> p t n")).then_inc(b_in, 16)
            head_loads(MLA_HEADS - 1, [3])
            spill(spill_a[MLA_HEADS - 1:MLA_HEADS], a_stage[:, :, :], mla_gated_hi, mla_gated_lo, MLA_HEADS, mla_spilled)
            sp.wait_ge(mla_spilled, 8 * 16)
            sp.wait_ge(mla_out, MLA_HEADS)

            def merge_loads(r):
                for j in range(4):
                    for i in range(6):
                        if i < 4:
                            n = r * 16 + (4 * j + i)
                            sp.wait_ge(g_lo_done, n + 1)
                            sp.dma_start(g_w[:, :], gate_w_d[n] if isinstance(n, int) else
                                         gate_w_d[bass.ds(n, 1)].rearrange("u p n -> (u p) n")).then_inc(gate_w_in, 16)
                        c = AHEAD + 6 * j + i
                        load(U_MG + c + r * 24, (U_MG + c) % RAWS)
                        if isinstance(r, int) and j == 0 and i < 4:
                            if i == 3:
                                sp.wait_ge(mla_spilled, 9 * 16)
                            for t in (2 * i, 2 * i + 1):
                                sp.dma_start(A[:, :, t, :].bitcast(F32), spill_a[t]).then_inc(a_in, 16)
                sp.wait_ge(gate_row_ready, r + 2)
                sp.dma_start(spill_gate[r] if isinstance(r, int) else spill_gate[bass.ds(r, 1)].rearrange("c v n -> (c v) n"),
                             gate_row[:, :]).then_inc(gate_spilled, 16)

            merge_loads(0)
            with sp.Fori(1, 4) as r:
                merge_loads(r)
            sp.wait_ge(w_used, U_OUT - 1)
            sp.wait_ge(gate_spilled, 5 * 16)
            sp.dma_start(gate_rows[:, :].rearrange("v (c n) -> v c n", n=512), spill_gate.rearrange("c v n -> v c n")).then_inc(gate_rows_in, 16)
            sp.dma_start(gate_bc[:, :], b_gate_d).then_inc(late_in, 16)
            sp.dma_start(fin_g[:, :], final_g_d).then_inc(late_in, 16)
            sp.wait_ge(w_used, U_OUT)
            sp.dma_start(y[:, :, :], x_d.rearrange("(t p) d -> p t d", p=P)).then_inc(y_in, 16)
            with sp.Fori(0, (U_END - U_OUT - AHEAD) // RAWS) as r:
                for c in range(RAWS):
                    load(U_OUT + AHEAD + r * RAWS + c, (U_OUT + AHEAD + c) % RAWS)
            for u in range(U_OUT + AHEAD + (U_END - U_OUT - AHEAD) // RAWS * RAWS, U_END):
                load(u, u % RAWS)
            for t in range(QB):
                for half in range(2):
                    sp.wait_ge(o_final, 2 * t + half + 1)
                    c = slice(half * D // 2, (half + 1) * D // 2)
                    sp.dma_start(out_d[t * P:(t + 1) * P, c], y[:, t, c]).then_inc(stored, 16)
            sp.wait_ge(stored, 2 * QB * 16)

        @block.gpsimd
        def _(g):
            def split_lo(u, s, w):
                g.wait_ge(w_hi_done, u + 1)
                g.tensor_tensor(w_lo[:, w, :], raw[:, s, :], w_hi[:, w, :].bitcast(F32), ALU.subtract).then_inc(w_lo_done, 1)

            g.wait_ge(x_rstd, 1)
            for i in range(4):
                for k in range(4 * i, 4 * i + 4):
                    g.tensor_tensor(xT[:, k, :], xT[:, k, :], rstd[:, :], ALU.mult).then_inc(x_normed, 1)
                g.wait_ge(scale_made, i + 1)
                for k in range(4 * i, 4 * i + 4):
                    g.wait_ge(x_normed, k + 1)
                    for v, c in ((0, slice(0, SEQ)), (1, slice(SEQ, TOK))):
                        ins = g.tensor_scalar(xT[:, k, c], xT[:, k, c], scale1[:, k, v:v + 1], shift[:, k, v:v + 1], ALU.mult, ALU.add)
                    ins.then_inc(h_made, 1)

            g.wait_ge(w_lo_done, U_Z)
            with g.Fori(U_Z // RAWS, U_LAST // RAWS) as r:
                for s in range(RAWS):
                    split_lo(r * RAWS + s, s, s % WS)
            for u in range(U_LAST // RAWS * RAWS, U_LAST):
                split_lo(u, u % RAWS, u % WS)
            g.wait_ge(m_ready, KT)
            for u in range(U_LAST, U_END):
                g.wait_ge(w_hi_done, u + 1)
                hi, lo = w_parts(u)
                g.tensor_tensor(lo, raw[:, u % RAWS, :], hi.bitcast(F32), ALU.subtract).then_inc(w_lo_done, 1)

        @block.tensor
        def _(pe):
            mm = nc.tensor.matmul
            PASS = ((w_hi, 0), (w_hi, 1), (w_lo, 0))

            def ada_unit(u, a, bank):
                pe.wait_ge(w_lo_done, u + 1)
                for half in range(2):
                    for lo, wt in enumerate(w_parts(u)):
                        ins = mm(ps[0:4, bank, :], silu_r[:, 2 * a + half, :], wt[:, half * 512:half * 512 + 512],
                                 start=a + half + lo == 0, stop=a == 7 and half + lo == 2)
                ins.then_inc(w_used, 1)

            def columns(n):
                pe.wait_ge(ada_row_ready, n + 1)
                if n:
                    pe.wait_ge(ada_col_out, n)
                for f in range(4):
                    ins = mm(ps[:, 2, 2 * f:2 * f + 2], ada_rows[0:4, n % 2, f * P:f * P + P], pair, start=True, stop=True)
                ins.then_inc(ada_col_ready, 1)

            def proj(w, kts, lat, ctx, k0=0, parts=None):
                for k in kts:
                    kk = k - k0
                    for n, (wt, lo) in enumerate(PASS):
                        wk = (parts[wt is w_lo] if parts else wt[:, w, :])[:, kk * P:kk * P + P]
                        st, sp_ = k == 0 and n == 0, k == KT - 1 and n == 2
                        ins = mm(lat, wk, (h_lo if lo else h_hi)[:, k, :], start=st, stop=sp_)
                        if ctx is not None:
                            ins = mm(ctx, wk, (hc_lo if lo else hc_hi)[:, k, :], start=st, stop=sp_)
                return ins

            def proj_tile(u, par, lat, ctx):
                for half in range(2):
                    pe.wait_ge(w_lo_done, u + half + 1)
                    proj((par + half) % WS, range(half * 8, half * 8 + 8), lat, ctx, half * 8).then_inc(w_used, 1)

            pe.wait_ge(silu_ready, 1)
            for n in range(CHUNKS):
                if n >= 2:
                    pe.wait_ge(ada_row_ready, n - 1)
                for a in range(8):
                    u = chunk_unit(n) + a
                    ada_unit(u, a, n % 2)
                    if n and a == 1:
                        if n == 1:
                            pe.wait_ge(const_in, 12 * 16)
                        columns(n - 1)
                    if SQ0 <= u < SQ0 + KT:
                        k = u - SQ0
                        if k == 0:
                            pe.wait_ge(const_made, 1)
                        pe.wait_ge(sq_made, k + 1)
                        mm(ps[:, 6, :], ones[:, :], sq[:, k % 2, 0:SEQ], start=k == 0, stop=k == KT - 1)
                        mm(ps[:, 7, 0:CTX], ones[:, :], sq[:, k % 2, SEQ:TOK], start=k == 0, stop=k == KT - 1).then_inc(sq_added, 1)
                i = n - (CHUNKS - EARLY)
                if i >= 0:
                    u = early_unit(i)
                    pe.wait_ge(w_lo_done, u + 1)
                    if i == EARLY - 1:
                        pe.wait_ge(ada_row_ready, CHUNKS - 1)
                    for k in range(8):
                        if i == 0:
                            pe.wait_ge(h_ready, k + 1)
                        if i == EARLY - 1 and k == 3:
                            columns(n)
                        ins = proj(0, [k], *z_out(i), 0, w_parts(u))
                    ins.then_inc(w_used, 1)

            for t in range(EARLY):
                pe.wait_ge(w_lo_done, U_S + t + 1)
                for k in range(8, KT):
                    if t == 0:
                        pe.wait_ge(h_ready, k + 1)
                    ins = proj(t % WS, [k], *z_out(t), 8)
                ins.then_inc(w_used, 1)
            for t in range(EARLY, 8):
                if t % 2 == 0:
                    pe.wait_ge(z_bank_free, 2 if t == 4 else 5)
                proj_tile(U_Z + 2 * (t - EARLY), 0, *z_out(t))

            def after_tile(t):
                pe.wait_ge(z_rest_out, t + 1)
                if t < 3:
                    m = 64 if t == 0 else P
                    if t >= 1:
                        pe.wait_ge(k_roped, t)
                    mm(ps[:, 4, :], rot[0:m, :], kraw[0:m, t % 2, 0:SEQ], start=True, stop=True).then_inc(k_rot_ready, 1)
                else:
                    if t == 4:
                        pe.wait_ge(v_T_out, 1)
                    for k in range(QB + CB):
                        ins = nc.tensor.transpose(two_banks(5)[:, k * P:k * P + P], kraw[:, t % 2, k * P:k * P + P], ident[:, :])
                    ins.then_inc(v_T_ready, 1)

            for t in range(5):
                b = t % 2
                if t >= 2:
                    pe.wait_ge(z_rest_out, t - 1)
                proj_tile(U_REST + 2 * t, 0, ps[:, b, :], ps[:, 2 + b, 0:CTX])
                if t == 0:
                    pe.wait_ge(z_bank_free, 3 * RT)
                if t == 3:
                    pe.wait_ge(n_added, 2)
                    mm(ps[:, 5, :], ones[:, :], nsum_kv[:, 0:SEQ], start=True, stop=True)
                    mm(ps[:, 6, 0:CTX], ones[:, :], nsum_kv[:, SEQ:TOK], start=True, stop=True)
                    mm(ps[:, 7, :], ones[:, :], nsum_q[:, :], start=True, stop=True).then_inc(n_sum, 1)
                if t == 4:
                    pe.wait_ge(n_root, 3)
                if t >= 1:
                    after_tile(t - 1)
            proj_tile(U_Q, 0, ps[:, 7, :], None)
            after_tile(4)
            pe.wait_ge(v_T_out, 2)
            pe.wait_ge(k_roped, 3)
            for j in range(2):
                pe.wait_ge(w_lo_done, U_Q + 2 + j + 1)
                proj(j, range(8 * j, 8 * j + 8), ps[:, 4, :], None, 8 * j).then_inc(w_used, 1)
                pe.wait_ge(swa_q_out, j + 1)
                mm(ps[:, 5 + j, :], rot[:, :], qf2[:, j, :], start=True, stop=True).then_inc(swa_q_rotated, 1)

            def swa_scores(g, s):
                b, n = s // GROUP, s % GROUP
                sb = two_banks(2 * (s % 2))
                lo, hi = max(b - 1, 0), min(b + 1, QB - 1)
                wn = (hi - lo + 1) * P
                if s >= 2:
                    pe.wait_ge(swa_exp, g * 16 + s - 1)
                elif s == 0:
                    pe.wait_ge(swa_q_lo, g * 4 + 2)
                    pe.wait_ge(swa_k_lo, g * 3 + 2)
                if s == GROUP:
                    pe.wait_ge(swa_k_lo, g * 3 + 3)
                if s == 3 * GROUP:
                    pe.wait_ge(swa_q_lo, g * 4 + 4)
                q = q_st[:, n, b * P:b * P + P]
                mm(sb[:, 512 - wn:512], q, k_hi2[:, lo * P:hi * P + P], start=True, stop=False)
                mm(sb[:, 512 - wn:512], q, k_lo2[:, lo * P:hi * P + P], start=False, stop=False)
                if b > 0:
                    mm(sb[:, 512 - wn:512 - wn + P], ident_r[:, :], masks_r[:, 0, :], start=False, stop=b == QB - 1)
                if b < QB - 1:
                    mm(sb[:, 384:512], ident_r[:, :], masks_r[:, 1, :], start=False, stop=True)
                mm(sb[:, 512:768], q, k_hi2[:, SEQ:TOK], start=True, stop=False)
                mm(sb[:, 512:768], q, k_lo2[:, SEQ:TOK], start=False, stop=True)
                head = GROUP * g + n
                mm(sb[:, 768:769], ones[0:1, :], sink8[0:1, head:head + 1], start=True, stop=True).then_inc(swa_s, 1)

            def swa_filler(g, s):
                shares = 2 if g < KV_GROUPS - 1 else 4
                f, part = s // shares, s % shares
                u = U_SWA + 8 * g + f
                if part == 0:
                    pe.wait_ge(w_lo_done, u + 1)
                    if f in (2, 4) and g < KV_GROUPS - 1:
                        pe.wait_ge(swa_q_out, 2 * (g + 1) + f // 2)
                    elif f % 2 == 0 and g + f:
                        pe.wait_ge(swa_gate_z, 2 * g + (1 if f else 0))
                    elif f == 0:
                        pe.wait_ge(swa_q_out, 1)
                ks = range((f % 2) * 8 + part * (8 // shares), (f % 2) * 8 + (part + 1) * (8 // shares))
                ins = proj(u % WS, ks, ps[:, 7, :], None, (f % 2) * 8)
                if part == shares - 1:
                    ins.then_inc(w_used, 1)

            def swa_transpose(g, s):
                tb = two_banks(4)
                pe.wait_ge(swa_prob, g * 16 + s + 1)
                if g * 16 + s >= 1:
                    pe.wait_ge(swa_pT_lo, g * 16 + s)
                for k in range(len(key_blocks(s // GROUP))):
                    ins = nc.tensor.transpose(tb[:, k * P:k * P + P], sprob[:, s % 2, k * P:k * P + P], ident[:, :])
                ins.then_inc(swa_pT, 1)

            def swa_values(g, b):
                blocks = key_blocks(b)
                pe.wait_ge(swa_v_lo, g + 1)
                pe.wait_ge(swa_out_free, g * 4 + b + 1)
                for half, pt in enumerate((spt_hi, spt_lo)):
                    pe.wait_ge((swa_pT_hi, swa_pT_lo)[half], g * 16 + 4 * b + 4)
                    for k, kb in enumerate(blocks):
                        ins = mm(ps[:, 6, :], v_st[:, kb, :], pt[:, k, :, :].rearrange("p g n -> p (g n)"),
                                 start=half == 0 and k == 0, stop=half == 1 and k == len(blocks) - 1)
                ins.then_inc(swa_out, 1)

            pe.wait_ge(const_r, 2)
            swa_scores(0, 0)
            for g in range(KV_GROUPS):
                last = g == KV_GROUPS - 1
                for s in range(16):
                    if s < 15:
                        swa_scores(g, s + 1)
                    swa_filler(g, s)
                    if s in ROTATE and not last:
                        j = ROTATE.index(s)
                        pe.wait_ge(swa_q_out, 2 * g + 2 + j + 1)
                        pe.wait_ge(swa_out_free, g * 4 + s // 4 + 1)
                        mm(ps[:, 6, :], rot[:, :], qf2[:, j, :], start=True, stop=True).then_inc(swa_q_rotated, 1)
                    if s % GROUP == 0 and g + s:
                        blk = g * QB + s // GROUP - 1
                        if blk % QB in (1, 2) and not last:
                            pe.wait_ge(swa_q_mixed, 2 * g + 2 + blk % QB)
                        swa_values(blk // QB, blk % QB)
                    swa_transpose(g, s)
                    if s == 15 and not last:
                        swa_scores(g + 1, 0)
            swa_values(KV_GROUPS - 1, QB - 1)

            def mla_proj(u, w, passes):
                for out, c0, mhi, mlo in passes:
                    for k in range(RT):
                        for n, (wt, lo) in enumerate(PASS):
                            ins = mm(out, wt[:, w, k * 256 + c0:k * 256 + c0 + P], (mlo if lo else mhi)(k),
                                     start=k == 0 and n == 0, stop=k == RT - 1 and n == 2)
                return ins

            def mla_scores(h, s):
                sb = two_banks(2 * (s % 2))
                if s >= 2:
                    pe.wait_ge(mla_exp, h * QB + (s - 1))
                q = slice(s * P, s * P + P)
                parts = ((qn_hi, kn_hi), (qn_lo, kn_hi), (qn_hi, kn_lo), (qr_st, kpe_hi), (qr_st, kpe_lo))
                for c0, c1 in ((0, SEQ), (SEQ, TOK)):
                    for n, (qq, kk) in enumerate(parts):
                        ins = mm(sb[:, c0:c1], qq[:, q], kk[:, c0:c1], start=n == 0, stop=n == len(parts) - 1)
                ins.then_inc(mla_s, 1)

            def mla_transpose(h, s):
                tb = two_banks(4)
                pe.wait_ge(mla_prob, h * QB + (s + 1))
                if s >= 1:
                    pe.wait_ge(mla_pT_lo, h * QB + s)
                for k in range(QB + CB):
                    ins = nc.tensor.transpose(tb[:, k * P:k * P + P], prob[:, s % 2, k * P:k * P + P], ident[:, :])
                ins.then_inc(mla_pT, 1)

            lat, cx = slice(0, SEQ), slice(SEQ, TOK)
            pe.wait_ge(n_lo, RT)
            pe.wait_ge(swa_gate_z, 8)
            with pe.Fori(0, MLA_HEADS) as h:
                u0 = U_MLA

                def kv_proj(c0, b):
                    return mla_proj(0, 0, [
                        (ps[:, b, :], c0, lambda k: ckv_hi[:, k, lat], lambda k: ckv_lo[:, k, lat]),
                        (ps[:, b + 1, 0:CTX], c0, lambda k: ckv_hi[:, k, cx], lambda k: ckv_lo[:, k, cx])])

                def q_proj(c0, b):
                    return mla_proj(0, 1, [(ps[:, b, :], c0, lambda k: cq_hi[:, k, :], lambda k: cq_lo[:, k, :])])

                def filler(k0, k1):
                    if k0 % 8 == 0:
                        pe.wait_ge(w_lo_done, h * 4 + (u0 + 3 + k0 // 8))
                    ins = proj(k0 // 8, range(k0, k1), ps[:, 7, :], None, k0 // 8 * 8)
                    if k1 % 8 == 0:
                        ins.then_inc(w_used, 1)

                def values(half):
                    cols = slice(half * 256, half * 256 + 256)
                    for p, (vv, pt) in enumerate(((v_hi, pt_hi), (v_lo, pt_hi), (v_hi, pt_lo))):
                        if p != 1:
                            pe.wait_ge(mla_pT_lo if p else mla_pT_hi, h * QB + (2 * half + 2))
                        for k in range(QB + CB):
                            ins = mm(ps[:, 6, cols], vv[:, k, :], pt[:, k, cols], start=p == 0 and k == 0,
                                     stop=p == 2 and k == QB + CB - 1)
                    return ins

                pe.wait_ge(w_lo_done, h * 4 + (u0 + 1))
                kv_proj(P, 2).then_inc(mla_v_proj, 1)
                kv_proj(0, 0).then_inc(w_used, 1)
                pe.wait_ge(mla_v_out, h + 1)
                for k in range(QB + CB):
                    ins = nc.tensor.transpose(two_banks(4)[:, k * P:k * P + P], prob[:, 0, k * P:k * P + P], ident[:, :])
                ins.then_inc(mla_v_T, 1)
                pe.wait_ge(mla_free, h + 1)
                pe.wait_ge(swa_out_free, 17)
                pe.wait_ge(n_lo, 2 * RT)
                pe.wait_ge(w_lo_done, h * 4 + (u0 + 2))
                q_proj(P, 6).then_inc(mla_qr_proj, 1)
                pe.wait_ge(mla_v_lo, h + 1)
                q_proj(0, 4).then_inc(w_used, 1)
                pe.wait_ge(mla_qr_out, h + 1)
                mm(ps[:, 5, :], rot[0:64, :], qrf[:, :], start=True, stop=True).then_inc(mla_q_rotated, 1)
                filler(0, 4)
                pe.wait_ge(mla_qk_lo, h * 2 + 2)
                pe.wait_ge(mla_qr_lo, h + 1)
                mla_scores(h, 0)
                for s in range(QB - 1):
                    mla_scores(h, s + 1)
                    filler(*((4, 8), (8, 12), (12, 14))[s])
                    mla_transpose(h, s)
                values(0)
                mla_transpose(h, QB - 1)
                filler(14, 16)
                values(1).then_inc(mla_out, 1)

            with pe.Fori(0, 4) as r:
                pe.wait_ge(gate_row_ready, r + 1)
                for j in range(4):
                    u0 = U_MG + 6 * j
                    b0 = 4 * (j % 2)

                    def gate_tile(i):
                        k = 4 * j + i
                        pe.wait_ge(g_lo_done, r * 16 + (k + 2))
                        mm(ps[0:2, 6, :], silu_r[:, k, 0:2], g_hi[:, :], start=k == 0, stop=False)
                        mm(ps[0:2, 6, :], silu_r[:, k, 0:2], g_lo[:, :], start=False, stop=k == KT - 1).then_inc(g_used, 1)

                    pe.wait_ge(mg_free, r * 4 + (j + 1))
                    for i in range(4):
                        pe.wait_ge(w_lo_done, r * 24 + (u0 + i + 1))
                        proj(i % 2, range(i % 2 * 8, i % 2 * 8 + 8), ps[:, b0 + i // 2, :], None, i % 2 * 8).then_inc(w_used, 1)
                        if i == 1:
                            pe.wait_ge(mla_free, MLA_HEADS + 1)
                        if i:
                            gate_tile(i - 1)
                    pe.wait_ge(mg_free, r * 4 + (j + 2))
                    for i, x in enumerate((B, A)):
                        pe.wait_ge((b_in, a_in)[i], (32, 8 * 16)[i])
                        pe.wait_ge(w_lo_done, r * 24 + (u0 + 4 + i + 1))
                        for k in range(8):
                            for n, (wt, lo) in enumerate(PASS):
                                ins = mm(ps[:, 3 - i, :], wt[:, i, k * P:k * P + P], x[:, lo, k, :],
                                         start=k == 0 and n == 0, stop=k == 7 and n == 2)
                        ins.then_inc(w_used, 1)
                        if i == 0:
                            gate_tile(3)

            def gate_onto_partitions():
                pe.wait_ge(gate_rows_in, 16)
                for c in range(4):
                    mm(ps[:, 4 + c, :], ones[0:2, :], gate_rows[:, c * 512:c * 512 + 512], start=True, stop=True).then_inc(gate_bc_sum, 1)

            def out_products(n, c, t, hi, lo):
                for half in range(2):
                    k, tt, mv = 2 * c + half, slice(t * P, t * P + P), slice(half * 512, half * 512 + 512)
                    o = ps[:, 4 * (n % 2) + t, :]
                    mm(o, m_hi[:, k, tt], hi[:, mv], start=k == 0, stop=False)
                    mm(o, m_lo[:, k, tt], hi[:, mv], start=False, stop=False)
                    ins = mm(o, m_hi[:, k, tt], lo[:, mv], start=False, stop=k == KT - 1)
                return ins

            pe.wait_ge(mg_free, KT + 2)
            for n in range(4):
                if n == 1:
                    pe.wait_ge(gate_ready, 4)
                for c in range(4 if n == 3 else 8):
                    u = U_OUT + 8 * n + c
                    pe.wait_ge(w_lo_done, u + 1)
                    if n == 0:
                        pe.wait_ge(m_ready, 2 * c + 2)
                    for t in range(QB):
                        if c == 0 and n >= 2:
                            pe.wait_ge(o_free, (n - 2) * QB + t + 1)
                        ins = out_products(n, c, t, *w_parts(u))
                        if c == 7 and t < QB - 1:
                            ins.then_inc(out_done, 1)
                    ins.then_inc(w_used, 1)
                    if n == 0 and c == 0:
                        gate_onto_partitions()
            for t in range(QB):
                for c in range(4, 8):
                    if t == 0:
                        pe.wait_ge(w_lo_done, U_LAST + c - 4 + 1)
                    ins = out_products(3, c, t, *w_parts(U_LAST + c - 4))
                ins.then_inc(out_done, 1)

        @block.scalar
        def _(act):
            def split_hi(c, off=0, per=0):
                if per == 0:
                    act.wait_ge(raw_full[c % RAWS], (c // RAWS + 1) * 16)
                    if w_slot(c)[1] > 0:
                        act.wait_ge(w_used, w_slot(c)[1])
                    act.copy(w_parts(c)[0], raw[:, c % RAWS, :]).then_inc(w_hi_done, 1)
                else:
                    act.wait_ge(raw_full[c % RAWS], (off * (per // RAWS) + (c // RAWS + 1)) * 16)
                    act.wait_ge(w_used, off * per + (c - 1))
                    act.copy(w_hi[:, c % WS, :], raw[:, c % RAWS, :]).then_inc(w_hi_done, 1)

            def biased(dst, src, b):
                return act.activation(dst, src, ACT.Identity, bias=b)

            act.wait_ge(c_in, 16)
            act.activation(silu_e, cT, ACT.Exp, scale=-1.0).then_inc(silu_exp, 1)
            split_hi(0)
            act.wait_ge(silu_step, 3)
            silu_parts = silu_r[:, :, :].rearrange("p k (v l) -> p k v l", l=2)
            act.copy(silu_parts[:, :, :, 0], silu_c).then_inc(silu_hi, 1)

            def row_out(n):
                act.wait_ge(w_used, chunk_unit(n) + 8)
                if n >= 2:
                    act.wait_ge(ada_col_ready, n - 1)
                act.copy(ada_rows[:, n % 2, :], ps[0:4, n % 2, :]).then_inc(ada_row_ready, 1)

            def h_hi_of(k):
                act.wait_ge(h_made, k + 1)
                act.copy(h_hi[:, k, :], xT[:, k, 0:SEQ])
                act.copy(hc_hi[:, k, :], xT[:, k, SEQ:TOK]).then_inc(h_hi_done, 1)

            row_after = {chunk_unit(n) + 8: n for n in range(CHUNKS)}
            for u in range(1, U_S + 1):
                split_hi(u)
                if u in row_after:
                    row_out(row_after[u])
                if SQ0 <= u < SQ0 + KT:
                    k = u - SQ0
                    act.wait_ge(x_in, (k // 4 + 1) * 16)
                    if k >= 2:
                        act.wait_ge(sq_added, k - 1)
                    act.activation(sq[:, k % 2, :], xT[:, k, :], ACT.Square).then_inc(sq_made, 1)
                if u == U_ROOT:
                    act.wait_ge(sq_added, KT)
                    act.wait_ge(const_made, 1)
                    act.activation(rstd[:, 0:SEQ], ps[:, 6, :], ACT.Sqrt, scale=1.0 / D, bias=eps_c)
                    act.activation(rstd[:, SEQ:TOK], ps[:, 7, 0:CTX], ACT.Sqrt, scale=1.0 / D, bias=eps_c).then_inc(x_root, 1)
                    act.wait_ge(const_in, 12 * 16)
                    act.copy(ident_r[:, :], ident[:, :]).then_inc(const_r, 1)
                    act.copy(masks_r[:, :, :], masks_f[:, :, :]).then_inc(const_r, 1)
                if u in H_AT:
                    h_hi_of(H_AT[u])
            h_hi_of(12)
            h_hi_of(13)
            split_hi(U_S + 1)
            h_hi_of(14)
            h_hi_of(15)

            def z_tile_out(t, used):
                lat, ctx = z_out(t)
                i = t // 2
                act.wait_ge(w_used, used)
                if t % 2:
                    biased(cq[:, i, :], lat, bias[:, t:t + 1]).then_inc(z_bank_free, 1)
                else:
                    biased(ckv[:, i, 0:SEQ], lat, bias[:, t:t + 1]).then_inc(z_bank_free, 1)
                    biased(ckv[:, i, SEQ:TOK], ctx, bias[:, t:t + 1]).then_inc(z_bank_free, 1)

            act.wait_ge(h_ready, KT)
            for t in range(EARLY):
                split_hi(U_S + t + 2)
                z_tile_out(t, U_S + t + 1)
            for t in range(EARLY, 8):
                u = U_Z + 2 * (t - EARLY)
                split_hi(u + 2)
                z_tile_out(t, u + 2)
                split_hi(u + 3)

            def rank_roots():
                act.wait_ge(n_sum, 1)
                for row, cols, src in ((0, slice(0, SEQ), ps[:, 5, :]), (0, slice(SEQ, TOK), ps[:, 6, 0:CTX]), (1, slice(0, SEQ), ps[:, 7, :])):
                    act.activation(nrstd[:, row, cols], src, ACT.Sqrt, scale=1.0 / RANK, bias=eps_c).then_inc(n_root, 1)
                act.activation(act_scratch, eps_c, ACT.Exp)

            for t in range(5):
                u = U_REST + 2 * t
                split_hi(u + 2)
                act.wait_ge(w_used, u + 2)
                if t >= 2:
                    act.wait_ge(k_roped, t - 1)
                if t == 2:
                    act.wait_ge(kpe_lo_done, 1)
                biased(kraw[:, t % 2, 0:SEQ], ps[:, t % 2, :], bias[:, 8 + t:9 + t])
                biased(kraw[:, t % 2, SEQ:TOK], ps[:, 2 + t % 2, 0:CTX], bias[:, 8 + t:9 + t]).then_inc(z_rest_out, 1)
                split_hi(u + 3)
                if t == 1:
                    act.wait_ge(k_roped, 1)
                    act.copy(kpe_hi[0:64, :], kraw[0:64, 0, :])
                    act.copy(kpe_hi[64:P, :], kraw[0:64, 0, :]).then_inc(kpe_hi_done, 1)
                if t == 3:
                    rank_roots()
                if t == 4:
                    act.wait_ge(v_T_ready, 1)
                    act.copy(vT_f[:, 0, :], two_banks(5)[:, 0:TOK]).then_inc(v_T_out, 1)
            split_hi(U_Q + 2)
            act.wait_ge(w_used, U_Q + 2)
            biased(qf2[:, 0, :], ps[:, 7, :], bias[:, B_SWA:B_SWA + 1]).then_inc(swa_q_out, 1)
            act.wait_ge(v_T_ready, 2)
            act.copy(vT_f[:, 1, :], two_banks(5)[:, 0:TOK]).then_inc(v_T_out, 1)
            split_hi(U_Q + 3)
            def swa_softmax(g, s):
                wn = P * len(key_blocks(s // GROUP)) + 1
                n = g * 16 + s
                act.wait_ge(swa_negmax, n + 1)
                if n >= 2:
                    act.wait_ge(swa_pT, n - 1)
                act.activation(sprob[:, s % 2, 0:wn], two_banks(2 * (s % 2))[:, 769 - wn:769], ACT.Exp,
                               bias=neg_max[:, s % 2:s % 2 + 1], scale=SWA_SCALE,
                               accum_out=row_sum[:, s % 2:s % 2 + 1]).then_inc(swa_exp, 1)

            def swa_keys(g, part):
                kr = ks_f[64 * (g % 2):64 * (g % 2) + 64, g // 2, K_PARTS[part]]
                act.copy(k_hi2[0:64, K_PARTS[part]], kr)
                act.copy(k_hi2[64:P, K_PARTS[part]], kr).then_inc(swa_k_hi, 1)

            def swa_queries(g, part, j):
                n, c = 4 * g + 2 * part + j, Q_PARTS[part]
                act.wait_ge(swa_q_mixed, 2 * g + j + 1)
                act.copy(q_st[0:64, 2 * j, c], qf2[0:64, j, c])
                act.copy(q_st[0:64, 2 * j + 1, c], qf2[64:P, j, c])
                if n:
                    act.wait_ge(swa_q_lo, n)
                act.copy(q_hiT[64:P, c], qf2[64:P, j, c]).then_inc(swa_q_hi, 1)

            def swa_out_low_of(blk):
                act.wait_ge(swa_out, blk + 1)
                act.copy(o_low[:, :], ps[64:P, 6, :]).then_inc(swa_out_low, 1)

            def swa_values_hi(g):
                act.copy(v_st[:, :, 0:64], vT_of(g)).then_inc(swa_v_hi, 1)

            def swa_gate_exp_of(g, j):
                act.wait_ge(swa_gate_z, 2 * g + j + 1)
                if g + j:
                    act.wait_ge(swa_gate_step, 3 * (2 * g + j))
                act.activation(gate_e[:, :], s_gate[:, j, :], ACT.Exp, scale=-1.0).then_inc(swa_gate_exp, 1)

            def swa_gated_hi_of(g, j):
                act.wait_ge(swa_gated, 2 * g + j + 1)
                act.wait_ge(swa_spilled, (2 * g + j + 1) * 16)
                act.copy(s_stage[:, 0, :], b_T[:, j, :]).then_inc(swa_gated_hi, 1)

            act.wait_ge(n_scaled, 2 * RT)
            for part in (0, 1):
                swa_keys(0, part)
            split_hi(U_Q + 4)
            swa_queries(0, 0, 0)
            act.wait_ge(w_used, U_Q + 4)
            biased(qf2[:, 1, :], ps[:, 4, :], bias[:, B_SWA + 1:B_SWA + 2]).then_inc(swa_q_out, 1)
            split_hi(U_Q + 5)
            swa_queries(0, 0, 1)
            swa_softmax(0, 0)
            swa_keys(0, 2)
            for j in range(2):
                swa_queries(0, 1, j)
            swa_values_hi(0)
            for g in range(KV_GROUPS):
                last = g == KV_GROUPS - 1
                shares = 4 if last else 2
                for s in range(16):
                    b, n = s // GROUP, s % GROUP
                    nb = len(key_blocks(b))
                    if s < 15:
                        swa_softmax(g, s + 1)
                    elif not last:
                        swa_keys(g + 1, 1)
                    if s % shares == shares - 1:
                        if s in (3, 7) and not last:
                            j = s // 4
                            act.wait_ge(w_used, U_SWA + 8 * g + 2 * j + 2)
                            if j == 0:
                                act.wait_ge(swa_q_lo, 4 * g + 4)
                            c = B_SWA + 4 * (g + 1) + j
                            biased(qf2[:, j, :], ps[:, 7, :], bias[:, c:c + 1]).then_inc(swa_q_out, 1)
                        split_hi(U_SWA + 8 * g + s // shares + 2)
                    if n == 0 and g * 4 + b >= 1:
                        swa_out_low_of(g * 4 + b - 1)
                        if s == 0:
                            swa_values_hi(g)
                    act.wait_ge(swa_pT, g * 16 + s + 1)
                    act.copy(spt_hi[:, 0:nb, n, :], two_banks(4)[:, 0:nb * P].rearrange("p (k n) -> p k n", n=P)).then_inc(swa_pT_hi, 1)
                    if s == 15 and not last:
                        swa_softmax(g + 1, 0)
                        swa_keys(g + 1, 2)
                        for j in range(2):
                            swa_queries(g + 1, 1, j)
                    if s in (13, 14) and not last:
                        if s == 13:
                            swa_keys(g + 1, 0)
                        swa_queries(g + 1, 0, s - 13)
                    if s == 1 and g:
                        swa_gated_hi_of(g - 1, 0)
                    if s == 3 and g:
                        swa_gated_hi_of(g - 1, 1)
                    if last and 4 <= s < 4 + RT:
                        act.wait_ge(swa_v_lo, KV_GROUPS)
                        act.wait_ge(swa_k_lo, 3 * KV_GROUPS)
                        act.copy(ckv_hi[:, s - 4, :], ckv[:, s - 4, :]).then_inc(n_hi, 1)
                    if s == (7 if last else 11):
                        swa_gate_exp_of(g, 0)
                    if s == 15:
                        swa_gate_exp_of(g, 1)
            swa_out_low_of(KV_GROUPS * QB - 1)
            for k in range(RT):
                act.copy(cq_hi[:, k, :], cq[:, k, :]).then_inc(n_hi, 1)
            act.wait_ge(n_lo, 2 * RT)

            def mla_softmax(h, s):
                act.wait_ge(mla_negmax, h * QB + (s + 1))
                if s >= 2:
                    act.wait_ge(mla_pT, h * QB + (s - 1))
                act.activation(prob[:, s % 2, :], two_banks(2 * (s % 2))[:, 0:TOK], ACT.Exp,
                               bias=neg_max[:, s % 2:s % 2 + 1], scale=MLA_SCALE,
                               accum_out=row_sum[:, s % 2:s % 2 + 1]).then_inc(mla_exp, 1)

            with act.Fori(0, MLA_HEADS) as h:
                u0 = U_MLA
                act.wait_ge(mla_v_proj, h + 1)
                act.copy(prob[:, 0, :], two_banks(2)[:, 0:TOK]).then_inc(mla_v_out, 1)
                act.wait_ge(w_used, h * 4 + (u0 + 1))
                act.copy(kn_hi[:, :], two_banks(0)[:, 0:TOK]).then_inc(mla_qk_hi, 1)
                act.wait_ge(mla_v_T, h + 1)
                act.copy(v_hi[:, :, :], two_banks(4)[:, 0:TOK].rearrange("p (k n) -> p k n", n=P)).then_inc(mla_v_hi, 1)
                split_hi(u0 + 2, h, 4)
                act.wait_ge(mla_qr_proj, h + 1)
                act.copy(qrf[:, :], ps[0:64, 6, :]).then_inc(mla_qr_out, 1)
                act.wait_ge(w_used, h * 4 + (u0 + 2))
                act.copy(qn_hi[:, :], ps[:, 4, :]).then_inc(mla_qk_hi, 1)
                act.wait_ge(mla_q_mixed, h + 1)
                act.copy(qr_st[0:64, :], qrf[:, :]).then_inc(mla_qr_hi, 1)
                split_hi(u0 + 3, h, 4)
                mla_softmax(h, 0)
                for s in range(QB):
                    if s < QB - 1:
                        mla_softmax(h, s + 1)
                    if s == 0:
                        split_hi(u0 + 4, h, 4)
                    if s == 0:
                        act.wait_ge(swa_last_spilled, 16)
                    act.wait_ge(mla_pT, h * QB + (s + 1))
                    act.copy(pt_hi[:, :, s * P:s * P + P], two_banks(4)[:, 0:TOK].rearrange("p (k n) -> p k n", n=P)).then_inc(mla_pT_hi, 1)
                split_hi(u0 + 5, h, 4)
                act.wait_ge(mla_gate_z, h + 1)
                act.activation(prob[:, 1, 0:SEQ], a_gate[:, :], ACT.Exp, scale=-1.0).then_inc(mla_gate_exp, 1)
                act.wait_ge(mla_free, h + 2)
                act.wait_ge(mla_spilled, (h + 1) * 16)
                act.copy(a_stage[:, 0, :], a_gate[:, :]).then_inc(mla_gated_hi, 1)

            act.wait_ge(nbias_made, 1)
            with act.Fori(0, 4) as r:
                for j in range(4):
                    u0 = U_MG + 6 * j

                    def gate_hi(i):
                        k = 4 * j + i
                        act.wait_ge(gate_w_in, (r * 16 + (k + 1)) * 16)
                        if k:
                            act.wait_ge(g_used, r * 16 + k)
                        else:
                            act.wait_ge(gate_row_ready, r + 1)
                        act.copy(g_hi[:, :], g_w[:, :]).then_inc(g_hi_done, 1)

                    gate_hi(0)
                    split_hi(u0 + 2, r, 24)
                    for i, sg in enumerate((sg_a, sg_b)):
                        act.wait_ge(w_used, r * 24 + (u0 + 2 * i + 2))
                        if i == 0:
                            act.wait_ge(mg_free, r * 4 + (j + 2))
                            act.wait_ge(mla_free, MLA_HEADS + 1)
                        else:
                            split_hi(u0 + 5, r, 24)
                        act.activation(sg[:, :], ps[:, 4 * (j % 2) + i, :], ACT.Exp, scale=-1.0,
                                       bias=nbias[:, bass.ds(r * 8 + (B_MG + 2 * j + i), 1)]).then_inc(mg_exp, 1)
                        if i == 0:
                            gate_hi(1)
                            split_hi(u0 + 3, r, 24)
                            split_hi(u0 + 4, r, 24)
                            gate_hi(2)
                        else:
                            gate_hi(3)
                    split_hi(u0 + 6, r, 24)
                    if j == 3:
                        act.wait_ge(g_used, r * 16 + 16)
                        act.wait_ge(gate_spilled, (r + 1) * 16)
                        act.copy(gate_row[:, :], ps[0:2, 6, :]).then_inc(gate_row_ready, 1)
                    split_hi(u0 + 7, r, 24)

            act.wait_ge(w_used, U_OUT)
            for k in range(KT):
                act.wait_ge(mg_free, k + 3)
                act.copy(m_hi[:, k, :], m_f[:, k, :]).then_inc(m_hi_done, 1)

            def out_square(n, t):
                act.wait_ge(o_added, n * QB + t + 1)
                if n + t:
                    act.wait_ge(o_squared, n * QB + t)
                act.activation(y_sq[:, :], y[:, t, n * 512:n * 512 + 512], ACT.Square,
                               accum_out=sumsq[:, n * QB + t:n * QB + t + 1]).then_inc(o_squared, 1)

            for n in range(4):
                for c in range(8):
                    u = U_OUT + 8 * n + c + 2
                    if u < U_END:
                        if u == U_LAST:
                            act.wait_ge(m_ready, KT)
                        split_hi(u)
                if n < 3:
                    for t in range(QB):
                        out_square(n, t)
            for t in range(QB):
                out_square(3, t)
                act.wait_ge(o_ms, t + 1)
                act.activation(tok_ms[:, t:t + 1], tok_ms[:, t:t + 1], ACT.Sqrt, scale=1.0 / D, bias=eps_c).then_inc(o_root, 1)

        @block.vector
        def _(dve):
            tt, ts, stt = dve.tensor_tensor, dve.tensor_scalar, dve.scalar_tensor_tensor

            def f(ap):
                return ap.bitcast(F32)

            dve.memset(eps_c, EPS)
            dve.memset(ones[:, :], 1.0).then_inc(const_made, 1)
            dve.memset(row_sum, 0.0).then_inc(gate_row_ready, 1)
            dve.memset(neg_max, 0.0).then_inc(swa_out_free, 1)
            dve.memset(row_inv, 0.0).then_inc(mla_free, 1)
            dve.memset(tok_ms, 0.0).then_inc(mg_free, 2)
            dve.memset(tok_inv, 0.0)
            dve.memset(sumsq, 0.0).then_inc(swa_spilled, 16)
            dve.memset(shift, 0.0).then_inc(mla_spilled, 16)
            dve.memset(scale1, 0.0).then_inc(gate_spilled, 16)
            dve.memset(neg_raw, 0.0).then_inc(g_lo_done, 1)
            dve.wait_ge(silu_exp, 1)
            ts(silu_e, silu_e, 1.0, None, ALU.add).then_inc(silu_step, 1)
            dve.wait_ge(silu_step, 1)
            dve.reciprocal(silu_e, silu_e).then_inc(silu_step, 1)
            dve.wait_ge(silu_step, 2)
            tt(silu_c, silu_e, cT, ALU.mult).then_inc(silu_step, 1)
            dve.wait_ge(silu_step, 3)
            dve.wait_ge(silu_hi, 1)
            silu_parts = silu_r[:, :, :].rearrange("p k (v l) -> p k v l", l=2)
            tt(silu_parts[:, :, :, 1], silu_c, f(silu_parts[:, :, :, 0]), ALU.subtract).then_inc(silu_ready, 1)

            def split_lo(u):
                dve.wait_ge(w_hi_done, u + 1)
                tt(w_parts(u)[1], raw[:, u % RAWS, :], f(w_parts(u)[0]), ALU.subtract).then_inc(w_lo_done, 1)

            def column_out(n):
                part, cols = n % 2, slice(4 * (n // 2), 4 * (n // 2) + 4)
                dve.wait_ge(ada_col_ready, n + 1)
                tt((shift, scale1)[part][:, cols, :], ps[:, 2, 0:8].rearrange("p (f v) -> p f v", v=2),
                   b_ada[:, KT * part + cols.start:KT * part + cols.stop, :], ALU.add).then_inc(ada_col_out, 1)
                if part:
                    dve.wait_ge(ada_col_out, n + 1)
                    stt(scale1[:, cols, :], scale1[:, cols, :], 1.0, norm_g[:, cols, :], ALU.add, ALU.mult).then_inc(scale_made, 1)

            def h_lo_of(k):
                dve.wait_ge(h_hi_done, k + 1)
                tt(h_lo[:, k, :], xT[:, k, 0:SEQ], f(h_hi[:, k, :]), ALU.subtract)
                tt(hc_lo[:, k, :], xT[:, k, SEQ:TOK], f(hc_hi[:, k, :]), ALU.subtract).then_inc(h_ready, 1)

            column_after = {chunk_unit(n + 1) + 3: n for n in range(CHUNKS - 1)}
            for u in range(U_S):
                split_lo(u)
                if u == chunk_unit(1) + 2:
                    dve.wait_ge(const_in, 12 * 16)
                    ts(nbias, bias, -1.0, None, ALU.mult)
                    ts(sink8, sink, 1.0 / SWA_SCALE, None, ALU.mult).then_inc(nbias_made, 1)
                if u in column_after:
                    column_out(column_after[u])
                if u == U_ROOT:
                    dve.wait_ge(x_root, 1)
                    dve.reciprocal(rstd[:, :], rstd[:, :]).then_inc(x_rstd, 1)
                if u in H_AT:
                    h_lo_of(H_AT[u])
            column_out(CHUNKS - 1)
            split_lo(U_S)
            for k in range(12, KT):
                h_lo_of(k)
            for u in range(U_S + 1, U_Z):
                split_lo(u)

            dve.wait_ge(z_bank_free, 3 * RT)
            for k in range(RT):
                tt(nsq_kv[:, k, :], ckv[:, k, :], ckv[:, k, :], ALU.mult).then_inc(n_sq, 1)
                tt(nsq_q[:, k, :], cq[:, k, :], cq[:, k, :], ALU.mult).then_inc(n_sq, 1)
            dve.wait_ge(n_sq, 2 * RT)
            dve.tensor_reduce(nsum_kv[:, :], nsq_kv[:, :, :].rearrange("p k n -> p n k"), AX.X, ALU.add).then_inc(n_added, 1)
            dve.tensor_reduce(nsum_q[:, :], nsq_q[:, :, :].rearrange("p k n -> p n k"), AX.X, ALU.add).then_inc(n_added, 1)
            for t in range(3):
                m = 64 if t == 0 else P
                dst = kraw[0:m, 0, 0:SEQ] if t == 0 else ks_f[:, t - 1, 0:SEQ]
                dve.wait_ge(k_rot_ready, t + 1)
                tt(krot[0:m, :], ps[0:m, 4, :], sin[0:m, :], ALU.mult).then_inc(k_step, 1)
                if t >= 1:
                    dve.tensor_copy(ks_f[:, t - 1, SEQ:TOK], kraw[:, t % 2, SEQ:TOK])
                tt(dst, kraw[0:m, t % 2, 0:SEQ], cos[0:m, :], ALU.mult).then_inc(k_step, 1)
                dve.wait_ge(k_step, 2 * t + 2)
                tt(dst, dst, krot[0:m, :], ALU.add).then_inc(k_roped, 1)
                if t == 0:
                    dve.wait_ge(kpe_hi_done, 1)
                    dve.wait_ge(k_roped, 1)
                    tt(kpe_lo[0:64, :], kraw[0:64, 0, :], f(kpe_hi[0:64, :]), ALU.subtract)
                    tt(kpe_lo[64:P, :], kraw[0:64, 0, :], f(kpe_hi[0:64, :]), ALU.subtract).then_inc(kpe_lo_done, 1)
            dve.wait_ge(n_root, 3)
            dve.reciprocal(nrstd[:, 0, :], nrstd[:, 0, :]).then_inc(n_rstd, 1)
            dve.reciprocal(nrstd[:, 1, 0:SEQ], nrstd[:, 1, 0:SEQ]).then_inc(n_rstd, 1)
            dve.wait_ge(n_rstd, 2)
            for k in range(RT):
                stt(ckv[:, k, :], ckv[:, k, :], kvn_g[:, k:k + 1], nrstd[:, 0, :], ALU.mult, ALU.mult).then_inc(n_scaled, 1)
                stt(cq[:, k, :], cq[:, k, :], qn_g[:, k:k + 1], nrstd[:, 1, 0:SEQ], ALU.mult, ALU.mult).then_inc(n_scaled, 1)

            def row_max(n, s, src, scores, max_done, negmax_done, scale):
                dve.wait_ge(scores, n)
                dve.tensor_reduce(neg_raw[:, s:s + 1], src, AX.X, ALU.max, negate=True).then_inc(max_done, 1)
                dve.wait_ge(max_done, n)
                ts(neg_max[:, s:s + 1], neg_raw[:, s:s + 1], scale, None, ALU.mult).then_inc(negmax_done, 1)

            def normalise(n, s, p, exp_done, inv_done, prob_done):
                dve.wait_ge(exp_done, n)
                dve.reciprocal(row_inv[:, s:s + 1], row_sum[:, s:s + 1]).then_inc(inv_done, 1)
                dve.wait_ge(inv_done, n)
                ts(p, p, row_inv[:, s:s + 1], None, ALU.mult).then_inc(prob_done, 1)

            def swa_unit(g, s, beside=None):
                nb = len(key_blocks(s // GROUP))
                n = g * 16 + s + 1
                row_max(n, s % 2, two_banks(2 * (s % 2))[:, 768 - nb * P:769], swa_s, swa_max, swa_negmax, SWA_SCALE)
                if beside is not None:
                    swa_side_work(g, beside)
                normalise(n, s % 2, sprob[:, s % 2, 0:nb * P], swa_exp, swa_inv, swa_prob)

            def sigmoid_of(e, n, step):
                ts(e, e, 1.0, None, ALU.add).then_inc(step, 1)
                dve.wait_ge(step, n + 1)
                dve.reciprocal(e, e).then_inc(step, 1)
                dve.wait_ge(step, n + 2)

            def swa_rope(n):
                j = n % 2
                if n:
                    dve.wait_ge(swa_q_mixed, n)
                dve.wait_ge(swa_q_rotated, n + 1)
                tt(qt[:, :], ps[:, (5 + j if n < 2 else 6), :], sin[:, :], ALU.mult)
                tt(qf2[:, j, :], qf2[:, j, :], cos[:, :], ALU.mult).then_inc(swa_q_step, 1)

            def swa_rope_add(n):
                dve.wait_ge(swa_q_step, n + 1)
                tt(qf2[:, n % 2, :], qf2[:, n % 2, :], qt[:, :], ALU.add).then_inc(swa_q_mixed, 1)

            def swa_keys_lo(g, part):
                rows, c = slice(64 * (g % 2), 64 * (g % 2) + 64), K_PARTS[part]
                dve.wait_ge(swa_k_hi, 3 * g + part + 1)
                tt(k_lo2[0:64, c], ks_f[rows, g // 2, c], f(k_hi2[rows, c]), ALU.subtract)
                tt(k_lo2[64:P, c], ks_f[rows, g // 2, c], f(k_hi2[rows, c]), ALU.subtract).then_inc(swa_k_lo, 1)

            def swa_queries_lo(g, part, j):
                c = Q_PARTS[part]
                dve.wait_ge(swa_q_hi, 4 * g + 2 * part + j + 1)
                dve.wait_ge(swa_q_mixed, 2 * g + j + 1)
                tt(q_st[64:P, 2 * j, c], qf2[0:64, j, c], f(q_st[0:64, 2 * j, c]), ALU.subtract)
                tt(q_st[64:P, 2 * j + 1, c], qf2[64:P, j, c], f(q_hiT[64:P, c]), ALU.subtract).then_inc(swa_q_lo, 1)

            def swa_block_out(blk):
                g, b = blk // QB, blk % QB
                dve.wait_ge(swa_out_low, blk + 1)
                if g and b == 0:
                    dve.wait_ge(swa_gated_lo, 2 * g)
                for odd in range(2):
                    ins = tt(b_T[64 * odd:64 * odd + 64, :, b * P:b * P + P],
                             ps[0:64, 6, :].rearrange("p (j o n) -> p j o n", o=2, n=P)[:, :, odd, :],
                             o_low[:, :].rearrange("p (j o n) -> p j o n", o=2, n=P)[:, :, odd, :], ALU.add)
                ins.then_inc(swa_out_free, 1)

            def swa_values_lo(g):
                dve.wait_ge(swa_v_hi, g + 1)
                tt(v_st[:, :, 64:P], vT_of(g), f(v_st[:, :, 0:64]), ALU.subtract).then_inc(swa_v_lo, 1)

            def swa_gate_of(g, j, pieces=range(4)):
                n = 3 * (2 * g + j)
                for p in pieces:
                    if p == 0:
                        dve.wait_ge(swa_gate_exp, 2 * g + j + 1)
                        ts(gate_e[:, :], gate_e[:, :], 1.0, None, ALU.add).then_inc(swa_gate_step, 1)
                        dve.wait_ge(swa_gate_step, n + 1)
                    ins = dve.reciprocal(gate_e[:, p * P:p * P + P], gate_e[:, p * P:p * P + P])
                    if p == 3:
                        ins.then_inc(swa_gate_step, 1)
                        dve.wait_ge(swa_gate_step, n + 2)
                        tt(s_gate[:, j, :], s_gate[:, j, :], gate_e[:, :], ALU.mult).then_inc(swa_gate_step, 1)

            def swa_gated_of(g, j):
                n = 2 * g + j
                dve.wait_ge(swa_gate_step, n * 3 + 3)
                dve.wait_ge(swa_out_free, g * 4 + 5)
                tt(b_T[:, j, :], b_T[:, j, :], s_gate[:, j, :], ALU.mult).then_inc(swa_gated, 1)

            def swa_gated_lo_of(g, j):
                dve.wait_ge(swa_gated_hi, 2 * g + j + 1)
                tt(s_stage[:, 1, :], b_T[:, j, :], f(s_stage[:, 0, :]), ALU.subtract).then_inc(swa_gated_lo, 1)

            for n in range(2):
                swa_rope(n)
                swa_rope_add(n)
                if n == 0:
                    for part in (0, 1):
                        swa_keys_lo(0, part)
                swa_queries_lo(0, 0, n)
            swa_unit(0, 0)
            swa_keys_lo(0, 2)
            for j in range(2):
                swa_queries_lo(0, 1, j)
            swa_values_lo(0)
            def swa_side_work(g, s):
                last = g == KV_GROUPS - 1
                if not last:
                    for j, at_s in enumerate(ROTATE):
                        if s == at_s + 1:
                            swa_rope(2 * g + 2 + j)
                        if s == at_s + 2:
                            swa_rope_add(2 * g + 2 + j)
                    if s == 14:
                        swa_keys_lo(g + 1, 0)
                        swa_queries_lo(g + 1, 0, 0)
                    if s == 15:
                        swa_queries_lo(g + 1, 0, 1)
                if g and s < 3:
                    swa_gate_of(g - 1, 1, (s + 1,))
                if g and s in (1, 3):
                    swa_gated_of(g - 1, s // 2)
                if g and s in (2, 4):
                    swa_gated_lo_of(g - 1, s // 2 - 1)
                p = s - (8 if last else 12)
                if 0 <= p < 4:
                    swa_gate_of(g, 0, (p,))

            for g in range(KV_GROUPS):
                last = g == KV_GROUPS - 1
                for s in range(16):
                    b, n = s // GROUP, s % GROUP
                    nb = len(key_blocks(b))
                    if s < 15:
                        swa_unit(g, s + 1, beside=s)
                    else:
                        if not last:
                            swa_keys_lo(g + 1, 1)
                        swa_side_work(g, s)
                    if s in ((7, 15) if last else (11, 15)):
                        j = int(s == 15)
                        c = B_SWA + 4 * g + 2 + j
                        u = U_SWA + 8 * g + (0 if last else 4) + 2 * j + 2
                        dve.wait_ge(w_used, u)
                        ts(s_gate[:, j, :], ps[:, 7, :], bias[:, c:c + 1], None, ALU.add).then_inc(swa_gate_z, 1)
                    if n == 0 and g * 4 + b >= 1:
                        swa_block_out(g * 4 + b - 1)
                        if s == 0:
                            swa_values_lo(g)
                    dve.wait_ge(swa_pT_hi, g * 16 + s + 1)
                    tt(spt_lo[:, 0:nb, n, :], two_banks(4)[:, 0:nb * P].rearrange("p (k n) -> p k n", n=P),
                       f(spt_hi[:, 0:nb, n, :]), ALU.subtract).then_inc(swa_pT_lo, 1)
                    if s == 15 and not last:
                        swa_unit(g + 1, 0)
                        swa_keys_lo(g + 1, 2)
                        for j in range(2):
                            swa_queries_lo(g + 1, 1, j)
                        swa_gate_of(g, 1, (0,))
            for k in range(RT):
                dve.wait_ge(n_hi, k + 1)
                tt(ckv_lo[:, k, :], ckv[:, k, :], f(ckv_hi[:, k, :]), ALU.subtract).then_inc(n_lo, 1)
            swa_block_out(KV_GROUPS * QB - 1)
            for k in range(RT):
                dve.wait_ge(n_hi, RT + k + 1)
                tt(cq_lo[:, k, :], cq[:, k, :], f(cq_hi[:, k, :]), ALU.subtract).then_inc(n_lo, 1)
            swa_gate_of(3, 1)
            for j, stage in enumerate((s_stage, s_stage_last)):
                swa_gated_of(3, j)
                dve.wait_ge(swa_gated, 7 + j)
                if j == 0:
                    dve.wait_ge(swa_spilled, 7 * 16)
                dve.tensor_copy(stage[:, 0, :], b_T[:, j, :]).then_inc(swa_gated_hi, 1)
                dve.wait_ge(swa_gated_hi, 7 + j)
                tt(stage[:, 1, :], b_T[:, j, :], f(stage[:, 0, :]), ALU.subtract).then_inc(swa_gated_lo, 1)

            def mla_unit(h, s):
                n = h * QB + (s + 1)
                row_max(n, s % 2, two_banks(2 * (s % 2))[:, 0:TOK], mla_s, mla_max, mla_negmax, MLA_SCALE)
                normalise(n, s % 2, prob[:, s % 2, :], mla_exp, mla_inv, mla_prob)

            with dve.Fori(0, MLA_HEADS) as h:
                u0 = U_MLA
                rope_cos, rope_sin = prob[0:64, 1, 0:SEQ], a_gate[0:64, :]
                dve.wait_ge(mla_qk_hi, h * 2 + 1)
                tt(kn_lo[:, :], two_banks(0)[:, 0:TOK], f(kn_hi[:, :]), ALU.subtract).then_inc(mla_qk_lo, 1)
                dve.wait_ge(mla_v_hi, h + 1)
                tt(v_lo[:, :, :], two_banks(4)[:, 0:TOK].rearrange("p (k n) -> p k n", n=P), f(v_hi[:, :, :]), ALU.subtract).then_inc(mla_v_lo, 1)
                dve.wait_ge(mla_qr_out, h + 1)
                tt(rope_cos, qrf[:, :], cos[0:64, :], ALU.mult)
                dve.wait_ge(swa_spilled, 8 * 16)
                dve.wait_ge(mla_q_rotated, h + 1)
                tt(rope_sin, ps[0:64, 5, :], sin[0:64, :], ALU.mult).then_inc(mla_q_step, 1)
                dve.wait_ge(mla_q_step, h + 1)
                tt(qrf[:, :], rope_cos, rope_sin, ALU.add).then_inc(mla_q_mixed, 1)
                dve.wait_ge(mla_qk_hi, h * 2 + 2)
                tt(qn_lo[:, :], ps[:, 4, :], f(qn_hi[:, :]), ALU.subtract).then_inc(mla_qk_lo, 1)
                dve.wait_ge(mla_qr_hi, h + 1)
                tt(qr_st[64:P, :], qrf[:, :], f(qr_st[0:64, :]), ALU.subtract).then_inc(mla_qr_lo, 1)
                mla_unit(h, 0)
                for s in range(QB):
                    if s < QB - 1:
                        mla_unit(h, s + 1)
                    dve.wait_ge(mla_pT_hi, h * QB + (s + 1))
                    tt(pt_lo[:, :, s * P:s * P + P], two_banks(4)[:, 0:TOK].rearrange("p (k n) -> p k n", n=P),
                       f(pt_hi[:, :, s * P:s * P + P]), ALU.subtract).then_inc(mla_pT_lo, 1)
                dve.wait_ge(w_used, h * 4 + (u0 + 4))
                ts(a_gate[:, :], ps[:, 7, :], bias[:, bass.ds(h + B_MLA, 1)], None, ALU.add).then_inc(mla_gate_z, 1)
                e = prob[:, 1, 0:SEQ]
                dve.wait_ge(mla_gate_exp, h + 1)
                sigmoid_of(e, h * 3, mla_gate_step)
                tt(a_gate[:, :], a_gate[:, :], e, ALU.mult).then_inc(mla_gate_step, 1)
                dve.wait_ge(mla_gate_step, h * 3 + 3)
                dve.wait_ge(mla_out, h + 1)
                tt(a_gate[:, :], ps[:, 6, :], a_gate[:, :], ALU.mult).then_inc(mla_free, 1)
                dve.wait_ge(mla_gated_hi, h + 1)
                tt(a_stage[:, 1, :], a_gate[:, :], f(a_stage[:, 0, :]), ALU.subtract).then_inc(mla_gated_lo, 1)
                dve.wait_ge(mla_gated_lo, h + 1)

            with dve.Fori(0, 4) as r:
                for j in range(4):
                    def gate_lo(i):
                        k = 4 * j + i
                        dve.wait_ge(g_hi_done, r * 16 + (k + 1))
                        tt(g_lo[:, :], g_w[:, :], f(g_hi[:, :]), ALU.subtract).then_inc(g_lo_done, 1)

                    for i, sg in enumerate((sg_a, sg_b)):
                        gate_lo(2 * i)
                        gate_lo(2 * i + 1)
                        dve.wait_ge(mg_exp, r * 8 + (2 * j + i + 1))
                        sigmoid_of(sg[:, :], (r * 8 + (2 * j + i)) * 2, mg_step)
                    for i, sg in ((1, sg_b), (0, sg_a)):
                        dve.wait_ge(mg_step, r * 16 + (4 * j + 2 * i + 2))
                        dve.wait_ge(w_used, r * 24 + (U_MG + 6 * j + 6 - i))
                        tt(sg[:, :], sg[:, :], ps[:, 2 + i, :], ALU.mult).then_inc(mg_mixed, 1)
                    dve.wait_ge(mg_mixed, r * 8 + (2 * j + 2))
                    dve.wait_ge(mla_spilled, 9 * 16)
                    tt(m_f[:, bass.ds(r * 4 + j, 1), :].rearrange("p a n -> p (a n)"), sg_a[:, :], sg_b[:, :], ALU.add).then_inc(mg_free, 1)
            def m_lo_of(k):
                dve.wait_ge(m_hi_done, k + 1)
                tt(m_lo[:, k, :], m_f[:, k, :], f(m_hi[:, k, :]), ALU.subtract).then_inc(m_ready, 1)

            for k in range(4):
                m_lo_of(k)
            dve.wait_ge(late_in, 32)
            for c in range(4):
                dve.wait_ge(gate_bc_sum, c + 1)
                gc = gate_bc[:, c * 512:c * 512 + 512]
                tt(gc, gc, ps[:, 4 + c, :], ALU.add).then_inc(gate_ready, 1)
            for k in range(4, KT):
                m_lo_of(k)

            dve.wait_ge(y_in, 16)
            dve.wait_ge(gate_ready, 4)
            for n in range(4):
                cc = slice(n * 512, n * 512 + 512)
                for t in range(QB):
                    if n < 3 and t == QB - 1:
                        dve.wait_ge(w_used, U_OUT + 8 * n + 8)
                    else:
                        dve.wait_ge(out_done, n * (QB - 1) + t + 1)
                    tt(y_add[:, t, :], ps[:, 4 * (n % 2) + t, :], gate_bc[:, cc], ALU.mult).then_inc(o_free, 1)
                    dve.wait_ge(o_free, n * QB + t + 1)
                    tt(y[:, t, cc], y[:, t, cc], y_add[:, t, :], ALU.add).then_inc(o_added, 1)
                    if n < 3:
                        continue
                    dve.wait_ge(o_squared, 3 * QB + t + 1)
                    dve.tensor_reduce(tok_ms[:, t:t + 1], sumsq.rearrange("p (n t) -> p t n", t=QB)[:, t:t + 1, :], AX.X, ALU.add).then_inc(o_ms, 1)
                    dve.wait_ge(o_root, t + 1)
                    dve.reciprocal(tok_inv[:, t:t + 1], tok_ms[:, t:t + 1]).then_inc(o_inv, 1)
                    dve.wait_ge(o_inv, t + 1)
                    for half in range(2):
                        c = slice(half * D // 2, (half + 1) * D // 2)
                        stt(y[:, t, c], y[:, t, c], tok_inv[:, t:t + 1], fin_g[:, c], ALU.mult, ALU.mult).then_inc(o_final, 1)


def rope_tables(np):
    n, grid_w = 16, 64
    inv = (np.float32(10000.0) ** (-np.arange(n, dtype=np.float32) / np.float32(n))).astype(np.float32)
    tok = np.arange(SEQ)
    pos = np.stack([tok // grid_w, tok % grid_w]).astype(np.float32)
    feat = np.arange(P) % 64
    ang = (pos[feat // 32] * inv[feat % 16][:, None]).astype(np.float32)
    rot = np.zeros((P, P), np.float32)
    for d in range(P):
        if d % 32 < 16:
            rot[d + 16, d] = -1.0
        else:
            rot[d - 16, d] = 1.0
    q, k = np.arange(P)[:, None], np.arange(P)[None, :]
    masks = np.zeros((P, 2, P), np.float32)
    masks[:, 0][k < q] = NEG
    masks[:, 1][k > q] = NEG
    return np.cos(ang).astype(np.float32), np.sin(ang).astype(np.float32), rot, np.eye(P, dtype=np.float32), masks


def kernel(**inputs):
    import numpy as np
    import concourse.bacc as bacc
    from concourse.bass_utils import run_bass_kernel_spmd as run

    a = {k: np.asarray(v) for k, v in inputs.items()}
    w_in, b_in = a["w_in"][0], a["b_in"][0]
    c_q, c_kv, k_pe, gate_a, q_s, k_s, v_s, gate_b, mg_a, mg_b = (
        0, 512, 1024, 1088, 2112, 3136, 3392, 3648, 4672, 6720)

    cols = []
    for i in range(RT):
        cols += [c_kv + P * i, c_q + P * i]
    cols += [k_pe, k_s, k_s + P, v_s, v_s + P]
    swa_cols = []
    swa_stream = [q_s, q_s + P]
    for g in range(KV_GROUPS):
        swa_cols += [q_s + 256 * g, q_s + 256 * g + P, gate_b + 256 * g, gate_b + 256 * g + P]
        if g < KV_GROUPS - 1:
            swa_stream += [q_s + 256 * (g + 1), q_s + 256 * (g + 1) + P]
        swa_stream += [gate_b + 256 * g, gate_b + 256 * g + P]
    mla_cols = [gate_a + P * h for h in range(MLA_HEADS)]
    mg_cols = []
    for j in range(KT):
        mg_cols += [mg_a + P * j, mg_b + P * j]

    def tile_units(w, c):
        t = w[:, c:c + P].reshape(-1, 8, P, P)
        return [u.transpose(1, 0, 2).reshape(P, UNIT) for u in t]

    def rank_unit(w, cs):
        t = np.concatenate([w[:, c0:c1] for c0, c1 in cs], axis=1)
        return t.reshape(RT, P, 256).transpose(1, 0, 2).reshape(P, UNIT)

    ada = a["w_ada"][0].reshape(8, 2, P, 12, 512).transpose(3, 0, 2, 1, 4).reshape(12, 8, P, UNIT)
    units = []
    for n in range(CHUNKS):
        units += list(ada[4 * (n % 2) + n // 2])
        if n >= CHUNKS - EARLY:
            units.append(tile_units(w_in, cols[n - (CHUNKS - EARLY)])[0])
    for c in cols[0:EARLY]:
        units.append(tile_units(w_in, c)[1])
    for c in cols[EARLY:] + swa_stream:
        units += tile_units(w_in, c)
    w_uq, w_ukv = a["w_uq"][0], a["w_ukv"][0]
    for h in range(MLA_HEADS):
        q0, k0 = h * (NOPE + ROPE), h * 256
        units.append(rank_unit(w_ukv, [(k0, k0 + 256)]))
        units.append(rank_unit(w_uq, [(q0, q0 + 192), (q0, q0 + 64)]))
        units += tile_units(w_in, mla_cols[h])
    for j in range(KT):
        units += tile_units(w_in, mg_cols[2 * j]) + tile_units(w_in, mg_cols[2 * j + 1])
        units += tile_units(a["w_branch_b"][0], P * j) + tile_units(a["w_branch_a"][0], P * j)
    w_out = a["w_out"][0]
    for n in range(4):
        for c in range(8):
            t = w_out[256 * c:256 * c + 256, 512 * n:512 * n + 512]
            units.append(t.reshape(2, P, 512).transpose(1, 0, 2).reshape(P, UNIT))
    stream = np.stack(units)
    gate_w = a["w_ada"][0][:, 2 * D:3 * D].reshape(KT, P, 4, 512).transpose(2, 0, 1, 3).reshape(GATE_TILES, P, 512)

    def columns(v):
        return v.reshape(-1, P).T

    def twice(v):
        return np.stack([columns(v), columns(v)], axis=-1)

    b_cols = [b_in[c:c + P] for c in cols + swa_cols + mla_cols + mg_cols]
    cos, sin, rot, ident, masks = rope_tables(np)
    b_ada = a["b_ada"][0]
    data = {
        "xT": np.concatenate([a["x"][0].T.reshape(KT, P, SEQ), a["ctx"][0].T.reshape(KT, P, CTX)], axis=2).transpose(1, 0, 2),
        "x": a["x"][0],
        "cT": np.stack([columns(a["c"][0]), columns(a["c_ctx"])], axis=-1),
        "gate_w": gate_w,
        "pair": np.array([[1, 0], [1, 0], [0, 1], [0, 1]], np.float32),
        "b_adaT": twice(b_ada[0:2 * D]),
        "b_gate": np.broadcast_to(b_ada[2 * D:3 * D], (P, D)),
        "norm_gT": twice(a["norm_g"][0]),
        "stream": stream,
        "biasT": np.stack(b_cols, axis=1),
        "qn_gT": columns(a["q_norm_g"][0]),
        "kvn_gT": columns(a["kv_norm_g"][0]),
        "sink": a["sink"],
        "final_g": np.broadcast_to(a["final_g"], (P, D)),
        "cos": cos, "sin": sin, "rot": rot, "ident": ident, "masks": masks,
    }
    nc = bacc.Bacc("TRN2", target_bir_lowering=False, num_devices=1)
    arrays, args = {}, []
    for name, v in data.items():
        v = np.ascontiguousarray(v)
        arrays["in_" + name] = v
        args.append(nc.dram_tensor("in_" + name, v.shape, mybir.dt.from_np(v.dtype), kind="ExternalInput").ap())
    out = nc.dram_tensor("out", (SEQ, D), F32, kind="ExternalOutput").ap()
    build(nc, *args, out)
    r = run(nc, [arrays], core_ids=[0])
    return r.results[0]["out"].reshape(1, SEQ, D)
```
